# Optimizing a Trainium2 kernel written in Bass

```python
import math
import jax, jax.numpy as jnp
from jax import lax
import numpy as np

D_MODEL = 1024
BATCH = 1
SEQ = 256
DEPTH = 1

CONV_DIM = 512
CONV_WIDTH = 3
NSA_HEADS = 8
NSA_KV_GROUPS = 2
NSA_HPG = NSA_HEADS // NSA_KV_GROUPS
NSA_HEAD_DIM = 64
NSA_DIM = NSA_HEADS * NSA_HEAD_DIM
CMP_LEN = 32
CMP_STRIDE = 16
CMP_HIDDEN = 256
SLC_LEN = 64
SLC_TOPN = 8
SLC_FORCE_BONUS = 1e6
WINDOW = 512
NSA_QBLOCK = 64
GDN_HEADS = 4
GDN_HEAD_DIM = 128
GDN_DIM = GDN_HEADS * GDN_HEAD_DIM
GDN_CONV = 4
GDN_CHUNK = 64
N_BRANCH = 3
BRANCH_DIM = 512
IN_SPLITS = (3 * CONV_DIM, NSA_DIM, 6 * NSA_KV_GROUPS * NSA_HEAD_DIM, 3 * NSA_HEADS, 3 * GDN_DIM, GDN_DIM, GDN_HEADS, GDN_HEADS)
D_IN = 3 * CONV_DIM + NSA_DIM + 6 * NSA_KV_GROUPS * NSA_HEAD_DIM + 3 * NSA_HEADS + 4 * GDN_DIM + 2 * GDN_HEADS
MOE_GROUPS = 4
EXPERTS_PER_GROUP = 8
N_EXPERTS = MOE_GROUPS * EXPERTS_PER_GROUP
TOPK_IN_GROUP = 2
EXPERT_FF = 512
MOE_BLOCK = 256
RMS_EPS = 1e-6
NEG_INF = -1e30


def split_last(u, sizes):
    out, start = [], 0
    for n in sizes:
        out.append(u[..., start:start + n])
        start += n
    return out

def rms_norm(x, gain):
    xf = x.astype(jnp.float32)
    y = xf * lax.rsqrt(jnp.mean(xf * xf, axis=-1, keepdims=True) + RMS_EPS)
    return (y * gain.astype(jnp.float32)).astype(x.dtype)

def l2_norm(x):
    return x * lax.rsqrt(jnp.sum(x * x, axis=-1, keepdims=True) + RMS_EPS)

def causal_depthwise_conv(x, w):
    k, c = w.shape
    return lax.conv_general_dilated(x, w[:, None, :].astype(x.dtype), window_strides=(1,), padding=[(k - 1, 0)], dimension_numbers=('NWC', 'WIO', 'NWC'), feature_group_count=c)

def alibi_slopes(n):
    return 2.0 ** (-8.0 * jnp.arange(1, n + 1, dtype=jnp.float32) / n)

def short_conv_mixer(u_a, conv_w):
    b_gate, c_gate, x_in = split_last(u_a, (CONV_DIM, CONV_DIM, CONV_DIM))
    return b_gate * causal_depthwise_conv(c_gate * x_in, conv_w)

def nsa_compress(kv, pe, w1, w2):
    b, s, g, d = kv.shape
    n_cmp = (s - CMP_LEN) // CMP_STRIDE + 1
    idx = jnp.arange(n_cmp)[:, None] * CMP_STRIDE + jnp.arange(CMP_LEN)[None, :]
    blocks = kv[:, idx] + pe[:, None, :]
    flat = jnp.moveaxis(blocks, 3, 2).reshape(b, n_cmp, g, CMP_LEN * d)
    return jax.nn.gelu(flat @ w1) @ w2

def nsa_mixer(u_q, u_kv, u_g, qk_gain, cmp_pe, cmp_w1, cmp_w2):
    b, s, _ = u_q.shape
    g, hpg, d, qbl = NSA_KV_GROUPS, NSA_HPG, NSA_HEAD_DIM, NSA_QBLOCK
    f32 = jnp.float32
    scale = d ** -0.5
    q = rms_norm(u_q.reshape(b, s, g, hpg, d), qk_gain[0])
    kv = u_kv.reshape(b, s, 6, g, d)
    k_c = rms_norm(nsa_compress(kv[:, :, 0], cmp_pe[0], cmp_w1[0], cmp_w2[0]), qk_gain[1])
    v_c = nsa_compress(kv[:, :, 1], cmp_pe[1], cmp_w1[1], cmp_w2[1])
    n_cmp = k_c.shape[1]
    n_slc = s // SLC_LEN
    top_n = min(SLC_TOPN, n_slc)
    k_s = rms_norm(kv[:, :, 2], qk_gain[2]).reshape(b, n_slc, SLC_LEN, g, d).transpose(0, 3, 1, 2, 4)
    v_s = kv[:, :, 3].reshape(b, n_slc, SLC_LEN, g, d).transpose(0, 3, 1, 2, 4)
    pad = ((0, 0), (WINDOW, 0), (0, 0), (0, 0))
    k_w = jnp.pad(rms_norm(kv[:, :, 4], qk_gain[3]), pad)
    v_w = jnp.pad(kv[:, :, 5], pad)
    gates = jax.nn.sigmoid(u_g.astype(f32)).reshape(b, s, 3, g, hpg)
    slopes = alibi_slopes(NSA_HEADS).reshape(g, hpg)
    cmp_lo = jnp.arange(n_cmp) * CMP_STRIDE
    cmp_end = cmp_lo + CMP_LEN - 1
    slc_lo = jnp.arange(n_slc) * SLC_LEN
    overlap = ((cmp_lo[:, None] < slc_lo[None, :] + SLC_LEN) & (cmp_lo[:, None] + CMP_LEN > slc_lo[None, :])).astype(f32)
    n_qb = s // qbl
    q_blocks = jnp.moveaxis(q.reshape(b, n_qb, qbl, g, hpg, d), 1, 0)
    g_blocks = jnp.moveaxis(gates.reshape(b, n_qb, qbl, 3, g, hpg), 1, 0)
    bi = jnp.arange(b)[:, None, None, None]
    gi = jnp.arange(g)[None, :, None, None]
    j_idx = jnp.arange(n_slc)

    def query_block(args):
        qb, gb, blk = args
        q0 = blk * qbl
        t = q0 + jnp.arange(qbl)
        dist_c = (t[:, None] - cmp_end[None, :]).astype(f32)
        ok_c = dist_c >= 0
        s_c = jnp.einsum('bqghd,bcgd->bghqc', qb, k_c).astype(f32) * scale
        s_c = jnp.where(ok_c, s_c - slopes[:, :, None, None] * dist_c, NEG_INF)
        p_c = jax.nn.softmax(s_c, axis=-1) * jnp.any(ok_c, axis=-1)[:, None].astype(f32)
        o_c = jnp.einsum('bghqc,bcgd->bqghd', p_c.astype(v_c.dtype), v_c)
        imp = jnp.einsum('bghqc,cj->bgqj', p_c, overlap)
        jt = (t // SLC_LEN)[:, None]
        forced = (j_idx[None, :] == 0) | (j_idx[None, :] == jt) | (j_idx[None, :] == jt - 1)
        score = jnp.where(j_idx[None, :] <= jt, imp + jnp.where(forced, SLC_FORCE_BONUS, 0.0), NEG_INF)
        _, sel = lax.top_k(score, top_n)
        k_sel = k_s[bi, gi, sel].reshape(b, g, qbl, top_n * SLC_LEN, d)
        v_sel = v_s[bi, gi, sel].reshape(b, g, qbl, top_n * SLC_LEN, d)
        pos_s = (sel[..., None] * SLC_LEN + jnp.arange(SLC_LEN)).reshape(b, g, qbl, top_n * SLC_LEN)
        dist_s = (t[None, None, :, None] - pos_s).astype(f32)[:, :, None]
        s_s = jnp.einsum('bqghd,bgqkd->bghqk', qb, k_sel).astype(f32) * scale
        s_s = jnp.where(dist_s >= 0, s_s - slopes[None, :, :, None, None] * dist_s, NEG_INF)
        p_s = jax.nn.softmax(s_s, axis=-1)
        o_s = jnp.einsum('bghqk,bgqkd->bqghd', p_s.astype(v_sel.dtype), v_sel)
        k_wb = lax.dynamic_slice_in_dim(k_w, q0, WINDOW + qbl, axis=1)
        v_wb = lax.dynamic_slice_in_dim(v_w, q0, WINDOW + qbl, axis=1)
        pos_w = q0 - WINDOW + jnp.arange(WINDOW + qbl)
        dist_w = t[:, None] - pos_w[None, :]
        ok_w = (dist_w >= 0) & (dist_w < WINDOW) & (pos_w[None, :] >= 0)
        s_w = jnp.einsum('bqghd,bkgd->bghqk', qb, k_wb).astype(f32) * scale
        s_w = jnp.where(ok_w, s_w - slopes[:, :, None, None] * dist_w.astype(f32), NEG_INF)
        p_w = jax.nn.softmax(s_w, axis=-1)
        o_w = jnp.einsum('bghqk,bkgd->bqghd', p_w.astype(v_wb.dtype), v_wb)
        o = gb[:, :, 0, :, :, None] * o_c + gb[:, :, 1, :, :, None] * o_s + gb[:, :, 2, :, :, None] * o_w
        return o.reshape(b, qbl, NSA_DIM).astype(qb.dtype)

    out = lax.map(query_block, (q_blocks, g_blocks, jnp.arange(n_qb)))
    return jnp.moveaxis(out, 0, 1).reshape(b, s, NSA_DIM)

def chunk_gated_delta_rule(q, k, v, g, beta):
    b, s, h, dk = q.shape
    dv = v.shape[-1]
    c = GDN_CHUNK
    n = s // c

    def to_chunks(a):
        return jnp.moveaxis(a.reshape((b, n, c, h) + a.shape[3:]), 3, 1)

    q, k, v, beta = to_chunks(q), to_chunks(k), to_chunks(v), to_chunks(beta)
    gc = jnp.cumsum(to_chunks(g), axis=-1)
    tri = jnp.tril(jnp.ones((c, c), dtype=bool))
    decay = jnp.where(tri, jnp.exp(jnp.where(tri, gc[..., :, None] - gc[..., None, :], 0.0)), 0.0)
    k_beta = k * beta[..., None]
    m = jnp.einsum('bhncd,bhnsd->bhncs', k_beta, k) * decay
    t_inv = lax.linalg.triangular_solve(m, jnp.broadcast_to(jnp.eye(c, dtype=m.dtype), m.shape), left_side=True, lower=True, unit_diagonal=True)
    u = t_inv @ (v * beta[..., None])
    w = t_inv @ (k_beta * jnp.exp(gc)[..., None])
    attn = jnp.einsum('bhncd,bhnsd->bhncs', q, k) * decay
    q_dec = q * jnp.exp(gc)[..., None]
    g_last = gc[..., -1:]
    k_dec = k * jnp.exp(g_last - gc)[..., None]
    chunk_decay = jnp.exp(g_last[..., 0])

    def step(state, xs):
        q_i, k_i, u_i, w_i, a_i, d_i = xs
        v_new = u_i - jnp.einsum('bhcd,bhde->bhce', w_i, state)
        o_i = jnp.einsum('bhcd,bhde->bhce', q_i, state) + jnp.einsum('bhcs,bhse->bhce', a_i, v_new)
        state = state * d_i[..., None, None] + jnp.einsum('bhcd,bhce->bhde', k_i, v_new)
        return state, o_i

    xs = tuple(jnp.moveaxis(a, 2, 0) for a in (q_dec, k_dec, u, w, attn, chunk_decay))
    _, o = lax.scan(step, jnp.zeros((b, h, dk, dv), q.dtype), xs)
    return o.transpose(1, 0, 3, 2, 4).reshape(b, s, h, dv)

def gated_deltanet_mixer(u_qkv, u_z, u_b, u_a, conv_w, a_log, dt_bias, out_gain):
    b, s, _ = u_qkv.shape
    f32 = jnp.float32
    qkv = jax.nn.silu(causal_depthwise_conv(u_qkv, conv_w)).astype(f32).reshape(b, s, 3, GDN_HEADS, GDN_HEAD_DIM)
    q = l2_norm(qkv[:, :, 0]) * GDN_HEAD_DIM ** -0.5
    k = l2_norm(qkv[:, :, 1])
    v = qkv[:, :, 2]
    beta = jax.nn.sigmoid(u_b.astype(f32))
    g = -jnp.exp(a_log.astype(f32)) * jax.nn.softplus(u_a.astype(f32) + dt_bias.astype(f32))
    o = chunk_gated_delta_rule(q, k, v, g, beta)
    o = rms_norm(o, out_gain) * jax.nn.silu(u_z.astype(f32).reshape(b, s, GDN_HEADS, GDN_HEAD_DIM))
    return o.reshape(b, s, GDN_DIM).astype(u_qkv.dtype)

def hybrid_mixer(h, w_in, conv_a_w, nsa_qk_gain, cmp_pe, cmp_w1, cmp_w2, gdn_conv_w, gdn_a_log, gdn_dt_bias, gdn_out_gain, w_branch, w_gate, b_gate, w_out):
    b, s, dm = h.shape
    u = h @ w_in
    u_a, u_nq, u_nkv, u_ng, u_gqkv, u_gz, u_gb, u_ga = split_last(u, IN_SPLITS)
    y_a = short_conv_mixer(u_a, conv_a_w)
    y_n = nsa_mixer(u_nq, u_nkv, u_ng, nsa_qk_gain, cmp_pe, cmp_w1, cmp_w2)
    y_g = gated_deltanet_mixer(u_gqkv, u_gz, u_gb, u_ga, gdn_conv_w, gdn_a_log, gdn_dt_bias, gdn_out_gain)
    branches = jnp.einsum('bsrc,rcd->bsrd', jnp.stack([y_a, y_n, y_g], axis=2), w_branch)
    gates = jax.nn.sigmoid((h @ w_gate + b_gate).astype(jnp.float32)).reshape(b, s, N_BRANCH, dm)
    merged = jnp.sum(gates * branches, axis=2).astype(h.dtype)
    return merged @ w_out

def hier_moe(h, w_rg, b_rg, w_re, b_re, w_eg, w_eu, w_ed):
    b, s, dm = h.shape
    n_tok = b * s
    n_asg = n_tok * TOPK_IN_GROUP
    xt = h.reshape(n_tok, dm)
    lg = (xt @ w_rg + b_rg).astype(jnp.float32)
    grp = jnp.argmax(lg, axis=-1)
    p_grp = jnp.take_along_axis(jax.nn.softmax(lg, axis=-1), grp[:, None], axis=-1)
    le = (xt @ w_re + b_re).astype(jnp.float32).reshape(n_tok, MOE_GROUPS, EXPERTS_PER_GROUP)
    le = jnp.take_along_axis(le, grp[:, None, None], axis=1)[:, 0]
    top_p, top_i = lax.top_k(jax.nn.softmax(le, axis=-1), TOPK_IN_GROUP)
    gate = top_p / jnp.sum(top_p, axis=-1, keepdims=True) * p_grp
    expert = (grp[:, None] * EXPERTS_PER_GROUP + top_i).reshape(n_asg)
    token = jnp.arange(n_asg) // TOPK_IN_GROUP
    order = jnp.argsort(expert)
    e_s, tok_s, gate_s = expert[order], token[order], gate.reshape(n_asg)[order]
    counts = jnp.bincount(expert, length=N_EXPERTS)
    n_blk = (counts + MOE_BLOCK - 1) // MOE_BLOCK
    start = jnp.cumsum(counts) - counts
    pad_start = (jnp.cumsum(n_blk) - n_blk) * MOE_BLOCK
    dest = pad_start[e_s] + jnp.arange(n_asg) - start[e_s]
    total_blk = n_asg // MOE_BLOCK + N_EXPERTS
    buf = jnp.zeros((total_blk * MOE_BLOCK, dm), h.dtype).at[dest].set(xt[tok_s])
    blk_expert = jnp.repeat(jnp.arange(N_EXPERTS), n_blk, total_repeat_length=total_blk)

    def expert_block(args):
        xb, e = args
        return (jax.nn.silu(xb @ w_eg[e]) * (xb @ w_eu[e])) @ w_ed[e]

    yb = lax.map(expert_block, (buf.reshape(total_blk, MOE_BLOCK, dm), blk_expert))
    y = yb.reshape(total_blk * MOE_BLOCK, dm)[dest] * gate_s[:, None].astype(h.dtype)
    return jax.ops.segment_sum(y, tok_s, num_segments=n_tok).reshape(b, s, dm)

def first_inputs(seed: int = 0) -> dict:
    key = jax.random.key(seed)
    ks = jax.random.split(key, 24)
    f32 = jnp.float32

    def nrm(k, shape, scale):
        return jax.random.normal(k, shape, f32) * scale

    out_scale = (2 * DEPTH) ** -0.5
    dt = jnp.exp(jax.random.uniform(ks[10], (DEPTH, GDN_HEADS), f32, math.log(1e-3), math.log(1e-1)))
    return {
        'x': nrm(ks[0], (BATCH, SEQ, D_MODEL), 1.0),
        'norm_mix': 1.0 + nrm(ks[1], (DEPTH, D_MODEL), 0.02),
        'w_in': nrm(ks[2], (DEPTH, D_MODEL, D_IN), D_MODEL ** -0.5),
        'conv_a_w': nrm(ks[3], (DEPTH, CONV_WIDTH, CONV_DIM), CONV_WIDTH ** -0.5),
        'nsa_qk_gain': 1.0 + nrm(ks[4], (DEPTH, 4, NSA_HEAD_DIM), 0.02),
        'cmp_pe': nrm(ks[5], (DEPTH, 2, CMP_LEN, NSA_HEAD_DIM), 0.02),
        'cmp_w1': nrm(ks[6], (DEPTH, 2, CMP_LEN * NSA_HEAD_DIM, CMP_HIDDEN), (CMP_LEN * NSA_HEAD_DIM) ** -0.5),
        'cmp_w2': nrm(ks[7], (DEPTH, 2, CMP_HIDDEN, NSA_HEAD_DIM), CMP_HIDDEN ** -0.5),
        'gdn_conv_w': nrm(ks[8], (DEPTH, GDN_CONV, 3 * GDN_DIM), GDN_CONV ** -0.5),
        'gdn_a_log': jnp.log(jax.random.uniform(ks[9], (DEPTH, GDN_HEADS), f32, 1.0, 16.0)),
        'gdn_dt_bias': dt + jnp.log(-jnp.expm1(-dt)),
        'gdn_out_gain': 1.0 + nrm(ks[11], (DEPTH, GDN_HEAD_DIM), 0.02),
        'w_branch': nrm(ks[12], (DEPTH, N_BRANCH, BRANCH_DIM, D_MODEL), BRANCH_DIM ** -0.5),
        'w_gate': nrm(ks[13], (DEPTH, D_MODEL, N_BRANCH * D_MODEL), D_MODEL ** -0.5),
        'b_gate': nrm(ks[14], (DEPTH, N_BRANCH * D_MODEL), 0.01),
        'w_out': nrm(ks[15], (DEPTH, D_MODEL, D_MODEL), D_MODEL ** -0.5 * out_scale),
        'norm_ffn': 1.0 + nrm(ks[16], (DEPTH, D_MODEL), 0.02),
        'w_router_group': nrm(ks[17], (DEPTH, D_MODEL, MOE_GROUPS), D_MODEL ** -0.5),
        'b_router_group': nrm(ks[18], (DEPTH, MOE_GROUPS), 0.01),
        'w_router_expert': nrm(ks[19], (DEPTH, D_MODEL, N_EXPERTS), D_MODEL ** -0.5),
        'b_router_expert': nrm(ks[20], (DEPTH, N_EXPERTS), 0.01),
        'w_expert_gate': nrm(ks[21], (DEPTH, N_EXPERTS, D_MODEL, EXPERT_FF), D_MODEL ** -0.5),
        'w_expert_up': nrm(ks[22], (DEPTH, N_EXPERTS, D_MODEL, EXPERT_FF), D_MODEL ** -0.5),
        'w_expert_down': nrm(ks[23], (DEPTH, N_EXPERTS, EXPERT_FF, D_MODEL), EXPERT_FF ** -0.5 * out_scale),
    }

def first_block(x, norm_mix, w_in, conv_a_w, nsa_qk_gain, cmp_pe, cmp_w1, cmp_w2, gdn_conv_w, gdn_a_log, gdn_dt_bias, gdn_out_gain, w_branch, w_gate, b_gate, w_out, norm_ffn, w_router_group, b_router_group, w_router_expert, b_router_expert, w_expert_gate, w_expert_up, w_expert_down):
    for l in range(DEPTH):
        h = rms_norm(x, norm_mix[l])
        x = x + hybrid_mixer(h, w_in[l], conv_a_w[l], nsa_qk_gain[l], cmp_pe[l], cmp_w1[l], cmp_w2[l], gdn_conv_w[l], gdn_a_log[l], gdn_dt_bias[l], gdn_out_gain[l], w_branch[l], w_gate[l], b_gate[l], w_out[l])
        h = rms_norm(x, norm_ffn[l])
        x = x + hier_moe(h, w_router_group[l], b_router_group[l], w_router_expert[l], b_router_expert[l], w_expert_gate[l], w_expert_up[l], w_expert_down[l])
    return x


DEPTH_2 = 4

N_MIXERS = 4
N_A = (DEPTH_2 + 3) // 4
N_B = (DEPTH_2 + 2) // 4
N_C = (DEPTH_2 + 1) // 4
N_D = DEPTH_2 // 4
A_HEADS = 4
A_DV = D_MODEL // A_HEADS
A_DK = A_DV // 2
A_CHUNK = 64
A_IN = 2 * A_HEADS * A_DK + 2 * A_HEADS * A_DV + 2 * A_HEADS
B_HEAD_DIM = 64
B_Q_HEADS = D_MODEL // B_HEAD_DIM
B_KV_HEADS = B_Q_HEADS // 8
B_WINDOW = 128
B_BLOCK = 128
B_IN = (B_Q_HEADS + 2 * B_KV_HEADS) * B_HEAD_DIM
C_EXPAND = 128
C_HEADS = D_MODEL // C_EXPAND
C_DK = C_EXPAND
C_DV = D_MODEL // C_HEADS
C_CHUNK = 16
C_IN = 2 * C_HEADS * C_DK + 2 * C_HEADS * C_DV
D_HEAD_DIM = 64
D_HEADS = D_MODEL // (2 * D_HEAD_DIM)
D_QBLOCK = 128
D_IN_2 = 3 * D_HEADS * 2 * D_HEAD_DIM
ROPE_THETA = 500000.0
ROT_FRAC = 4
FFN_HIDDEN = -(-8 * D_MODEL // (3 * 256)) * 256
DEEPNORM_ALPHA = (2 * DEPTH_2) ** 0.25
DEEPNORM_BETA = (8 * DEPTH_2) ** -0.25
F32 = jnp.float32


def layer_norm(x, g, b, eps=1e-5):
    xf = x.astype(F32)
    mu = xf.mean(-1, keepdims=True)
    var = jnp.square(xf - mu).mean(-1, keepdims=True)
    return ((xf - mu) * lax.rsqrt(var + eps) * g.astype(F32) + b.astype(F32)).astype(x.dtype)

def head_rms_norm(h, w, eps=1e-6):
    hf = h.astype(F32)
    return hf * lax.rsqrt(jnp.mean(hf * hf, -1, keepdims=True) + eps) * w.astype(F32)

def partial_rope(x, positions):
    hd = x.shape[-1]
    rot = hd // ROT_FRAC
    half = rot // 2
    inv = jnp.power(ROPE_THETA, -jnp.arange(half, dtype=F32) * 2.0 / rot)
    ang = positions.astype(F32)[..., None] * inv
    cos = jnp.cos(ang)[:, :, None, :]
    sin = jnp.sin(ang)[:, :, None, :]
    xf = x.astype(F32)
    x1, x2 = xf[..., :half], xf[..., half:rot]
    out = jnp.concatenate([x1 * cos - x2 * sin, x2 * cos + x1 * sin, xf[..., rot:]], axis=-1)
    return out.astype(x.dtype)

def to_chunks(a, L):
    r = a.reshape(a.shape[0], a.shape[1] // L, L, *a.shape[2:])
    return jnp.swapaxes(jnp.moveaxis(r, 1, 0), 2, 3)

def from_chunks(a):
    r = jnp.moveaxis(jnp.swapaxes(a, 2, 3), 0, 1)
    return r.reshape(r.shape[0], r.shape[1] * r.shape[2], *r.shape[3:])

def mlstm_mixer(h, w_in, b_gate, norm_w, w_out):
    bsz, seq, _ = h.shape
    qk, vw = A_HEADS * A_DK, A_HEADS * A_DV
    proj = (h @ w_in).astype(F32)
    q = proj[..., :qk].reshape(bsz, seq, A_HEADS, A_DK)
    k = proj[..., qk:2 * qk].reshape(bsz, seq, A_HEADS, A_DK) * (A_DK ** -0.5)
    v = proj[..., 2 * qk:2 * qk + vw].reshape(bsz, seq, A_HEADS, A_DV)
    o = jax.nn.sigmoid(proj[..., 2 * qk + vw:2 * qk + 2 * vw]).reshape(bsz, seq, A_HEADS, A_DV)
    gates = proj[..., 2 * qk + 2 * vw:] + b_gate.astype(F32)
    i_pre = gates[..., :A_HEADS]
    log_f = jax.nn.log_sigmoid(gates[..., A_HEADS:])
    causal = jnp.tril(jnp.ones((A_CHUNK, A_CHUNK), bool))

    def step(carry, xs):
        C, n, m = carry
        qc, kc, vc, ic, fc = xs
        b = jnp.cumsum(fc, axis=-1)
        dmat = jnp.where(causal, b[..., :, None] - b[..., None, :] + ic[..., None, :], -jnp.inf)
        m_inter = b + m[..., None]
        m_t = jnp.maximum(m_inter, dmat.max(-1))
        a = jnp.einsum('bhtd,bhsd->bhts', qc, kc) * jnp.exp(dmat - m_t[..., None])
        w_inter = jnp.exp(m_inter - m_t)
        num = jnp.einsum('bhts,bhse->bhte', a, vc) + w_inter[..., None] * jnp.einsum('bhtd,bhde->bhte', qc, C)
        den = a.sum(-1) + w_inter * jnp.einsum('bhtd,bhd->bht', qc, n)
        h_out = num / jnp.maximum(jnp.abs(den), jnp.exp(-m_t))[..., None]
        b_last = b[..., -1]
        g = b_last[..., None] - b + ic
        m_new = jnp.maximum(b_last + m, g.max(-1))
        decay = jnp.exp(b_last + m - m_new)
        ws = jnp.exp(g - m_new[..., None])
        C_new = decay[..., None, None] * C + jnp.einsum('bhs,bhsd,bhse->bhde', ws, kc, vc)
        n_new = decay[..., None] * n + jnp.einsum('bhs,bhsd->bhd', ws, kc)
        return (C_new, n_new, m_new), h_out

    init = (jnp.zeros((bsz, A_HEADS, A_DK, A_DV), F32),
            jnp.zeros((bsz, A_HEADS, A_DK), F32),
            jnp.zeros((bsz, A_HEADS), F32))
    xs = (to_chunks(q, A_CHUNK), to_chunks(k, A_CHUNK), to_chunks(v, A_CHUNK),
          to_chunks(i_pre, A_CHUNK), to_chunks(log_f, A_CHUNK))
    _, ys = lax.scan(step, init, xs)
    hs = from_chunks(ys)
    y = head_rms_norm(hs, norm_w.reshape(A_HEADS, A_DV)) * o
    return y.reshape(bsz, seq, vw).astype(w_out.dtype) @ w_out

def swa_mixer(h, positions, w_in, sinks, w_out):
    bsz, seq, _ = h.shape
    nb = seq // B_BLOCK
    grp = B_Q_HEADS // B_KV_HEADS
    qw, kw = B_Q_HEADS * B_HEAD_DIM, B_KV_HEADS * B_HEAD_DIM
    proj = h @ w_in
    q = partial_rope(proj[..., :qw].reshape(bsz, seq, B_Q_HEADS, B_HEAD_DIM), positions)
    k = partial_rope(proj[..., qw:qw + kw].reshape(bsz, seq, B_KV_HEADS, B_HEAD_DIM), positions)
    v = proj[..., qw + kw:].reshape(bsz, seq, B_KV_HEADS, B_HEAD_DIM)
    qb = jnp.moveaxis(q.reshape(bsz, nb, B_BLOCK, B_KV_HEADS, grp, B_HEAD_DIM), 1, 0)

    def band(a):
        ap = jnp.pad(a, ((0, 0), (B_BLOCK, 0), (0, 0), (0, 0)))
        ap = ap.reshape(bsz, nb + 1, B_BLOCK, B_KV_HEADS, B_HEAD_DIM)
        return jnp.moveaxis(jnp.concatenate([ap[:, :-1], ap[:, 1:]], axis=2), 1, 0)

    kb, vb = band(k), band(v)
    sink = sinks.astype(F32).reshape(1, B_KV_HEADS, grp, 1, 1)
    scale = B_HEAD_DIM ** -0.5

    def block(args):
        qi, ki, vi, n = args
        s = jnp.einsum('bqhgd,bkhd->bhgqk', qi, ki, preferred_element_type=F32) * scale
        qpos = n * B_BLOCK + jnp.arange(B_BLOCK)
        kpos = (n - 1) * B_BLOCK + jnp.arange(2 * B_BLOCK)
        rel = qpos[:, None] - kpos[None, :]
        valid = (rel >= 0) & (rel < B_WINDOW) & (kpos >= 0)[None, :]
        s = jnp.where(valid, s, -jnp.inf)
        mx = jnp.maximum(s.max(-1, keepdims=True), sink)
        p = jnp.exp(s - mx)
        p = p / (p.sum(-1, keepdims=True) + jnp.exp(sink - mx))
        return jnp.einsum('bhgqk,bkhd->bqhgd', p, vi.astype(F32))

    out = lax.map(block, (qb, kb, vb, jnp.arange(nb)))
    out = jnp.moveaxis(out, 0, 1).reshape(bsz, seq, qw)
    return out.astype(w_out.dtype) @ w_out

def hgrn2_mixer(h, lower_bound, w_in, norm_w, w_out):
    bsz, seq, _ = h.shape
    kw, vw = C_HEADS * C_DK, C_HEADS * C_DV
    proj = (h @ w_in).astype(F32)
    q = proj[..., :kw]
    f_pre = proj[..., kw:2 * kw]
    i_in = proj[..., 2 * kw:2 * kw + vw]
    g_out = proj[..., 2 * kw + vw:]
    lb = lower_bound.astype(F32)
    log_f = jnp.logaddexp(jnp.log(lb), jnp.log1p(-lb) + jax.nn.log_sigmoid(f_pre))
    k = (1.0 - lb) * jax.nn.sigmoid(-f_pre)
    heads = lambda a, d: a.reshape(bsz, seq, C_HEADS, d)
    causal = jnp.tril(jnp.ones((C_CHUNK, C_CHUNK), bool))[:, :, None]

    def step(S, xs):
        qc, kc, vc, fc = xs
        cf = jnp.cumsum(fc, axis=2)
        diff = cf[:, :, :, None, :] - cf[:, :, None, :, :]
        decay = jnp.exp(jnp.where(causal, diff, -jnp.inf))
        a = jnp.einsum('bhtd,bhtsd,bhsd->bhts', qc, decay, kc)
        o = jnp.einsum('bhts,bhse->bhte', a, vc) + jnp.einsum('bhtd,bhde->bhte', qc * jnp.exp(cf), S)
        last = cf[:, :, -1:, :]
        S_new = jnp.exp(last[:, :, 0, :])[..., None] * S + jnp.einsum('bhsd,bhse->bhde', kc * jnp.exp(last - cf), vc)
        return S_new, o

    xs = (to_chunks(heads(q, C_DK), C_CHUNK), to_chunks(heads(k, C_DK), C_CHUNK),
          to_chunks(heads(i_in, C_DV), C_CHUNK), to_chunks(heads(log_f, C_DK), C_CHUNK))
    _, ys = lax.scan(step, jnp.zeros((bsz, C_HEADS, C_DK, C_DV), F32), xs)
    o = from_chunks(ys)
    y = head_rms_norm(o, norm_w.reshape(C_HEADS, C_DV)) * jax.nn.silu(heads(g_out, C_DV))
    return y.reshape(bsz, seq, vw).astype(w_out.dtype) @ w_out

def diff_mixer(h, positions, lam_init, w_in, lam_vec, norm_w, w_out):
    bsz, seq, _ = h.shape
    nb = seq // D_QBLOCK
    w = D_HEADS * 2 * D_HEAD_DIM
    proj = h @ w_in
    q = partial_rope(proj[..., :w].reshape(bsz, seq, 2 * D_HEADS, D_HEAD_DIM), positions)
    k = partial_rope(proj[..., w:2 * w].reshape(bsz, seq, 2 * D_HEADS, D_HEAD_DIM), positions)
    q = q.reshape(bsz, seq, D_HEADS, 2, D_HEAD_DIM)
    k = k.reshape(bsz, seq, D_HEADS, 2, D_HEAD_DIM)
    v = proj[..., 2 * w:].reshape(bsz, seq, D_HEADS, 2 * D_HEAD_DIM).astype(F32)
    lv = lam_vec.astype(F32)
    lam = jnp.exp(jnp.sum(lv[0] * lv[1])) - jnp.exp(jnp.sum(lv[2] * lv[3])) + lam_init
    qb = jnp.moveaxis(q.reshape(bsz, nb, D_QBLOCK, D_HEADS, 2, D_HEAD_DIM), 1, 0)
    kpos = jnp.arange(seq)
    scale = D_HEAD_DIM ** -0.5

    def block(args):
        qi, n = args
        s = jnp.einsum('bqhcd,bkhcd->bhcqk', qi, k, preferred_element_type=F32) * scale
        qpos = n * D_QBLOCK + jnp.arange(D_QBLOCK)
        s = jnp.where(kpos[None, :] <= qpos[:, None], s, -jnp.inf)
        p = jax.nn.softmax(s, axis=-1)
        a = p[:, :, 0] - lam * p[:, :, 1]
        return jnp.einsum('bhqk,bkhe->bqhe', a, v)

    out = lax.map(block, (qb, jnp.arange(nb)))
    out = jnp.moveaxis(out, 0, 1).reshape(bsz, seq, D_HEADS, 2 * D_HEAD_DIM)
    out = head_rms_norm(out, norm_w) * (1.0 - lam_init)
    return out.reshape(bsz, seq, w).astype(w_out.dtype) @ w_out

def swiglu(h, w_in, w_out):
    gu = h @ w_in
    return (jax.nn.silu(gu[..., :FFN_HIDDEN]) * gu[..., FFN_HIDDEN:]) @ w_out

def second_inputs(seed: int = 0) -> dict:
    key = jax.random.key(seed)
    ks = jax.random.split(key, 26)
    nrm = lambda k, shape, s: jax.random.normal(k, shape, F32) * s
    D = D_MODEL
    beta = DEEPNORM_BETA
    x = nrm(ks[0], (BATCH, SEQ, D), 1.0)
    c = nrm(ks[1], (BATCH, D), 1.0)
    positions = jnp.broadcast_to(jnp.arange(SEQ, dtype=jnp.int32), (BATCH, SEQ))
    ada_w = nrm(ks[2], (DEPTH_2, 2, D, 3 * D), 0.1 * D ** -0.5)
    ada_b = nrm(ks[3], (DEPTH_2, 2, 3 * D), 0.01)
    ln_g = 1.0 + nrm(ks[4], (DEPTH_2, 2, D), 0.02)
    ln_b = nrm(ks[5], (DEPTH_2, 2, D), 0.01)
    mlstm_w_in = nrm(ks[6], (N_A, D, A_IN), D ** -0.5)
    mlstm_b_gate = jnp.concatenate(
        [nrm(ks[7], (N_A, A_HEADS), 0.1),
         jnp.linspace(3.0, 6.0, A_HEADS, dtype=F32) + nrm(ks[8], (N_A, A_HEADS), 0.1)], axis=-1)
    mlstm_norm = 1.0 + nrm(ks[9], (N_A, A_HEADS * A_DV), 0.02)
    mlstm_w_out = nrm(ks[10], (N_A, A_HEADS * A_DV, D), beta * (A_HEADS * A_DV) ** -0.5)
    swa_w_in = nrm(ks[11], (N_B, D, B_IN), D ** -0.5)
    swa_sinks = nrm(ks[12], (N_B, B_Q_HEADS), 0.5)
    swa_w_out = nrm(ks[13], (N_B, B_Q_HEADS * B_HEAD_DIM, D), beta * (B_Q_HEADS * B_HEAD_DIM) ** -0.5)
    hgrn_w_in = nrm(ks[14], (N_C, D, C_IN), D ** -0.5)
    hgrn_lower_bounds = nrm(ks[15], (DEPTH_2, C_HEADS * C_DK), 0.1)
    hgrn_norm = 1.0 + nrm(ks[16], (N_C, C_HEADS * C_DV), 0.02)
    hgrn_w_out = nrm(ks[17], (N_C, C_HEADS * C_DV, D), beta * (C_HEADS * C_DV) ** -0.5)
    diff_w_in = nrm(ks[18], (N_D, D, D_IN_2), D ** -0.5)
    diff_lambda = nrm(ks[19], (N_D, 4, D_HEAD_DIM), 0.1)
    diff_norm = 1.0 + nrm(ks[20], (N_D, 2 * D_HEAD_DIM), 0.02)
    diff_w_out = nrm(ks[21], (N_D, D_HEADS * 2 * D_HEAD_DIM, D), beta * (D_HEADS * 2 * D_HEAD_DIM) ** -0.5)
    ffn_w_in = nrm(ks[22], (DEPTH_2, D, 2 * FFN_HIDDEN), D ** -0.5)
    ffn_w_out = nrm(ks[23], (DEPTH_2, FFN_HIDDEN, D), beta * FFN_HIDDEN ** -0.5)
    return {"x": x, "c": c, "positions": positions, "ada_w": ada_w, "ada_b": ada_b,
            "ln_g": ln_g, "ln_b": ln_b,
            "mlstm_w_in": mlstm_w_in, "mlstm_b_gate": mlstm_b_gate, "mlstm_norm": mlstm_norm,
            "mlstm_w_out": mlstm_w_out,
            "swa_w_in": swa_w_in, "swa_sinks": swa_sinks, "swa_w_out": swa_w_out,
            "hgrn_w_in": hgrn_w_in, "hgrn_lower_bounds": hgrn_lower_bounds, "hgrn_norm": hgrn_norm,
            "hgrn_w_out": hgrn_w_out,
            "diff_w_in": diff_w_in, "diff_lambda": diff_lambda, "diff_norm": diff_norm,
            "diff_w_out": diff_w_out,
            "ffn_w_in": ffn_w_in, "ffn_w_out": ffn_w_out}

def second_block(x, c, positions, ada_w, ada_b, ln_g, ln_b,
              mlstm_w_in, mlstm_b_gate, mlstm_norm, mlstm_w_out,
              swa_w_in, swa_sinks, swa_w_out,
              hgrn_w_in, hgrn_lower_bounds, hgrn_norm, hgrn_w_out,
              diff_w_in, diff_lambda, diff_norm, diff_w_out,
              ffn_w_in, ffn_w_out):
    cond = jax.nn.silu(c.astype(F32))
    lbs = jnp.cumsum(jax.nn.softmax(hgrn_lower_bounds.astype(F32), axis=0), axis=0)
    lbs = lbs - lbs[0]
    for i in range(DEPTH_2):
        mixer, j = i % N_MIXERS, i // N_MIXERS
        mod = jnp.einsum('bd,sde->sbe', cond, ada_w[i].astype(F32)) + ada_b[i][:, None, :].astype(F32)
        shift, scale, gate = jnp.split(mod.astype(x.dtype), 3, axis=-1)
        h = x * (1 + scale[0][:, None]) + shift[0][:, None]
        if mixer == 0:
            y = mlstm_mixer(h, mlstm_w_in[j], mlstm_b_gate[j], mlstm_norm[j], mlstm_w_out[j])
        elif mixer == 1:
            y = swa_mixer(h, positions, swa_w_in[j], swa_sinks[j], swa_w_out[j])
        elif mixer == 2:
            y = hgrn2_mixer(h, lbs[i], hgrn_w_in[j], hgrn_norm[j], hgrn_w_out[j])
        else:
            lam_init = 0.8 - 0.6 * math.exp(-0.3 * i)
            y = diff_mixer(h, positions, lam_init, diff_w_in[j], diff_lambda[j], diff_norm[j], diff_w_out[j])
        x = layer_norm(DEEPNORM_ALPHA * x + (1 + gate[0][:, None]) * y.astype(x.dtype), ln_g[i, 0], ln_b[i, 0])
        h = x * (1 + scale[1][:, None]) + shift[1][:, None]
        y = swiglu(h, ffn_w_in[i], ffn_w_out[i])
        x = layer_norm(DEEPNORM_ALPHA * x + (1 + gate[1][:, None]) * y.astype(x.dtype), ln_g[i, 1], ln_b[i, 1])
    return x


def setup_inputs(seed=0):
    out = dict(first_inputs(seed))
    for name, value in second_inputs(seed + 1).items():
        if name != "x":
            out[name + "_2"] = value
    return out


def reference(
    x, norm_mix, w_in, conv_a_w, nsa_qk_gain, cmp_pe, cmp_w1, cmp_w2, gdn_conv_w, gdn_a_log,
    gdn_dt_bias, gdn_out_gain, w_branch, w_gate, b_gate, w_out, norm_ffn, w_router_group,
    b_router_group, w_router_expert, b_router_expert, w_expert_gate, w_expert_up, w_expert_down,
    c_2, positions_2, ada_w_2, ada_b_2, ln_g_2, ln_b_2, mlstm_w_in_2, mlstm_b_gate_2,
    mlstm_norm_2, mlstm_w_out_2, swa_w_in_2, swa_sinks_2, swa_w_out_2, hgrn_w_in_2,
    hgrn_lower_bounds_2, hgrn_norm_2, hgrn_w_out_2, diff_w_in_2, diff_lambda_2, diff_norm_2,
    diff_w_out_2, ffn_w_in_2, ffn_w_out_2,
):
    x = first_block(
        x, norm_mix, w_in, conv_a_w, nsa_qk_gain, cmp_pe, cmp_w1, cmp_w2, gdn_conv_w, gdn_a_log,
        gdn_dt_bias, gdn_out_gain, w_branch, w_gate, b_gate, w_out, norm_ffn, w_router_group,
        b_router_group, w_router_expert, b_router_expert, w_expert_gate, w_expert_up,
        w_expert_down,
    )
    return second_block(
        x, c_2, positions_2, ada_w_2, ada_b_2, ln_g_2, ln_b_2, mlstm_w_in_2, mlstm_b_gate_2,
        mlstm_norm_2, mlstm_w_out_2, swa_w_in_2, swa_sinks_2, swa_w_out_2, hgrn_w_in_2,
        hgrn_lower_bounds_2, hgrn_norm_2, hgrn_w_out_2, diff_w_in_2, diff_lambda_2, diff_norm_2,
        diff_w_out_2, ffn_w_in_2, ffn_w_out_2,
    )


_drawn_inputs = setup_inputs


def setup_inputs(seed=0):
    import zlib

    import numpy as np

    out = dict(_drawn_inputs(seed))
    spreads = {}
    factors = {'nsa_qk_gain': 5.988,
     'cmp_pe': 8.0,
     'gdn_out_gain': 4.898,
     'b_gate': 8.0,
     'b_router_group': 5.395,
     'b_router_expert': 4.738,
     'ada_b_2': 5.105,
     'mlstm_norm_2': 8.0,
     'swa_sinks_2': 8.0,
     'hgrn_lower_bounds_2': 6.007,
     'hgrn_norm_2': 8.0,
     'diff_norm_2': 8.0}
    for name, (base, spread) in spreads.items():
        noise = np.random.default_rng([zlib.crc32(name.encode()), seed]).standard_normal(out[name].shape)
        drawn = base * np.exp(spread * noise) if base else spread * noise
        out[name] = __import__('jax').numpy.asarray(drawn.astype(out[name].dtype))
    for name, factor in factors.items():
        out[name] = (out[name] * factor).astype(out[name].dtype)
    return out
```

```python
import math
from contextlib import ExitStack

import numpy as np

import concourse.bass as bass
from concourse import mybir

F32 = mybir.dt.float32
I32 = mybir.dt.int32
ALU = mybir.AluOpType
ACT = mybir.ActivationFunctionType
AX = mybir.AxisListType
P = 128
BANK = 512
NEG = -1e30


class Kept:
    pass


class Chain:

    def __init__(self, eng, sem):
        self.eng, self.sem, self.n = eng, sem, 0

    def __call__(self, ins):
        self.n += 1
        ins.then_inc(self.sem, 1)
        self.eng.wait_ge(self.sem, self.n)


class Stage:

    def __init__(self, nc, name):
        self.nc, self.name, self.ctx, self.sems = nc, name, ExitStack(), []

    def __enter__(self):
        self.ctx.__enter__()
        return self

    def __exit__(self, *a):
        out = self.ctx.__exit__(*a)
        if a[0] is None and self.sems:
            for sem in self.sems:
                self.nc.gpsimd.sem_clear(sem)
                self.nc.release_semaphore(sem)
        return out

    def sem(self, name):
        self.sems.append(self.nc.alloc_semaphore(f"{self.name}_{name}"))
        return self.sems[-1]

    def sb(self, name, shape, dt=F32):
        return self.ctx.enter_context(self.nc.sbuf_tensor(f"{self.name}_{name}", shape, dt))

    def block(self):
        return self.ctx.enter_context(self.nc.Block())


def persistent(nc, ctx, T):
    k = Kept()
    k.nc, k.T, k.NT, k.stop = nc, T, T // P, None
    sb = lambda name, shape: ctx.enter_context(nc.sbuf_tensor(name, shape, F32))
    k.X = sb("X", [P, k.NT, 1024])
    k.hT = sb("hT", [P, 8, T])
    k.ident = sb("ident", [P, P])
    k.ones = sb("ones", [P, P])
    k.zero = sb("zero", [P, P])
    k.upto = sb("upto", [P, P])
    k.nhalf = sb("nhalf", [P, 64])
    k.wring = sb("wring", [P, 3, 4096])
    k.mod = sb("mod", [P, 3072])
    k.ps = ctx.enter_context(nc.psum_tensor("ps", [P, 8, BANK], F32))
    with Stage(nc, "const") as st:
        filled = st.sem("filled")
        block = st.block()

        @block.gpsimd
        def _(pool):
            pool.memset(k.ident[:], 0.0).then_inc(filled, 1)
            pool.memset(k.ones[:], 1.0).then_inc(filled, 1)
            pool.memset(k.nhalf[:], -0.5)
            pool.memset(k.zero[:], 0.0)
            pool.wait_ge(filled, 2)
            pool.affine_select(out=k.ident[:], in_=k.ident[:], compare_op=ALU.not_equal, fill=1.0,
                               base=0, pattern=[[-1, P]], channel_multiplier=1)
            pool.affine_select(out=k.upto[:], in_=k.ones[:], compare_op=ALU.is_ge, fill=0.0,
                               base=0, pattern=[[1, P]], channel_multiplier=-1)
    return k


def load(k, name, pairs):
    nc = k.nc
    with Stage(nc, name) as st:
        landed = st.sem("landed")
        block = st.block()

        @block.sync
        def _(sp):
            with nc.allow_non_contiguous_dma("small vectors"):
                for dst, src in pairs:
                    sp.dma_start(dst, src).then_inc(landed, 16)
            sp.wait_ge(landed, 16 * len(pairs))


def rows(src, n=P):
    return src.partition_broadcast(n)


def gemm(k, name, xT, KT, w, N, finish, feature_major=False, bias=None):
    nc, T, ring, ps = k.nc, k.T, k.wring, k.ps
    chunks = [(n0, min(n0 + BANK, N)) for n0 in range(0, N, BANK)]
    R = 3
    with Stage(nc, name) as st:
        landed = [st.sem(f"landed{i}") for i in range(R)]
        filled = [st.sem(f"filled{j}") for j in range(2)]
        drained = [st.sem(f"drained{j}") for j in range(2)]
        block = st.block()

        def slot(c):
            n = chunks[c][1] - chunks[c][0]
            return ring[:, c % R, :KT * n].rearrange("p (k n) -> p k n", k=KT)

        def halves(c):
            n = chunks[c][1] - chunks[c][0]
            return [0, 1] if not feature_major or n > 2 * P else [0]

        @block.sync
        def _(sp):
            for c, (n0, n1) in enumerate(chunks):
                if c >= R:
                    sp.wait_ge(filled[1], c - R + 1)
                with nc.allow_non_contiguous_dma("narrow chunk"):
                    sp.dma_start(slot(c), w[:, n0:n1].rearrange("(k p) n -> p k n", p=P)
                                 ).then_inc(landed[c % R], 16)

        @block.tensor
        def _(pe):
            count = [0, 0]
            for c, (n0, n1) in enumerate(chunks):
                n = n1 - n0
                pe.wait_ge(landed[c % R], 16 * (c // R + 1))
                for j in halves(c):
                    if count[j] >= 2:
                        pe.wait_ge(drained[j], count[j] - 1)
                    bank = ps[:, 2 * j + count[j] % 2, :]
                    count[j] += 1
                    if feature_major:
                        for i in range(2 * j, min(2 * j + 2, -(-n // P))):
                            m = min(P, n - i * P)
                            for kt in range(KT):
                                last = pe.matmul(bank[:m, (i % 2) * T:(i % 2 + 1) * T],
                                                 slot(c)[:, kt, i * P:i * P + m], xT[:, kt, :],
                                                 start=kt == 0, stop=kt == KT - 1)
                    else:
                        for kt in range(KT):
                            last = pe.matmul(bank[:, :n], xT[:, kt, j * P:(j + 1) * P], slot(c)[:, kt, :],
                                             start=kt == 0, stop=kt == KT - 1 and bias is None)
                        if bias is not None:
                            last = pe.matmul(bank[:, :n], k.ones[0:1, :], bias[0:1, n0:n1],
                                             start=False, stop=True)
                    last.then_inc(filled[j], 1)

        def drain(eng, j):
            seen = 0
            for c, (n0, n1) in enumerate(chunks):
                if j not in halves(c):
                    continue
                eng.wait_ge(filled[j], seen + 1)
                last = finish(eng, ps[:, 2 * j + seen % 2, :], j, n0, n1)
                last.then_inc(drained[j], 1)
                seen += 1

        @block.scalar
        def _(act):
            drain(act, 0)

        @block.vector
        def _(dve):
            drain(dve, 1)


def transpose_in(k, name, src, dst, n_tiles=8, scale=None, src_cols=None,
                 factor=1.0):
    nc, T, ps = k.nc, k.T, k.ps
    cols = src_cols or (lambda t, i: src[:, t, i * P:(i + 1) * P])
    with Stage(nc, name) as st:
        turned, copied = st.sem("turned"), st.sem("copied")
        block = st.block()

        @block.tensor
        def _(pe):
            for i in range(n_tiles):
                if i >= 8:
                    pe.wait_ge(copied, i - 7)
                for t in range(k.NT):
                    last = pe.transpose(ps[:, i % 8, t * P:(t + 1) * P], cols(t, i), k.ident[:])
                last.then_inc(turned, 1)

        @block.scalar
        def _(act):
            for i in range(n_tiles):
                act.wait_ge(turned, i + 1)
                act.activation(dst[:, i, :], ps[:, i % 8, :T], ACT.Copy if scale is None else ACT.Identity,
                               scale=factor if scale is None else scale[:, i:i + 1]).then_inc(copied, 1)


def rms_rows(k, name, src, dst, gain=None, groups=1, mean=True, factor=1.0):
    nc, NT = k.nc, k.NT
    d = src.shape[2] // groups
    shape = [P, NT, groups, d]
    with Stage(nc, name) as st:
        sq = st.sb("sq", shape)
        ss = st.sb("ss", [P, NT, groups])
        step, summed, rooted = st.sem("step"), st.sem("summed"), st.sem("rooted")
        block = st.block()
        v = src.rearrange("p t (g d) -> p t g d", g=groups)
        w = dst.rearrange("p t (g d) -> p t g d", g=groups)
        sf = ss[:].rearrange("p t g -> p (t g)")
        c = 1.0 / d if mean else 1.0

        @block.vector
        def _(dve):
            after = Chain(dve, step)
            after(dve.tensor_tensor(sq[:], v, v, ALU.mult))
            after(dve.tensor_reduce(ss[:], sq[:], AX.X, ALU.add))
            dve.tensor_scalar(ss[:], ss[:], c / factor ** 2, 1e-6 / factor ** 2, ALU.mult, ALU.add
                              ).then_inc(summed, 1)
            dve.wait_ge(rooted, 1)
            op = dve.tensor_tensor(w, v, ss[:].unsqueeze(3).to_broadcast(shape), ALU.mult)
            if gain is not None:
                after(op)
                dve.tensor_tensor(w, w, gain.unsqueeze(1).unsqueeze(1).to_broadcast(shape), ALU.mult)

        @block.gpsimd
        def _(pool):
            pool.wait_ge(summed, 1)
            pool.tensor_tensor(sf, sf, k.nhalf[:, :NT * groups], ALU.pow).then_inc(rooted, 1)


def attention(k, name, units, q_of, k_of, v_of, bias_of, out_of, dv, sink_of=None, minus=None,
              keys=None):
    nc, ps = k.nc, k.ps
    G = len(units[0][0])
    keys = keys or (lambda t: list(range(t + 1)))
    NK = max(len(keys(t)) for _, t in units) * P
    O = G // 2 if minus else G
    with Stage(nc, name) as st:
        S = st.sb("S", [P, 2, G, NK])
        PT = st.sb("PT", [P, 2, O, NK])
        mx = st.sb("mx", [P, 2, G])
        sm = st.sb("sm", [P, 2, G])
        es = st.sb("es", [P, 2, G])
        step = st.sem("step")
        scored, biased, shifted, raised = st.sem("scored"), st.sem("biased"), st.sem("shifted"), st.sem("raised")
        mixed, turned, turned_out = st.sem("mixed"), st.sem("turned"), st.sem("turned_out")
        applied, stored, sunk = st.sem("applied"), st.sem("stored"), st.sem("sunk")
        block = st.block()
        sc = lambda u: ps[:, 2 * (u % 2):2 * (u % 2) + 2, :].rearrange("p b (g n) -> p g b n", n=256)
        pairs = lambda ap: ap.rearrange("p (g b) n -> p g b n", b=2)
        tr = ps[:, 4:6, :].rearrange("p b (g n) -> p (b g) n", n=256)
        ob = lambda u: ps[:, 6 + u % 2, :O * dv].rearrange("p (g n) -> p g n", n=dv)

        @block.tensor
        def _(pe):
            def scores(u):
                heads, t = units[u]
                if u >= 2:
                    pe.wait_ge(biased, u - 1)
                for g, h in enumerate(heads):
                    for i, kt in enumerate(keys(t)):
                        last = pe.matmul(sc(u)[:, g // 2, g % 2, i * P:(i + 1) * P], q_of(h, t), k_of(h, kt),
                                         start=True, stop=True)
                last.then_inc(scored, 1)

            scores(0)
            for u, (heads, t) in enumerate(units):
                if u + 1 < len(units):
                    scores(u + 1)
                if minus:
                    pe.wait_ge(mixed, u + 1)
                else:
                    pe.wait_ge(raised, u + 1)
                if u >= 1:
                    pe.wait_ge(turned_out, u)
                for g in range(O):
                    for i, kt in enumerate(keys(t)):
                        last = pe.transpose(tr[:, g, i * P:(i + 1) * P],
                                            S[:, u % 2, 2 * g if minus else g, i * P:(i + 1) * P], k.ident[:])
                last.then_inc(turned, 1)
                pe.wait_ge(turned_out, u + 1)
                if u >= 2:
                    pe.wait_ge(stored, u - 1)
                for g in range(O):
                    h = heads[2 * g] if minus else heads[g]
                    for i, kt in enumerate(keys(t)):
                        last = pe.matmul(ob(u)[:, g, :], PT[:, u % 2, g, i * P:(i + 1) * P], v_of(h, kt),
                                         start=i == 0, stop=i == len(keys(t)) - 1)
                last.then_inc(applied, 1)

        @block.scalar
        def _(act):
            for u, (heads, t) in enumerate(units):
                n = len(keys(t)) * P
                act.wait_ge(shifted, u + 1)
                act.activation(S[:, u % 2, :, :n], S[:, u % 2, :, :n], ACT.Exp).then_inc(raised, 1)
                if sink_of:
                    act.activation(es[:, u % 2, :], es[:, u % 2, :], ACT.Exp).then_inc(sunk, 1)
                act.wait_ge(turned, u + 1)
                if u >= 2:
                    act.wait_ge(applied, u - 1)
                act.activation(PT[:, u % 2, :, :n], tr[:, :O, :n], ACT.Copy).then_inc(turned_out, 1)

        @block.vector
        def _(dve):
            after = Chain(dve, step)

            def shift(u):
                heads, t = units[u]
                n = len(keys(t)) * P
                s, m, b = S[:, u % 2, :, :n], mx[:, u % 2, :], u % 2
                dve.wait_ge(scored, u + 1)
                if u >= 2:
                    dve.wait_ge(turned, u - 1)
                dve.tensor_tensor(pairs(s), sc(u)[:, :G // 2, :, :n], pairs(bias_of(heads, t)), ALU.add
                                  ).then_inc(biased, 1)
                dve.wait_ge(biased, u + 1)
                after(dve.tensor_reduce(m, s, AX.X, ALU.max))
                if sink_of:
                    after(dve.tensor_tensor(m, m, sink_of(heads), ALU.max))
                    after(dve.tensor_tensor(es[:, b, :], sink_of(heads), m, ALU.subtract))
                dve.tensor_tensor(s, s, m.unsqueeze(2).to_broadcast([P, G, n]), ALU.subtract
                                  ).then_inc(shifted, 1)

            def finish(u):
                heads, t = units[u]
                n = len(keys(t)) * P
                s, l = S[:, u % 2, :, :n], sm[:, u % 2, :]
                dve.wait_ge(raised, u + 1)
                after(dve.tensor_reduce(l, s, AX.X, ALU.add))
                if sink_of:
                    dve.wait_ge(sunk, u + 1)
                    after(dve.tensor_tensor(l, l, es[:, u % 2, :], ALU.add))
                after(dve.reciprocal(l, l))
                if minus:
                    after(dve.tensor_tensor(s, s, l.unsqueeze(2).to_broadcast([P, G, n]), ALU.mult))
                    for g in range(O):
                        last = dve.scalar_tensor_tensor(S[:, u % 2, 2 * g, :n], S[:, u % 2, 2 * g + 1, :n],
                                                        minus(g), S[:, u % 2, 2 * g, :n], ALU.mult, ALU.add)
                    last.then_inc(mixed, 1)

            shift(0)
            for u, (heads, t) in enumerate(units):
                if u + 1 < len(units):
                    shift(u + 1)
                finish(u)
                dve.wait_ge(applied, u + 1)
                out = out_of(heads, t)
                if minus:
                    dve.tensor_copy(out, ob(u)).then_inc(stored, 1)
                else:
                    dve.tensor_tensor(out, ob(u), sm[:, u % 2, :].unsqueeze(2).to_broadcast([P, G, dv]),
                                      ALU.mult).then_inc(stored, 1)


def dump(k, name, pairs):
    with Stage(k.nc, name) as st:
        stored = st.sem("stored")
        block = st.block()

        @block.sync
        def _(sp):
            for dst, src in pairs:
                sp.dma_start(dst, src).then_inc(stored, 16)
            sp.wait_ge(stored, 16 * len(pairs))


def on_vector(k, name, body):
    with Stage(k.nc, name) as st:
        step = st.sem("step")
        block = st.block()

        @block.vector
        def _(dve):
            body(dve, Chain(dve, step))


def on_scalar(k, name, body):
    with Stage(k.nc, name) as st:
        step = st.sem("step")
        block = st.block()

        @block.scalar
        def _(act):
            body(act, Chain(act, step))


def on_gpsimd(k, name, body):
    with Stage(k.nc, name) as st:
        step = st.sem("step")
        block = st.block()

        @block.gpsimd
        def _(pool):
            body(pool, Chain(pool, step))


def on_tensor(k, name, body):
    with Stage(k.nc, name) as st:
        block = st.block()

        @block.tensor
        def _(pe):
            body(pe)


def level_masks(k, masks):
    def body(pool, after):
        after(pool.memset(masks[:], 0.0))
        for v in range(7):
            b = 2 ** v
            half = masks[:, v, :].rearrange("s (n h j) -> s n h j", h=2, j=b)[:, :, 1, :]
            after(pool.memset(half, 1.0))
            after(pool.affine_select(out=half, in_=half, compare_op=ALU.is_ge, fill=0.0, base=0,
                                     pattern=[[-2 * b, P // (2 * b)], [0, b]], channel_multiplier=1))
            after(pool.affine_select(out=half, in_=half, compare_op=ALU.is_ge, fill=0.0, base=b - 1,
                                     pattern=[[2 * b, P // (2 * b)], [0, b]], channel_multiplier=-1))
    on_gpsimd(k, "level_masks", body)


def copier(nc, eng):
    return eng.copy if eng is nc.scalar else eng.tensor_copy


def tokens_to(k, dst):
    return lambda eng, psum, j, n0, n1: copier(k.nc, eng)(dst[:, j, n0:n1], psum[:, :n1 - n0])


def features_to(k, dst):
    def finish(eng, psum, j, n0, n1):
        i = n0 // P + 2 * j
        return copier(k.nc, eng)(dst[:, i:i + 2, :], psum[:, :2 * k.T].rearrange("p (i t) -> p i t", i=2))
    return finish


def turn_out(k, name, src, dst, n_tiles):
    with Stage(k.nc, name) as st:
        turned, copied = st.sem("turned"), st.sem("copied")
        block = st.block()
        groups = [(t, i, min(i + 4, n_tiles)) for t in range(k.NT) for i in range(0, n_tiles, 4)]

        @block.tensor
        def _(pe):
            for n, (t, i0, i1) in enumerate(groups):
                if n >= 8:
                    pe.wait_ge(copied, n - 7)
                for i in range(i0, i1):
                    last = pe.transpose(k.ps[:, n % 8, (i - i0) * P:(i - i0 + 1) * P],
                                        src[:, i, t * P:(t + 1) * P], k.ident[:])
                last.then_inc(turned, 1)

        @block.scalar
        def _(act):
            for n, (t, i0, i1) in enumerate(groups):
                act.wait_ge(turned, n + 1)
                act.copy(dst[:, t, i0 * P:i1 * P], k.ps[:, n % 8, :(i1 - i0) * P]).then_inc(copied, 1)


def alibi(k, name, table, dist, heads, width, step, offset):
    def fill(pool, after):
        for t in range(k.NT):
            after(pool.iota(dist[:, t, :], pattern=[[step, width]], base=offset - t * P,
                            channel_multiplier=-1, allow_small_or_imprecise_dtypes=True))
            for h in range(heads):
                after(pool.tensor_scalar(table[:, t, h, :width], dist[:, t, :],
                                         2.0 ** (-8.0 * (h + 1) / heads), None, ALU.mult))
            after(pool.affine_select(out=table[:, t, :, :width], in_=table[:, t, :, :width],
                                     compare_op=ALU.is_ge, fill=NEG, base=t * P - offset,
                                     pattern=[[0, heads], [-step, width]], channel_multiplier=1))
    on_gpsimd(k, name, fill)


def sparse_attention(k, A, scratch, y, ctx):
    nc, T, NT, ps = k.nc, k.T, k.NT, k.ps
    D, H, G = 64, 8, 2
    NC = (T - 32) // 16 + 1
    with ExitStack() as own:
        sb = lambda name, shape: own.enter_context(nc.sbuf_tensor("nsa_" + name, shape, F32))
        U = sb("U", [P, NT, 1304])
        gains = sb("gains", [P, 4, D])
        qT, kT = sb("qT", [P, 4, T]), sb("kT", [P, 2, 2, T])
        KD = sb("KD", [P, 2, NT, 2, 2, D])
        bias, dist = sb("bias", [P, NT, H, T]), sb("dist", [P, NT, T])
        O = sb("O", [P, NT, 3, H * D])
        flat = sb("flat", [2 * NC, 2, 2048])
        flatT = sb("flatT", [P, 2, 16, 2 * NC])
        pe_c = sb("pe_c", [P, 2, 16])
        w2 = sb("w2", [P, 2, 2, D])
        hid, g1, g2 = (sb(n, [P, 2, 2, 2 * NC]) for n in ("hid", "g1", "g2"))
        kc, vc = sb("kc", [2 * NC, 2, D]), sb("vc", [2 * NC, D])
        kss = sb("kss", [2 * NC, 1])
        kcT = sb("kcT", [P, 2 * NC])
        vbd = sb("vbd", [P, H * D])
        cb = sb("cb", [P, NT, H, 16])
        pc, pcT = sb("pc", [P, NT, H, 16]), sb("pcT", [P, NT, P])
        cm, cl, seen = sb("cm", [P, NT, H]), sb("cl", [P, NT, H]), sb("seen", [P, NT, H])

        load(k, "nsa_load", [(gains[:], A["nsa_qk_gain"][0].partition_broadcast(P)),
                             (pe_c[:, 0, :], A["cmp_pe"][0, 0].rearrange("(j l) d -> (l d) j", l=2)),
                             (pe_c[:, 1, :], A["cmp_pe"][0, 1].rearrange("(j l) d -> (l d) j", l=2)),
                             (w2[:, 0], A["cmp_w2"][0, 0].rearrange("(j p) d -> p j d", p=P)),
                             (w2[:, 1], A["cmp_w2"][0, 1].rearrange("(j p) d -> p j d", p=P))])
        alibi(k, "nsa_alibi", bias, dist, H, T, 1, 0)
        alibi(k, "nsa_alibi_c", cb, dist[:, :, :NC], H, NC, 16, 31)
        gemm(k, "nsa_in", k.hT, 8, A["w_in"][0][:, 1536:2840], 1304, tokens_to(k, U))
        dump(k, "nsa_out", [(scratch[c, g, t * P:(t + 1) * P, :],
                             U[:, t, 512 + (2 * c + g) * D:512 + (2 * c + g + 1) * D])
                            for c in range(2) for g in range(G) for t in range(NT)])
        load(k, "nsa_flat", [(flat[g * NC:(g + 1) * NC, c, :],
                              bass.AP(tensor=scratch.tensor, offset=(c * G + g) * T * D,
                                      ap=[[16 * D, NC], [1, 32 * D]]))
                             for c in range(2) for g in range(G)])

        def turn_flat(pe):
            for c in range(2):
                for j in range(16):
                    pe.transpose(ps[:, c, j * 2 * NC:(j + 1) * 2 * NC], flat[:, c, j * P:(j + 1) * P],
                                 k.ident[:2 * NC, :2 * NC])
        on_tensor(k, "nsa_tf", turn_flat)

        def add_pe(dve, after):
            for c in range(2):
                dve.tensor_tensor(flatT[:, c], ps[:, c, :32 * NC].rearrange("p (j n) -> p j n", j=16),
                                  pe_c[:, c, :].unsqueeze(2).to_broadcast([P, 16, 2 * NC]), ALU.add)
        on_vector(k, "nsa_pe", add_pe)
        for c in range(2):
            compress_hidden(k, f"nsa_c{c}", A["cmp_w1"][0, c], flatT[:, c], hid[:, c])

        def gelu_a(dve, after):
            after(dve.tensor_tensor(g1[:], hid[:], hid[:], ALU.mult))
            after(dve.tensor_scalar(g1[:], g1[:], 0.044715, 1.0, ALU.mult, ALU.add))
            after(dve.tensor_tensor(g1[:], g1[:], hid[:], ALU.mult))
        on_vector(k, "nsa_ga", gelu_a)
        on_scalar(k, "nsa_gb", lambda act, after:
                  act.activation(g2[:], g1[:], ACT.Tanh, scale=math.sqrt(2 / math.pi)))

        def gelu_c(dve, after):
            after(dve.tensor_scalar(g2[:], g2[:], 1.0, 0.5, ALU.add, ALU.mult))
            after(dve.tensor_tensor(hid[:], hid[:], g2[:], ALU.mult))
        on_vector(k, "nsa_gc", gelu_c)

        def second(pe):
            for c in range(2):
                for j in range(2):
                    pe.matmul(ps[:2 * NC, c, :D], hid[:, c, j, :], w2[:, c, j, :], start=j == 0, stop=j == 1)
        on_tensor(k, "nsa_w2", second)

        def kc_norm(dve, after):
            after(dve.memset(vbd[:], 0.0))
            after(dve.tensor_copy(vc[:], ps[:2 * NC, 1, :D]))
            after(dve.tensor_copy(kc[:, 0, :], ps[:2 * NC, 0, :D]))
            after(dve.tensor_tensor(kc[:, 1, :], kc[:, 0, :], kc[:, 0, :], ALU.mult))
            after(dve.tensor_reduce(kss[:], kc[:, 1, :], AX.X, ALU.add))
            after(dve.tensor_scalar(kss[:], kss[:], 1.0 / D, 1e-6, ALU.mult, ALU.add))
        on_vector(k, "nsa_kn", kc_norm)
        on_gpsimd(k, "nsa_kr", lambda pool, after:
                  pool.tensor_tensor(kss[:], kss[:], k.nhalf[:2 * NC, :1], ALU.pow))

        def kc_scale(dve, after):
            after(dve.scalar_tensor_tensor(kc[:, 0, :], kc[:, 0, :], kss[:, 0:1], gains[:2 * NC, 1, :],
                                           ALU.mult, ALU.mult))
            dve.tensor_copy(kc[:, 1, :], kc[:, 0, :])
        on_vector(k, "nsa_ks", kc_scale)
        load(k, "nsa_vbd", [(vbd[16 * h:16 * h + NC, h * D:(h + 1) * D],
                             vc[(h // 4) * NC:(h // 4 + 1) * NC, :]) for h in range(H)])
        on_tensor(k, "nsa_kt", lambda pe: pe.transpose(
            ps[:, 0, :2 * NC], kc[:].rearrange("n u d -> n (u d)"), k.ident[:2 * NC, :2 * NC]))
        on_vector(k, "nsa_kv", lambda dve, after: dve.tensor_copy(kcT[:], ps[:, 0, :2 * NC]))

        rms_rows(k, "nsa_q", U[:, :, 0:512], U[:, :, 0:512], gains[:, 0, :], groups=H)
        for n, (a, gi) in enumerate(((768, 2), (1024, 3))):
            rms_rows(k, f"nsa_k{n}", U[:, :, a:a + 128], U[:, :, a:a + 128], gains[:, gi, :], groups=G)

        def twice(dve, after):
            for n, a in enumerate((768, 1024)):
                for u in range(2):
                    dve.tensor_copy(KD[:, n, :, :, u, :], U[:, :, a:a + 128].rearrange("p t (g d) -> p t g d", g=G))
        on_vector(k, "nsa_twice", twice)
        transpose_in(k, "nsa_qT", U, qT, 4, factor=D ** -0.5)
        for n in range(2):
            transpose_in(k, f"nsa_kT{n}", None, kT[:, n], 2,
                         src_cols=lambda t, i, n=n: KD[:, n, t, i].rearrange("p u d -> p (u d)"))
        half = lambda h: slice((h % 2) * D, (h % 2 + 1) * D)
        units = [(list(range(g * 4, g * 4 + 4)), t) for t in range(NT) for g in range(G)]
        for n, a in enumerate((896, 1152)):
            attention(k, f"nsa_a{n}", units,
                      q_of=lambda h, t: qT[half(h), h // 2, t * P:(t + 1) * P],
                      k_of=lambda h, kt, n=n: kT[half(h), n, h // 4, kt * P:(kt + 1) * P],
                      v_of=lambda h, kt, a=a: U[:, kt, a + (h // 4) * D:a + (h // 4 + 1) * D],
                      bias_of=lambda hs, t: bias[:, t, hs[0]:hs[-1] + 1, :(t + 1) * P],
                      out_of=lambda hs, t, n=n: O[:, t, 1 + n, hs[0] * D:(hs[-1] + 1) * D].rearrange(
                          "p (g d) -> p g d", d=D), dv=D)

        def c_scores(pe):
            for t in range(NT):
                for h in range(H):
                    pe.matmul(ps[:, 2 * t + h % 2, h // 2 * 16:h // 2 * 16 + NC], qT[half(h), h // 2, t * P:(t + 1) * P],
                              kcT[half(h), (h // 4) * NC:(h // 4 + 1) * NC], start=True, stop=True)
        on_tensor(k, "nsa_cs", c_scores)
        flat2 = lambda x: x[:].rearrange("p t h -> p (t h)")
        pcv = pc[:].rearrange("p t h n -> p (t h) n")

        def c_shift(dve, after):
            after(dve.memset(pc[:], 0.0))
            for t in range(NT):
                pair = lambda x: x[:, t].rearrange("p (g b) n -> p g b n", b=2)[:, :, :, :NC]
                after(dve.tensor_tensor(pair(pc), ps[:, 2 * t:2 * t + 2, :64].rearrange(
                    "p b (g n) -> p g b n", n=16)[:, :, :, :NC], pair(cb), ALU.add))
            after(dve.tensor_reduce(flat2(cm), pcv[:, :, :NC], AX.X, ALU.max))
            after(dve.tensor_tensor(pcv[:, :, :NC], pcv[:, :, :NC],
                                    flat2(cm).unsqueeze(2).to_broadcast([P, NT * H, NC]), ALU.subtract))
            after(dve.tensor_scalar(seen[:], cm[:], NEG / 2, None, ALU.is_gt))
        on_vector(k, "nsa_c1", c_shift)
        on_scalar(k, "nsa_c2", lambda act, after: act.activation(pcv[:, :, :NC], pcv[:, :, :NC], ACT.Exp))

        def c_norm(dve, after):
            after(dve.tensor_reduce(flat2(cl), pcv[:, :, :NC], AX.X, ALU.add))
            after(dve.reciprocal(cl[:], cl[:]))
            after(dve.tensor_tensor(cl[:], cl[:], seen[:], ALU.mult))
            dve.tensor_tensor(pcv[:, :, :NC], pcv[:, :, :NC],
                              flat2(cl).unsqueeze(2).to_broadcast([P, NT * H, NC]), ALU.mult)
        on_vector(k, "nsa_c3", c_norm)
        on_tensor(k, "nsa_c4", lambda pe: [pe.transpose(
            ps[:, t, :P], pc[:, t].rearrange("p h n -> p (h n)"), k.ident[:]) for t in range(NT)])
        on_vector(k, "nsa_c5", lambda dve, after: [dve.tensor_copy(pcT[:, t], ps[:, t, :P]) for t in range(NT)])
        on_tensor(k, "nsa_c6", lambda pe: [pe.matmul(ps[:, t, :], pcT[:, t], vbd[:], start=True, stop=True)
                                           for t in range(NT)])
        gates = U[:, :, 1280:1304]
        on_scalar(k, "nsa_g", lambda act, after: act.activation(gates, gates, ACT.Sigmoid))

        def combine(dve, after):
            for t in range(NT):
                after(dve.tensor_copy(O[:, t, 0, :], ps[:, t, :]))
                Ot = O[:, t].rearrange("p b (h d) -> p (b h) d", d=D)
                after(dve.tensor_tensor(Ot, Ot, U[:, t, 1280:1304].unsqueeze(2).to_broadcast([P, 24, D]), ALU.mult))
                after(dve.tensor_tensor(y[:, t, :], O[:, t, 0, :], O[:, t, 1, :], ALU.add))
                after(dve.tensor_tensor(y[:, t, :], y[:, t, :], O[:, t, 2, :], ALU.add))
        on_vector(k, "nsa_y", combine)


def compress_hidden(k, name, w1, xT, hid):
    nc, ps, N = k.nc, k.ps, xT.shape[2]
    w = k.wring[:, 0, :].rearrange("p (k n) -> p k n", k=16)
    with Stage(nc, name) as st:
        landed, filled = st.sem("landed"), st.sem("filled")
        block = st.block()

        @block.sync
        def _(sp):
            sp.dma_start(w, w1.rearrange("(k p) n -> p k n", p=P)).then_inc(landed, 16)

        @block.tensor
        def _(pe):
            pe.wait_ge(landed, 16)
            for j in range(2):
                for kt in range(16):
                    last = pe.matmul(ps[:, j, :N], w[:, kt, j * P:(j + 1) * P], xT[:, kt, :],
                                     start=kt == 0, stop=kt == 15)
                last.then_inc(filled, 1)

        @block.vector
        def _(dve):
            for j in range(2):
                dve.wait_ge(filled, j + 1)
                dve.tensor_copy(hid[:, j, :], ps[:, j, :N])


def column(v, n=None):
    return v.rearrange("(i p) -> p i", p=P)


def gated_delta(k, A, masks, y):
    nc, T, NT, ps = k.nc, k.T, k.NT, k.ps
    H, D = 4, 128
    assert NT == 2
    with ExitStack() as own:
        sb = lambda name, shape: own.enter_context(nc.sbuf_tensor("gdn_" + name, shape, F32))
        cw = sb("cw", [P, 4, 12])
        alog, dt, gain = sb("alog", [P, H]), sb("dt", [P, H]), sb("gain", [P, D])
        Z = sb("Z", [P, NT, 520])
        raw, conv = sb("raw", [P, 12, T + 3]), sb("conv", [P, 12, T])
        tok = sb("tok", [P, NT, 1536])
        load(k, "gdn_load", [(cw[:, j, :], column(A["gdn_conv_w"][0, j])) for j in range(4)]
             + [(alog[:], rows(A["gdn_a_log"][0])), (dt[:], rows(A["gdn_dt_bias"][0])),
                (gain[:], rows(A["gdn_out_gain"][0]))])
        gemm(k, "gdn_in", k.hT, 8, A["w_in"][0][:, 2840:4376], 1536, features_to(k, raw[:, :, 3:]),
             feature_major=True)
        gemm(k, "gdn_z", k.hT, 8, A["w_in"][0][:, 4376:4896], 520, tokens_to(k, Z))

        def convolve(dve, after):
            after(dve.memset(raw[:, :, 0:3], 0.0))
            for j in range(4):
                for i in range(12):
                    if j == 0:
                        op = dve.tensor_scalar(conv[:, i, :], raw[:, i, 0:T], cw[:, 0, i:i + 1], None, ALU.mult)
                    else:
                        op = dve.scalar_tensor_tensor(conv[:, i, :], raw[:, i, j:j + T], cw[:, j, i:i + 1],
                                                      conv[:, i, :], ALU.mult, ALU.add)
                after(op)
        on_vector(k, "gdn_conv", convolve)
        on_scalar(k, "gdn_silu", lambda act, after: act.activation(conv[:], conv[:], ACT.Silu))
        turn_out(k, "gdn_tok", conv, tok, 12)
        rms_rows(k, "gdn_q", tok[:, :, 0:512], tok[:, :, 0:512], groups=H, mean=False, factor=D ** -0.5)
        rms_rows(k, "gdn_k", tok[:, :, 512:1024], tok[:, :, 512:1024], groups=H, mean=False)
        beta, sp, ab, g = (sb(n, [P, NT, H]) for n in ("beta", "sp", "ab", "g"))
        gcs = sb("gcs", [P, NT, 2, H])
        e1, e2 = sb("e1", [P, NT, H]), sb("e2", [P, NT, H])

        def decay_in(dve, after):
            after(dve.tensor_tensor(sp[:], Z[:, :, 516:520], dt[:].unsqueeze(1).to_broadcast([P, NT, H]), ALU.add))
            after(dve.tensor_scalar(ab[:], sp[:], -1.0, None, ALU.mult))
            after(dve.tensor_tensor(ab[:], ab[:], sp[:], ALU.min))
        on_vector(k, "gdn_g1", decay_in)

        def soft(act, after):
            after(act.activation(ab[:], ab[:], ACT.Exp))
            after(act.activation(ab[:], ab[:], ACT.Ln, bias=1.0))
            act.activation(alog[:], alog[:], ACT.Exp)
            act.activation(beta[:], Z[:, :, 512:516], ACT.Sigmoid)
            act.activation(Z[:, :, 0:512], Z[:, :, 0:512], ACT.Silu)
        on_scalar(k, "gdn_g2", soft)

        def decay(dve, after):
            after(dve.scalar_tensor_tensor(g[:], sp[:], 0.0, ab[:], ALU.max, ALU.add))
            after(dve.scalar_tensor_tensor(g[:], g[:], -1.0, alog[:].unsqueeze(1).to_broadcast([P, NT, H]),
                                           ALU.mult, ALU.mult))
        on_vector(k, "gdn_g3", decay)
        part = lambda x, i: x[:].rearrange("p a b -> p (a b)")[:, i * NT * H * P:(i + 1) * NT * H * P].rearrange(
            "p (t h c) -> p t h c", t=NT, h=H)
        grep, Ti, XX = (part(conv, i) for i in range(3))
        kb, kbg, CT = (part(raw, i) for i in range(3))
        on_vector(k, "gdn_g4", lambda dve, after: dve.tensor_copy(
            grep, g[:].unsqueeze(3).to_broadcast([P, NT, H, P])))

        def running(pe):
            for t in range(NT):
                pe.matmul(ps[:, t, 0:H], k.upto[:], g[:, t, :], start=True, stop=True)
                pe.matmul(ps[:, t, H:2 * H], k.ones[:], g[:, t, :], start=True, stop=True)
                for h in range(H):
                    pe.matmul(ps[:, 2 + t, h * P:(h + 1) * P], grep[:, t, h, :], k.upto[:], start=True, stop=True)
        on_tensor(k, "gdn_run", running)
        DT = sb("DT", [P, NT, H, P])

        def decays(dve, after):
            after(dve.tensor_copy(gcs[:].rearrange("p t u h -> p t (u h)"), ps[:, 0:2, :2 * H]))
            after(dve.tensor_copy(e1[:], gcs[:, :, 0, :]))
            after(dve.tensor_tensor(e2[:], gcs[:, :, 1, :], gcs[:, :, 0, :], ALU.subtract))
            after(dve.tensor_tensor(DT[:], ps[:, 2:4, :].rearrange("p t (h c) -> p t h c", h=H),
                                    e1[:].unsqueeze(3).to_broadcast([P, NT, H, P]), ALU.subtract))
            after(dve.tensor_scalar(DT[:], DT[:], 0.0, None, ALU.min))
        on_vector(k, "gdn_d1", decays)

        el = sb("el", [P, NT, H])

        def exps(act, after):
            act.activation(DT[:], DT[:], ACT.Exp)
            act.activation(el[:], gcs[:, :, 1, :], ACT.Exp)
            act.activation(e1[:], e1[:], ACT.Exp)
            act.activation(e2[:], e2[:], ACT.Exp)
        on_scalar(k, "gdn_d2", exps)
        vb, kd = (sb(n, [P, NT, H, D]) for n in ("vb", "kd"))
        qd = sb("qd", [P, H, D])
        q4, k4, v4 = (tok[:, :, a:a + 512].rearrange("p t (h d) -> p t h d", h=H) for a in (0, 512, 1024))
        by = lambda x: x.unsqueeze(3).to_broadcast([P, NT, H, D])

        def weigh(dve, after):
            dve.tensor_tensor(DT[:], DT[:], k.upto[:].unsqueeze(1).unsqueeze(1).to_broadcast([P, NT, H, P]), ALU.mult)
            dve.tensor_tensor(vb[:], v4, by(beta[:]), ALU.mult)
            dve.tensor_tensor(kd[:], k4, by(e2[:]), ALU.mult)
            dve.tensor_tensor(qd[:], q4[:, 1], e1[:, 1].unsqueeze(2).to_broadcast([P, H, D]), ALU.mult)
            after(dve.tensor_tensor(kb, k4, by(beta[:]), ALU.mult))
            dve.tensor_tensor(kbg, kb, by(e1[:]), ALU.mult)
        on_vector(k, "gdn_w", weigh)
        qT, kT, kbT, qdT = (sb(n, [P, H, T]) for n in ("qT", "kT", "kbT", "qdT"))
        for n, (src, dst) in enumerate(((tok[:, :, 0:512], qT), (tok[:, :, 512:1024], kT),
                                        (kb.rearrange("p t h d -> p t (h d)"), kbT))):
            transpose_in(k, f"gdn_t{n}", src, dst, H)
        transpose_in(k, "gdn_t3", None, qdT, H, src_cols=lambda t, i: qd[:, i, :])
        MT, AT = sb("MT", [P, NT, H, P]), sb("AT", [P, NT, H, P])

        def products(pe):
            for t in range(NT):
                for h in range(H):
                    kh = kT[:, h, t * P:(t + 1) * P]
                    pe.matmul(ps[:, t, h * P:(h + 1) * P], kh, kbT[:, h, t * P:(t + 1) * P], start=True, stop=True)
                    pe.matmul(ps[:, 2 + t, h * P:(h + 1) * P], kh, qT[:, h, t * P:(t + 1) * P], start=True, stop=True)
        on_tensor(k, "gdn_kk", products)
        bank = lambda i: ps[:, i:i + 2, :].rearrange("p t (h c) -> p t h c", h=H)
        on_vector(k, "gdn_m", lambda dve, after: [
            dve.tensor_tensor(MT[:], bank(0), DT[:], ALU.mult), dve.tensor_tensor(AT[:], bank(2), DT[:], ALU.mult)])
        TT = sb("TT", [P, NT, H, P])
        solve_unit_triangle(k, "gdn_s", MT, masks, Ti, TT[:], CT, XX, NT, H)

        vn, S = vb, sb("S", [P, H, D])
        wT = sb("wT", [P, H, P])

        def uw(pe):
            for h in range(H):
                for t in range(NT):
                    pe.matmul(ps[:, t, h * D:(h + 1) * D], TT[:, t, h, :], vb[:, t, h, :], start=True, stop=True)
                pe.matmul(ps[:, 2, h * P:(h + 1) * P], kbg[:, 1, h, :], TT[:, 1, h, :], start=True, stop=True)
        on_tensor(k, "gdn_uw", uw)
        on_vector(k, "gdn_u", lambda dve, after: [
            dve.tensor_copy(vn[:], bank(0)),
            dve.tensor_copy(wT[:], ps[:, 2, :].rearrange("p (h c) -> p h c", h=H))])

        def first_chunk(pe):
            for h in range(H):
                pe.matmul(ps[:, 0, h * D:(h + 1) * D], AT[:, 0, h, :], vn[:, 0, h, :], start=True, stop=True)
                pe.matmul(ps[:, 1, h * D:(h + 1) * D], kd[:, 0, h, :], vn[:, 0, h, :], start=True, stop=True)
        on_tensor(k, "gdn_c0", first_chunk)
        on_vector(k, "gdn_s0", lambda dve, after: [
            dve.tensor_copy(tok[:, 0, 0:512], ps[:, 0, :]),
            dve.tensor_copy(S[:], ps[:, 1, :].rearrange("p (h c) -> p h c", h=H))])
        on_tensor(k, "gdn_ws", lambda pe: [pe.matmul(ps[:, 0, h * D:(h + 1) * D], wT[:, h, :], S[:, h, :],
                                                     start=True, stop=True) for h in range(H)])
        on_vector(k, "gdn_v1", lambda dve, after: dve.tensor_tensor(
            vn[:, 1], vn[:, 1], ps[:, 0, :].rearrange("p (h c) -> p h c", h=H), ALU.subtract))

        def second_chunk(pe):
            for h in range(H):
                pe.matmul(ps[:, 1, h * D:(h + 1) * D], qdT[:, h, P:2 * P], S[:, h, :], start=True, stop=False)
                pe.matmul(ps[:, 1, h * D:(h + 1) * D], AT[:, 1, h, :], vn[:, 1, h, :], start=False, stop=True)
        on_tensor(k, "gdn_c1", second_chunk)
        on_vector(k, "gdn_o1", lambda dve, after: dve.tensor_copy(tok[:, 1, 0:512], ps[:, 1, :]))
        rms_rows(k, "gdn_o", tok[:, :, 0:512], tok[:, :, 512:1024], gain[:], groups=H)
        on_vector(k, "gdn_y", lambda dve, after: dve.tensor_tensor(
            y[:], tok[:, :, 512:1024], Z[:, :, 0:512], ALU.mult))


def solve_unit_triangle(k, name, MT, masks, Ti, TT, CT, XX, NT, H):
    ps, nc = k.ps, k.nc
    b = lambda i: ps[:, i, :].rearrange("p (h c) -> p h c", h=H)
    with Stage(nc, name) as st:
        step = st.sem("step")
        joined = [st.sem(f"joined{t}") for t in range(NT)]
        crossed = [st.sem(f"crossed{t}") for t in range(NT)]
        held = [st.sem(f"held{t}") for t in range(NT)]
        closed = [st.sem(f"closed{t}") for t in range(NT)]
        block = st.block()
        L = masks.shape[1]

        @block.vector
        def _(dve):
            after = Chain(dve, step)
            for x in (Ti, TT):
                op = dve.tensor_copy(x, k.ident[:].unsqueeze(1).unsqueeze(1).to_broadcast([P, NT, H, P]))
            after(op)
            for v in range(L):
                for t in range(NT):
                    dve.tensor_tensor(CT[:, t], MT[:, t], masks[:, v, :].unsqueeze(1).to_broadcast([P, H, P]),
                                      ALU.mult).then_inc(joined[t], 1)
                for t in range(NT):
                    dve.wait_ge(crossed[t], v + 1)
                    dve.tensor_copy(XX[:, t], b(t)).then_inc(held[t], 1)
                for t in range(NT):
                    dve.wait_ge(closed[t], v + 1)
                    dve.tensor_tensor(Ti[:, t], Ti[:, t], b(2 + t), ALU.subtract)
                    op = dve.tensor_tensor(TT[:, t], TT[:, t], b(4 + t), ALU.subtract)
                after(op)

        @block.tensor
        def _(pe):
            for v in range(L):
                for t in range(NT):
                    pe.wait_ge(joined[t], v + 1)
                    for h in range(H):
                        last = pe.matmul(b(t)[:, h], CT[:, t, h], Ti[:, t, h], start=True, stop=True)
                    last.then_inc(crossed[t], 1)
                for t in range(NT):
                    pe.wait_ge(held[t], v + 1)
                    for h in range(H):
                        pe.matmul(b(2 + t)[:, h], TT[:, t, h], XX[:, t, h], start=True, stop=True)
                        last = pe.matmul(b(4 + t)[:, h], XX[:, t, h], TT[:, t, h], start=True, stop=True)
                    last.then_inc(closed[t], 1)


def short_conv(k, A, y):
    nc, T = k.nc, k.T
    with ExitStack() as own:
        sb = lambda name, shape: own.enter_context(nc.sbuf_tensor("sc_" + name, shape, F32))
        cw, u, cx = sb("cw", [P, 3, 4]), sb("u", [P, 12, T]), sb("cx", [P, 4, T + 2])
        load(k, "sc_load", [(cw[:, j, :], column(A["conv_a_w"][0, j])) for j in range(3)])
        gemm(k, "sc_in", k.hT, 8, A["w_in"][0][:, 0:1536], 1536, features_to(k, u), feature_major=True)

        def body(dve, after):
            after(dve.memset(cx[:, :, 0:2], 0.0))
            after(dve.tensor_tensor(cx[:, :, 2:], u[:, 4:8, :], u[:, 8:12, :], ALU.mult))
            for j in range(3):
                for i in range(4):
                    if j == 0:
                        op = dve.tensor_scalar(y[:, i, :], cx[:, i, 0:T], cw[:, 0, i:i + 1], None, ALU.mult)
                    else:
                        op = dve.scalar_tensor_tensor(y[:, i, :], cx[:, i, j:j + T], cw[:, j, i:i + 1],
                                                      y[:, i, :], ALU.mult, ALU.add)
                after(op)
            dve.tensor_tensor(y[:], y[:], u[:, 0:4, :], ALU.mult)
        on_vector(k, "sc_conv", body)


def merge_branches(k, A, yT):
    nc, NT = k.nc, k.NT
    with ExitStack() as own:
        sb = lambda name, shape: own.enter_context(nc.sbuf_tensor("mb_" + name, shape, F32))
        gates, tmp, merged = sb("gates", [P, NT, 3072]), sb("tmp", [P, NT, BANK]), sb("merged", [P, NT, 1024])
        bias = sb("bias", [1, 3072])
        load(k, "mb_load", [(bias[:], A["b_gate"])])
        gemm(k, "mb_gates", k.hT, 8, A["w_gate"][0], 3072, tokens_to(k, gates), bias=bias)
        on_scalar(k, "mb_sig", lambda act, after: act.activation(gates[:], gates[:], ACT.Sigmoid))
        for r in range(3):
            branch = sb(f"branch{r}", [P, NT, 1024]) if r == 0 else branch
            gemm(k, f"mb_branch{r}", yT[r], 4, A["w_branch"][0, r], 1024, tokens_to(k, branch))

            def weigh(dve, after, r=r):
                g = gates[:, :, r * 1024:(r + 1) * 1024]
                after(dve.tensor_tensor(merged[:] if r == 0 else branch[:], branch[:], g, ALU.mult))
                if r:
                    dve.tensor_tensor(merged[:], merged[:], branch[:], ALU.add)
            on_vector(k, f"mb_w{r}", weigh)
        transpose_in(k, "mb_t", merged, k.hT)
        gemm(k, "mb_out", k.hT, 8, A["w_out"][0], 1024, tokens_to(k, branch))
        on_vector(k, "mb_x", lambda dve, after: dve.tensor_tensor(k.X[:], k.X[:], branch[:], ALU.add))


def swiglu(k, name, n_blocks, source, seed, finish, weigh=False):
    nc, T, NT, ps = k.nc, k.T, k.NT, k.ps
    U, FT = 2, 2
    whole, rest = divmod(n_blocks, U)
    W = k.wring[:].rearrange("p a b -> p (a b)")[:, :U * 6144].rearrange("p (u n) -> p u n", u=U)
    gate = lambda u: W[:, u, 0:2048].rearrange("p (k n) -> p k n", k=8)
    up = lambda u: W[:, u, 2048:4096].rearrange("p (k n) -> p k n", k=8)
    down = lambda u: W[:, u, 4096:6144].rearrange("p (f n) -> p f n", f=FT)
    with Stage(nc, name) as st:
        act_out = st.sb("silu", [P, U * FT, T])
        hidden = st.sb("hidden", [P, U * FT, T])
        factor = st.sb("factor", [P, U, T]) if weigh else None
        landed_in = [st.sem(f"landed_in{u}") for u in range(U)]
        landed_out = [st.sem(f"landed_out{u}") for u in range(U)]
        read_out = [st.sem(f"read_out{u}") for u in range(U)]
        filled = [st.sem(f"filled{b}") for b in range(U * FT)]
        silued = [st.sem(f"silued{b}") for b in range(U * FT)]
        hid = [st.sem(f"hid{b}") for b in range(U * FT)]
        weighed = st.sem("weighed")
        summed, stored = st.sem("summed"), st.sem("stored")
        block = st.block()
        N_IN = 48 if weigh else 32

        @block.sync
        def _(sp):
            def fetch_in(i, u):
                g, v, _, f = source(i, u)
                sp.dma_start(gate(u), g.rearrange("(k p) n -> p k n", p=P)).then_inc(landed_in[u], 16)
                sp.dma_start(up(u), v.rearrange("(k p) n -> p k n", p=P)).then_inc(landed_in[u], 16)
                if weigh:
                    sp.dma_start(factor[:, u, :], f.partition_broadcast(P)).then_inc(landed_in[u], 16)

            def fetch_out(i, u):
                _, _, d, _ = source(i, u)
                sp.dma_start(down(u), d.rearrange("(f p) n -> p f n", p=P)).then_inc(landed_out[u], 16)

            def refill(i, u):
                for f in range(FT):
                    sp.wait_ge(filled[u * FT + f], i)
                if weigh:
                    for f in range(FT):
                        sp.wait_ge(hid[u * FT + f], i)
                fetch_in(i, u)
                sp.wait_ge(read_out[u], i)
                fetch_out(i, u)

            for u in range(U):
                fetch_in(0, u)
                fetch_out(0, u)
            with sp.Fori(1, whole) as i:
                for u in range(U):
                    refill(i, u)
            for u in range(rest):
                refill(whole, u)

        @block.tensor
        def _(pe):
            for t in range(NT):
                for n in range(2):
                    pe.matmul(ps[:, 4 + 2 * t + n, :], seed, k.X[:, t, n * BANK:(n + 1) * BANK],
                              start=True, stop=False, skip_group_check=True)

            def body(i, u, first=False):
                pe.wait_ge(landed_in[u], (i + 1) * N_IN)
                for f in range(FT):
                    b = u * FT + f
                    if not first:
                        pe.wait_ge(hid[b], i)
                    for o, w in ((0, gate(u)), (T, up(u))):
                        for kt in range(8):
                            last = pe.matmul(ps[:, b, o:o + T], w[:, kt, f * P:(f + 1) * P], k.hT[:, kt, :],
                                             start=kt == 0, stop=kt == 7)
                    last.then_inc(filled[b], 1)
                pe.wait_ge(landed_out[u], (i + 1) * 16)
                for f in range(FT):
                    b = u * FT + f
                    pe.wait_ge(hid[b], i + 1)
                    for t in range(NT):
                        for n in range(2):
                            last = pe.matmul(ps[:, 4 + 2 * t + n, :], hidden[:, b, t * P:(t + 1) * P],
                                             down(u)[:, f, n * BANK:(n + 1) * BANK],
                                             start=False, stop=False, skip_group_check=True)
                last.then_inc(read_out[u], 1)

            for u in range(U):
                body(0, u, first=True)
            with pe.Fori(1, whole) as i:
                for u in range(U):
                    body(i, u)
            for u in range(rest):
                body(whole, u)
            for t in range(NT):
                for n in range(2):
                    last = pe.matmul(ps[:, 4 + 2 * t + n, :], k.zero[:], k.X[:, t, n * BANK:(n + 1) * BANK],
                                     start=False, stop=True, skip_group_check=True)
            last.then_inc(summed, 1)

        @block.scalar
        def _(act):
            def body(i, u, first=False):
                for f in range(FT):
                    b = u * FT + f
                    act.wait_ge(filled[b], i + 1)
                    act.activation(act_out[:, b, :], ps[:, b, 0:T], ACT.Silu).then_inc(silued[b], 1)
            for u in range(U):
                body(0, u, first=True)
            with act.Fori(1, whole) as i:
                for u in range(U):
                    body(i, u)
            for u in range(rest):
                body(whole, u)

        @block.vector
        def _(dve):
            def body(i, u, first=False):
                for f in range(FT):
                    b = u * FT + f
                    dve.wait_ge(silued[b], i + 1)
                    if not first:
                        dve.wait_ge(read_out[u], i)
                    if weigh:
                        dve.wait_ge(landed_in[u], (i + 1) * N_IN)
                        dve.tensor_tensor(act_out[:, b, :], act_out[:, b, :], factor[:, u, :], ALU.mult
                                          ).then_inc(weighed, 1)
                        dve.wait_ge(weighed, i * (U * FT) + (b + 1))
                    dve.tensor_tensor(hidden[:, b, :], act_out[:, b, :], ps[:, b, T:2 * T], ALU.mult
                                      ).then_inc(hid[b], 1)
            for u in range(U):
                body(0, u, first=True)
            with dve.Fori(1, whole) as i:
                for u in range(U):
                    body(i, u)
            for u in range(rest):
                body(whole, u)
            dve.wait_ge(summed, 1)
            for t in range(NT):
                finish(dve, ps[:, 4 + 2 * t:6 + 2 * t, :].rearrange("p b n -> p (b n)"), t)


def route(k, A, table):
    nc, T, NT, ps = k.nc, k.T, k.NT, k.ps
    NG, NE = 4, 8
    with ExitStack() as own:
        sb = lambda name, shape: own.enter_context(nc.sbuf_tensor("rt_" + name, shape, F32))
        lg, le = sb("lg", [P, NT, NG]), sb("le", [P, NT, NG * NE])
        bg, be = sb("bg", [P, NG]), sb("be", [P, NG * NE])
        mg, zg, d2, w1, w2 = (sb(n, [P, NT]) for n in ("mg", "zg", "d2", "w1", "w2"))
        m1, m2 = sb("m1", [P, NT]), sb("m2", [P, NT])
        pick, cum = sb("pick", [P, NT, NG]), sb("cum", [P, NT, NE])
        ex = sb("ex", [P, NT, NG])
        mine, one, two = (sb(n, [P, NT, NE]) for n in ("mine", "one", "two"))
        G, GT = sb("G", [P, NT, NG, NE]), sb("GT", [NG * NE, T])
        load(k, "rt_load", [(bg[:], rows(A["b_router_group"][0])), (be[:], rows(A["b_router_expert"][0]))])
        gemm(k, "rt_g", k.hT, 8, A["w_router_group"][0], NG, tokens_to(k, lg))
        gemm(k, "rt_e", k.hT, 8, A["w_router_expert"][0], NG * NE, tokens_to(k, le))

        def first(dve, after, x, best, mask, n):
            for t in range(NT):
                after(dve.tensor_scalar(mask[:, t, :], x[:, t, :], best[:, t:t + 1], None, ALU.is_equal))
                after(dve.tensor_tensor_scan(cum[:, t, :n], k.ones[:, :n], mask[:, t, :], 0.0, ALU.mult, ALU.add))
                after(dve.scalar_tensor_tensor(mask[:, t, :], cum[:, t, :n], 1.0, mask[:, t, :],
                                               ALU.is_equal, ALU.mult))

        def choose(dve, after):
            after(dve.tensor_tensor(lg[:], lg[:], bg[:].unsqueeze(1).to_broadcast([P, NT, NG]), ALU.add))
            after(dve.tensor_tensor(le[:], le[:], be[:].unsqueeze(1).to_broadcast([P, NT, NG * NE]), ALU.add))
            after(dve.tensor_reduce(mg[:], lg[:], AX.X, ALU.max))
            first(dve, after, lg, mg, pick, NG)
            after(dve.tensor_tensor(ex[:], lg[:], mg[:].unsqueeze(2).to_broadcast([P, NT, NG]), ALU.subtract))
            for t in range(NT):
                for g in range(NG):
                    lt, pt = le[:, t, g * NE:(g + 1) * NE], pick[:, t, g:g + 1]
                    if g == 0:
                        after(dve.tensor_scalar(mine[:, t, :], lt, pt, None, ALU.mult))
                    else:
                        after(dve.scalar_tensor_tensor(mine[:, t, :], lt, pt, mine[:, t, :], ALU.mult, ALU.add))
            after(dve.tensor_reduce(m1[:], mine[:], AX.X, ALU.max))
            first(dve, after, mine, m1, one, NE)
            after(dve.scalar_tensor_tensor(mine[:], one[:], NEG, mine[:], ALU.mult, ALU.add))
            after(dve.tensor_reduce(m2[:], mine[:], AX.X, ALU.max))
            first(dve, after, mine, m2, two, NE)
            after(dve.tensor_tensor(d2[:], m2[:], m1[:], ALU.subtract))
        on_vector(k, "rt_choose", choose)

        def exps(act, after):
            act.activation(ex[:], ex[:], ACT.Exp)
            act.activation(d2[:], d2[:], ACT.Exp)
        on_scalar(k, "rt_exp", exps)

        def weights(dve, after):
            after(dve.tensor_reduce(zg[:], ex[:], AX.X, ALU.add))
            after(dve.scalar_tensor_tensor(w1[:], d2[:], 1.0, zg[:], ALU.add, ALU.mult))
            after(dve.reciprocal(w1[:], w1[:]))
            after(dve.tensor_tensor(w2[:], w1[:], d2[:], ALU.mult))
            by = lambda x: x[:].unsqueeze(2).to_broadcast([P, NT, NE])
            after(dve.tensor_tensor(one[:], one[:], by(w1), ALU.mult))
            after(dve.tensor_tensor(two[:], two[:], by(w2), ALU.mult))
            after(dve.tensor_tensor(one[:], one[:], two[:], ALU.add))
            for t in range(NT):
                for g in range(NG):
                    dve.tensor_scalar(G[:, t, g, :], one[:, t, :], pick[:, t, g:g + 1], None, ALU.mult)
        on_vector(k, "rt_weights", weights)
        on_tensor(k, "rt_turn", lambda pe: [pe.transpose(
            ps[:NG * NE, 0, t * P:(t + 1) * P], G[:, t].rearrange("p g e -> p (g e)"), k.ident[:])
            for t in range(NT)])
        on_vector(k, "rt_copy", lambda dve, after: dve.tensor_copy(GT[:], ps[:NG * NE, 0, :T]))
        dump(k, "rt_store", [(table, GT[:])])


def first_block(k, A, masks, scratch, table):
    nc, NT, T = k.nc, k.NT, k.T
    with ExitStack() as own:
        sb = lambda name, shape: own.enter_context(nc.sbuf_tensor("fb_" + name, shape, F32))
        gain = sb("gain", [P, 2, 8])
        load(k, "fb_load", [(k.X[:], A["x"][0].rearrange("(t p) n -> p t n", p=P)),
                            (gain[:, 0, :], column(A["norm_mix"][0])), (gain[:, 1, :], column(A["norm_ffn"][0]))])
        y = sb("y", [P, NT, 512])
        yT = [sb(f"yT{r}", [P, 4, T]) for r in range(3)]
        with nc.sbuf_tensor("fb_h", [P, NT, 1024], F32) as h:
            rms_rows(k, "fb_rms", k.X[:], h[:])
            transpose_in(k, "fb_hT", h, k.hT, scale=gain[:, 0, :])
        short_conv(k, A, yT[0])
        sparse_attention(k, A, scratch, y, None)
        transpose_in(k, "fb_yn", y, yT[1], 4)
        gated_delta(k, A, masks, y)
        transpose_in(k, "fb_yg", y, yT[2], 4)
        merge_branches(k, A, yT)
        with nc.sbuf_tensor("fb_h2", [P, NT, 1024], F32) as h:
            rms_rows(k, "fb_rms2", k.X[:], h[:])
            transpose_in(k, "fb_h2T", h, k.hT, scale=gain[:, 1, :])
        route(k, A, table)
        wg, wu, wd = (A[f"w_expert_{n}"][0] for n in ("gate", "up", "down"))

        def source(e, u):
            one = bass.ds(e, 1)
            flat = lambda x: x.rearrange("a k n -> (a k) n")
            return (flat(wg[one, :, u * 256:(u + 1) * 256]), flat(wu[one, :, u * 256:(u + 1) * 256]),
                    flat(wd[one, u * 256:(u + 1) * 256, :]), table[one, :].rearrange("a t -> (a t)"))
        swiglu(k, "moe", 64, source, k.ident[:],
               lambda dve, psum, t: dve.tensor_copy(k.X[:, t, :], psum), weigh=True)


ALPHA = 8 ** 0.25
ROPE_THETA = 500000.0


def modulation(k, name, w, bias):
    nc, ps = k.nc, k.ps
    R, N = 3, 6
    with Stage(nc, name) as st:
        landed = [st.sem(f"landed{i}") for i in range(R)]
        biased, filled, drained, step = st.sem("biased"), st.sem("filled"), st.sem("drained"), st.sem("step")
        block = st.block()
        slot = lambda c: k.wring[:, c % R, :].rearrange("p (k n) -> p k n", k=8)

        @block.sync
        def _(sp):
            sp.dma_start(k.mod[:], rows(bias)).then_inc(biased, 16)
            for c in range(N):
                if c >= R:
                    sp.wait_ge(filled, c - R + 1)
                sp.dma_start(slot(c), w[:, c * BANK:(c + 1) * BANK].rearrange("(k p) n -> p k n", p=P)
                             ).then_inc(landed[c % R], 16)

        @block.tensor
        def _(pe):
            for c in range(N):
                pe.wait_ge(landed[c % R], 16 * (c // R + 1))
                if c >= 2:
                    pe.wait_ge(drained, c - 1)
                for kt in range(8):
                    last = pe.matmul(ps[:, c % 2, :], k.cond[:, kt, :], slot(c)[:, kt, :],
                                     start=kt == 0, stop=kt == 7)
                last.then_inc(filled, 1)

        @block.vector
        def _(dve):
            dve.wait_ge(biased, 16)
            for c in range(N):
                dve.wait_ge(filled, c + 1)
                m = k.mod[:, c * BANK:(c + 1) * BANK]
                dve.scalar_tensor_tensor(m, ps[:, c % 2, :], 0.0 if c < 2 else 1.0, m, ALU.add, ALU.add
                                         ).then_inc(drained, 1)


def modulate(k, name, h):
    shape = [P, k.NT, 1024]
    row = lambda i: k.mod[:, i * 1024:(i + 1) * 1024].unsqueeze(1).to_broadcast(shape)

    def body(dve, after):
        after(dve.tensor_tensor(h[:], k.X[:], row(1), ALU.mult))
        dve.tensor_tensor(h[:], h[:], row(0), ALU.add)
    on_vector(k, name + "_mod", body)
    transpose_in(k, name + "_hT", h, k.hT)


def residual_norm(k, name, y, g, b):
    nc, NT, X = k.nc, k.NT, k.X
    shape = [P, NT, 1024]
    with Stage(nc, name) as st:
        gr, br = st.sb("g", [P, 1024]), st.sb("b", [P, 1024])
        mean, var = st.sb("mean", [P, NT]), st.sb("var", [P, NT])
        landed, step, summed, rooted = st.sem("landed"), st.sem("step"), st.sem("summed"), st.sem("rooted")
        block = st.block()
        row = lambda r: r.unsqueeze(1).to_broadcast(shape)

        @block.sync
        def _(sp):
            sp.dma_start(gr[:], rows(g)).then_inc(landed, 16)
            sp.dma_start(br[:], rows(b)).then_inc(landed, 16)

        @block.vector
        def _(dve):
            after = Chain(dve, step)
            after(dve.tensor_tensor(y[:], y[:], row(k.mod[:, 2048:3072]), ALU.mult))
            after(dve.scalar_tensor_tensor(X[:], X[:], ALPHA, y[:], ALU.mult, ALU.add))
            after(dve.tensor_reduce(mean[:], X[:], AX.X, ALU.add))
            after(dve.tensor_scalar(mean[:], mean[:], 1.0 / 1024, None, ALU.mult))
            for t in range(NT):
                op = dve.tensor_scalar(X[:, t], X[:, t], mean[:, t:t + 1], None, ALU.subtract)
            after(op)
            after(dve.tensor_tensor(y[:], X[:], X[:], ALU.mult))
            after(dve.tensor_reduce(var[:], y[:], AX.X, ALU.add))
            dve.tensor_scalar(var[:], var[:], 1.0 / 1024, 1e-5, ALU.mult, ALU.add).then_inc(summed, 1)
            dve.wait_ge(landed, 32)
            dve.wait_ge(rooted, 1)
            for t in range(NT):
                op = dve.scalar_tensor_tensor(X[:, t], X[:, t], var[:, t:t + 1], gr[:], ALU.mult, ALU.mult)
            after(op)
            dve.tensor_tensor(X[:], X[:], row(br[:]), ALU.add)

        @block.gpsimd
        def _(pool):
            pool.wait_ge(summed, 1)
            pool.tensor_tensor(var[:], var[:], k.nhalf[:, :NT], ALU.pow).then_inc(rooted, 1)


def mlstm(k, A, y):
    nc, T, NT, ps = k.nc, k.T, k.NT, k.ps
    H, DK, DV = 4, 128, 256
    with ExitStack() as own:
        sb = lambda name, shape: own.enter_context(nc.sbuf_tensor("ml_" + name, shape, F32))
        qkT, VO = sb("qkT", [P, 8, T]), sb("VO", [P, NT, 2056])
        bg, norm = sb("bg", [P, 8]), sb("norm", [P, 1024])
        load(k, "ml_load", [(bg[:], rows(A["mlstm_b_gate_2"][0])), (norm[:], rows(A["mlstm_norm_2"][0]))])
        w = A["mlstm_w_in_2"][0]
        gemm(k, "ml_qk", k.hT, 8, w[:, 0:1024], 1024, features_to(k, qkT), feature_major=True)
        gemm(k, "ml_vo", k.hT, 8, w[:, 1024:3080], 2056, tokens_to(k, VO))
        gt, ab, nf = sb("gt", [P, NT, 8]), sb("ab", [P, NT, H]), sb("nf", [P, NT, H])
        rep = sb("rep", [P, NT, 2, H, P])

        def pre(dve, after):
            after(dve.tensor_tensor(gt[:], VO[:, :, 2048:2056], bg[:].unsqueeze(1).to_broadcast([P, NT, 8]), ALU.add))
            after(dve.tensor_scalar(ab[:], gt[:, :, 4:8], -1.0, None, ALU.mult))
            after(dve.tensor_tensor(ab[:], ab[:], gt[:, :, 4:8], ALU.min))
        on_vector(k, "ml_p1", pre)

        def soft(act, after):
            after(act.activation(ab[:], ab[:], ACT.Exp))
            after(act.activation(ab[:], ab[:], ACT.Ln, bias=1.0))
            act.activation(VO[:, :, 1024:2048], VO[:, :, 1024:2048], ACT.Sigmoid)
        on_scalar(k, "ml_p2", soft)

        def repeat(dve, after):
            after(dve.tensor_scalar(nf[:], gt[:, :, 4:8], 0.0, None, ALU.min))
            after(dve.tensor_tensor(nf[:], ab[:], nf[:], ALU.subtract))
            dve.tensor_copy(rep[:, :, 0], gt[:, :, 0:4].unsqueeze(3).to_broadcast([P, NT, H, P]))
            dve.tensor_copy(rep[:, :, 1], nf[:].unsqueeze(3).to_broadcast([P, NT, H, P]))
        on_vector(k, "ml_p3", repeat)

        def rows_of_R(pe):
            for h in range(H):
                for t in range(NT):
                    out = ps[:, h // 2, (h % 2) * T + t * P:(h % 2) * T + (t + 1) * P]
                    pe.matmul(out, rep[:, t, 0, h], k.ident[:], start=True, stop=False)
                    for r in range(t):
                        pe.matmul(out, rep[:, r, 1, h], k.ones[:], start=False, stop=False)
                    pe.matmul(out, rep[:, t, 1, h], k.upto[:], start=False, stop=True)
            for t in range(NT):
                for r in range(t + 1):
                    pe.matmul(ps[:, 2, t * H:(t + 1) * H], k.upto[:] if r == t else k.ones[:], nf[:, r, :],
                              start=r == 0, stop=r == t)
        on_tensor(k, "ml_R", rows_of_R)
        W, c, em = sb("W", [P, NT, H, T]), sb("c", [P, NT, H]), sb("em", [P, NT, H])

        def weights(dve, after):
            for t in range(NT):
                after(dve.tensor_tensor(W[:, t], ps[:, 0:2, :].rearrange("p b (h s) -> p (b h) s", s=T),
                                        k.causal[:, t, :].unsqueeze(1).to_broadcast([P, H, T]), ALU.add))
            after(dve.tensor_reduce(c[:], W[:], AX.X, ALU.max))
            after(dve.tensor_scalar(c[:], c[:], 0.0, None, ALU.max))
            dve.tensor_tensor(W[:], W[:], c[:].unsqueeze(3).to_broadcast([P, NT, H, T]), ALU.subtract)
            dve.tensor_tensor(em[:], ps[:, 2, :NT * H].rearrange("p (t h) -> p t h", t=NT), c[:], ALU.subtract)
        on_vector(k, "ml_W", weights)
        on_scalar(k, "ml_E", lambda act, after: [act.activation(W[:], W[:], ACT.Exp),
                                                 act.activation(em[:], em[:], ACT.Exp)])
        den, PT = sb("den", [P, NT, H]), sb("PT", [P, H, T])
        for t in range(NT):
            n = (t + 1) * P
            on_tensor(k, f"ml_s{t}", lambda pe, t=t, n=n: [pe.matmul(
                ps[:, h // 2, (h % 2) * T:(h % 2) * T + n], qkT[:, h, t * P:(t + 1) * P], qkT[:, 4 + h, :n],
                start=True, stop=True) for h in range(H)])

            def weigh(dve, after, t=t, n=n):
                s = W[:, t, :, :n]
                after(dve.scalar_tensor_tensor(s, ps[:, 0:2, :].rearrange("p b (h s) -> p (b h) s", s=T)[:, :, :n],
                                               DK ** -0.5, s, ALU.mult, ALU.mult))
                after(dve.tensor_reduce(den[:, t], s, AX.X, ALU.add))
                after(dve.tensor_scalar(c[:, t], den[:, t], -1.0, None, ALU.mult))
                after(dve.tensor_tensor(den[:, t], den[:, t], c[:, t], ALU.max))
                after(dve.tensor_tensor(den[:, t], den[:, t], em[:, t], ALU.max))
                after(dve.reciprocal(den[:, t], den[:, t]))
            on_vector(k, f"ml_w{t}", weigh)
            on_tensor(k, f"ml_t{t}", lambda pe, t=t: [pe.transpose(
                ps[:, h // 2, (h % 2) * T + r * P:(h % 2) * T + (r + 1) * P], W[:, t, h, r * P:(r + 1) * P],
                k.ident[:]) for h in range(H) for r in range(t + 1)])
            on_vector(k, f"ml_c{t}", lambda dve, after, n=n: dve.tensor_copy(
                PT[:, :, :n], ps[:, 0:2, :].rearrange("p b (h s) -> p (b h) s", s=T)[:, :, :n]))

            def apply(pe, t=t):
                for h in range(H):
                    for r in range(t + 1):
                        pe.matmul(ps[:, 2 + h // 2, (h % 2) * DV:(h % 2 + 1) * DV], PT[:, h, r * P:(r + 1) * P],
                                  VO[:, r, h * DV:(h + 1) * DV], start=r == 0, stop=r == t)
            on_tensor(k, f"ml_a{t}", apply)
            on_vector(k, f"ml_o{t}", lambda dve, after, t=t: dve.tensor_tensor(
                y[:, t].rearrange("p (h d) -> p h d", h=H), ps[:, 2:4, :].rearrange("p b (h d) -> p (b h) d", d=DV),
                den[:, t].unsqueeze(2).to_broadcast([P, H, DV]), ALU.mult))
        rms_rows(k, "ml_n", y[:], y[:], groups=H)

        def gated(dve, after):
            after(dve.tensor_tensor(y[:], y[:], norm[:].unsqueeze(1).to_broadcast([P, NT, 1024]), ALU.mult))
            dve.tensor_tensor(y[:], y[:], VO[:, :, 1024:2048], ALU.mult)
        on_vector(k, "ml_y", gated)


def rope_tables(k, positions, cos, sin):
    nc, NT, half = k.nc, k.NT, 8
    with ExitStack() as own:
        sb = lambda name, shape, dt=F32: own.enter_context(nc.sbuf_tensor("rp_" + name, shape, dt))
        pi, pf = sb("pi", [P, NT], I32), sb("pf", [P, NT])
        ang, turns, whole = sb("ang", [P, NT, half]), sb("turns", [P, NT, half]), sb("whole", [P, NT, half], I32)
        load(k, "rp_load", [(pi[:], positions.rearrange("(t p) -> p t", p=P))])
        c1 = 6.28125
        c2 = float(np.float32(np.round((2 * math.pi - c1) * 2 ** 20) / 2 ** 20))
        c3 = 2 * math.pi - c1 - c2

        def body(dve, after):
            after(dve.tensor_copy(pf[:], pi[:]))
            for i in range(half):
                inv = float(np.float32(ROPE_THETA ** (-i * 2.0 / 16)))
                op = dve.tensor_scalar(ang[:, :, i], pf[:], inv, None, ALU.mult)
            after(op)
            for dst, quarter in ((cos, 0.25), (sin, 0.0)):
                after(dve.tensor_scalar(turns[:], ang[:], 1 / (2 * math.pi), quarter, ALU.mult, ALU.add))
                after(dve.tensor_copy(whole[:], turns[:]))
                after(dve.tensor_copy(turns[:], whole[:]))
                after(dve.scalar_tensor_tensor(dst[:], turns[:], -c1, ang[:], ALU.mult, ALU.add))
                after(dve.scalar_tensor_tensor(dst[:], turns[:], -c2, dst[:], ALU.mult, ALU.add))
                after(dve.scalar_tensor_tensor(dst[:], turns[:], -c3, dst[:], ALU.mult, ALU.add))
                after(dve.tensor_scalar(dst[:], dst[:], quarter * 2 * math.pi, math.pi, ALU.add, ALU.min))
                after(dve.tensor_scalar(dst[:], dst[:], -math.pi, None, ALU.max))
        on_vector(k, "rp_ang", body)
        on_scalar(k, "rp_sin", lambda act, after: [act.activation(cos[:], cos[:], ACT.Sin),
                                                   act.activation(sin[:], sin[:], ACT.Sin)])


def rotate(k, name, x, heads, cos, sin, tmp):
    shape = [P, k.NT, heads, 8]
    v = x.rearrange("p t (h d) -> p t h d", h=heads)
    x1, x2 = v[:, :, :, 0:8], v[:, :, :, 8:16]
    c, s = (z[:].unsqueeze(2).to_broadcast(shape) for z in (cos, sin))

    def body(dve, after):
        dve.tensor_tensor(tmp[:, 0], x1, c, ALU.mult)
        dve.tensor_tensor(tmp[:, 1], x2, s, ALU.mult)
        dve.tensor_tensor(tmp[:, 2], x2, c, ALU.mult)
        after(dve.tensor_tensor(tmp[:, 3], x1, s, ALU.mult))
        dve.tensor_tensor(x1, tmp[:, 0], tmp[:, 1], ALU.subtract)
        dve.tensor_tensor(x2, tmp[:, 2], tmp[:, 3], ALU.add)
    on_vector(k, name, body)


def windowed(k, A, cos, sin, y):
    nc, T, NT = k.nc, k.T, k.NT
    H, G, D = 16, 2, 64
    with ExitStack() as own:
        sb = lambda name, shape: own.enter_context(nc.sbuf_tensor("wa_" + name, shape, F32))
        U, KD = sb("U", [P, NT, 1280]), sb("KD", [P, NT, G, 2, D])
        qT, kT = sb("qT", [P, 8, T]), sb("kT", [P, G, T])
        band, sinks, tmp = sb("band", [P, NT, T]), sb("sinks", [P, H]), sb("tmp", [P, 4, NT, 18, 8])
        load(k, "wa_load", [(sinks[:], rows(A["swa_sinks_2"][0]))])
        gemm(k, "wa_in", k.hT, 8, A["swa_w_in_2"][0], 1280, tokens_to(k, U))
        rotate(k, "wa_rope", U[:, :, 0:1152], 18, cos, sin, tmp)

        def mask(pool, after):
            for t in range(NT):
                pool.affine_select(out=band[:, t, :], in_=k.causal[:, t, :], compare_op=ALU.is_gt, fill=NEG,
                                   base=P - t * P, pattern=[[1, T]], channel_multiplier=-1)
        on_gpsimd(k, "wa_mask", mask)
        on_vector(k, "wa_twice", lambda dve, after: [dve.tensor_copy(
            KD[:, :, :, u, :], U[:, :, 1024:1152].rearrange("p t (g d) -> p t g d", g=G)) for u in range(2)])
        transpose_in(k, "wa_qT", U, qT, 8, factor=D ** -0.5)
        transpose_in(k, "wa_kT", None, kT, G, src_cols=lambda t, i: KD[:, t, i].rearrange("p u d -> p (u d)"))
        half = lambda h: slice((h % 2) * D, (h % 2 + 1) * D)
        attention(k, "wa_a", [(list(range(h, h + 4)), t) for t in range(NT) for h in range(0, H, 4)],
                  q_of=lambda h, t: qT[half(h), h // 2, t * P:(t + 1) * P],
                  k_of=lambda h, kt: kT[half(h), h // 8, kt * P:(kt + 1) * P],
                  v_of=lambda h, kt: U[:, kt, 1152 + (h // 8) * D:1152 + (h // 8 + 1) * D],
                  bias_of=lambda hs, t: band[:, t, :(t + 1) * P].unsqueeze(1).to_broadcast([P, 4, (t + 1) * P]),
                  out_of=lambda hs, t: y[:, t, hs[0] * D:(hs[-1] + 1) * D].rearrange("p (g d) -> p g d", d=D),
                  dv=D, sink_of=lambda hs: sinks[:, hs[0]:hs[-1] + 1])


def hgrn(k, A, masks, layer, y):
    nc, T, NT, ps = k.nc, k.T, k.NT, k.ps
    H, D = 8, 128
    LV = 8
    with ExitStack() as own:
        sb = lambda name, shape: own.enter_context(nc.sbuf_tensor("hg_" + name, shape, F32))
        QF, IG = sb("QF", [P, 16, T]), sb("IG", [P, NT, 2048])
        lo, norm = sb("lo", [P, 4, 8]), sb("norm", [P, 1024])
        lb, lc, mx = sb("lb", [P, 8]), sb("lc", [P, 8]), sb("mx", [P, 8])
        K, cf = sb("K", [P, H, T]), sb("cf", [P, H, T])
        E = sb("E", [P, 2, H, T])
        QE, KE = sb("QE", [P, H, T]), sb("KE", [P, H, T])
        aT, aX = sb("aT", [P, NT, H, P]), sb("aX", [P, H, P])
        load(k, "hg_load", [(lo[:, i, :], column(A["hgrn_lower_bounds_2"][i])) for i in range(4)]
             + [(norm[:], rows(A["hgrn_norm_2"][0]))])
        w = A["hgrn_w_in_2"][0]
        gemm(k, "hg_qf", k.hT, 8, w[:, 0:2048], 2048, features_to(k, QF), feature_major=True)
        gemm(k, "hg_ig", k.hT, 8, w[:, 2048:4096], 2048, tokens_to(k, IG))
        on_vector(k, "hg_l1", lambda dve, after: [
            after(dve.tensor_reduce(mx[:], lo[:].rearrange("p l i -> p i l"), AX.X, ALU.max)),
            after(dve.tensor_tensor(lo[:], lo[:], mx[:].unsqueeze(1).to_broadcast([P, 4, 8]), ALU.subtract))])
        on_scalar(k, "hg_l2", lambda act, after: [
            act.activation(lo[:], lo[:], ACT.Exp),
            act.activation(K[:], QF[:, 8:16, :], ACT.Exp, scale=-1.0)])
        Q = QF[:, 0:8, :]
        wide_ = lambda x: x[:].unsqueeze(2).to_broadcast([P, H, T])
        F = QF[:, 8:16, :]

        def gates(dve, after):
            after(dve.tensor_reduce(mx[:], lo[:].rearrange("p l i -> p i l"), AX.X, ALU.add))
            after(dve.reciprocal(mx[:], mx[:]))
            after(dve.tensor_reduce(lb[:], lo[:, 1:layer + 1].rearrange("p l i -> p i l"), AX.X, ALU.add))
            after(dve.tensor_tensor(lb[:], lb[:], mx[:], ALU.mult))
            after(dve.tensor_scalar(lc[:], lb[:], -1.0, 1.0, ALU.mult, ALU.add))
            after(dve.tensor_scalar(K[:], K[:], 1e30, None, ALU.min))
            after(dve.tensor_scalar(F, K[:], 1.0, None, ALU.add))
            after(dve.reciprocal(F, F))
            after(dve.tensor_tensor(F, F, wide_(lc), ALU.mult))
            after(dve.tensor_tensor(K[:], K[:], F, ALU.mult))
            after(dve.tensor_tensor(F, F, wide_(lb), ALU.add))
            after(dve.memset(aT[:], 0.0))
        on_vector(k, "hg_g", gates)
        on_scalar(k, "hg_ln", lambda act, after: act.activation(F, F, ACT.Ln))

        def running(dve, after):
            for h in range(H):
                dve.tensor_tensor_scan(cf[:, h, :], k.onesT[:], F[:, h, :], 0.0, ALU.mult, ALU.add)
        on_vector(k, "hg_cf", running)

        with Stage(nc, "hg_lv") as st:
            step, ready = st.sem("step"), st.sem("ready")
            spread, raised = st.sem("spread"), st.sem("raised")
            scaled, multiplied, taken = st.sem("scaled"), st.sem("multiplied"), st.sem("taken")
            block = st.block()

            def cut(x, v):
                b = 2 ** v
                z = x.rearrange("p h (n u j) -> p h n u j", u=2, j=b)
                return z[:, :, :, 0, :], z[:, :, :, 1, :]

            @block.vector
            def _(dve):
                def exponents(v):
                    b, n = 2 ** v, T // 2 ** (v + 1)
                    c0, c1 = cut(cf[:], v)
                    e0, e1 = cut(E[:, v % 2], v)
                    mid = c0[:, :, :, b - 1:b]
                    if n == 1:
                        c0, c1, e0, e1, mid = (z[:, :, 0, :] for z in (c0, c1, e0, e1, mid))
                        mid = mid.to_broadcast([P, H, b])
                    else:
                        mid = mid.to_broadcast([P, H, n, b])
                    dve.tensor_tensor(e0, mid, c0, ALU.subtract)
                    dve.tensor_tensor(e1, c1, mid, ALU.subtract).then_inc(spread, 1)

                exponents(0)
                for v in range(LV + 1):
                    if v + 1 < LV:
                        if v >= 1:
                            dve.wait_ge(scaled, v)
                        exponents(v + 1)
                    if v >= 1:
                        dve.wait_ge(multiplied, v)
                    if v < LV:
                        dve.wait_ge(raised, v + 1)
                        dve.tensor_tensor(QE[:], Q, E[:, v % 2], ALU.mult)
                        dve.tensor_tensor(KE[:], K[:], E[:, v % 2], ALU.mult).then_inc(scaled, 1)
                        dve.wait_ge(multiplied, v + 1)
                        if v < LV - 1:
                            dve.copy_predicated(
                                aT[:].rearrange("p t h c -> p (t h) c"),
                                masks[:, v, :].bitcast(mybir.dt.uint32).unsqueeze(1).to_broadcast([P, NT * H, P]),
                                ps[:, 0:4, :].rearrange("p b (h c) -> p (b h) c", c=P)).then_inc(taken, 1)
                        else:
                            dve.tensor_copy(aX[:].rearrange("p h c -> p (h c)"),
                                            ps[:, 0:2, :].rearrange("p b n -> p (b n)")).then_inc(taken, 1)
                        dve.wait_ge(taken, v + 1)
                    else:
                        dve.copy_predicated(
                            aT[:].rearrange("p t h c -> p (t h) c"),
                            k.ident[:].bitcast(mybir.dt.uint32).unsqueeze(1).to_broadcast([P, NT * H, P]),
                            ps[:, 4:8, :].rearrange("p b (h c) -> p (b h) c", c=P))

            @block.scalar
            def _(act):
                for v in range(LV):
                    act.wait_ge(spread, v + 1)
                    act.activation(E[:, v % 2], E[:, v % 2], ACT.Exp).then_inc(raised, 1)

            @block.tensor
            def _(pe):
                for v in range(LV):
                    pe.wait_ge(scaled, v + 1)
                    if v >= 1:
                        pe.wait_ge(taken, v)
                    for h in range(H):
                        if v < LV - 1:
                            for t in range(NT):
                                i = t * H + h
                                last = pe.matmul(ps[:, i // 4, i % 4 * P:(i % 4 + 1) * P],
                                                 KE[:, h, t * P:(t + 1) * P], QE[:, h, t * P:(t + 1) * P],
                                                 start=True, stop=True)
                        else:
                            last = pe.matmul(ps[:, h // 4, h % 4 * P:(h % 4 + 1) * P], KE[:, h, 0:P], QE[:, h, P:T],
                                             start=True, stop=True)
                    if v == LV - 1:
                        for h in range(H):
                            for t in range(NT):
                                i = t * H + h
                                last = pe.matmul(ps[:, 4 + i // 4, i % 4 * P:(i % 4 + 1) * P],
                                                 K[:, h, t * P:(t + 1) * P], Q[:, h, t * P:(t + 1) * P],
                                                 start=True, stop=True)
                    last.then_inc(multiplied, 1)

        def apply(pe):
            for h in range(H):
                v = lambda t: IG[:, t, h * D:(h + 1) * D]
                o = lambda t: ps[:, 2 * t + h // 4, h % 4 * D:(h % 4 + 1) * D]
                pe.matmul(o(0), aT[:, 0, h], v(0), start=True, stop=True)
                pe.matmul(o(1), aX[:, h], v(0), start=True, stop=False)
                pe.matmul(o(1), aT[:, 1, h], v(1), start=False, stop=True)
        on_tensor(k, "hg_pv", apply)
        on_scalar(k, "hg_silu", lambda act, after: [
            act.activation(IG[:, :, 1024:2048], IG[:, :, 1024:2048], ACT.Silu)])
        on_vector(k, "hg_o", lambda dve, after: dve.tensor_copy(
            y[:].rearrange("p t n -> p (t n)"), ps[:, 0:4, :].rearrange("p b n -> p (b n)")))
        rms_rows(k, "hg_n", y[:], y[:], groups=H)

        def gated(dve, after):
            after(dve.tensor_tensor(y[:], y[:], norm[:].unsqueeze(1).to_broadcast([P, NT, 1024]), ALU.mult))
            dve.tensor_tensor(y[:], y[:], IG[:, :, 1024:2048], ALU.mult)
        on_vector(k, "hg_y", gated)


def differential(k, A, cos, sin, layer, y):
    nc, T, NT = k.nc, k.T, k.NT
    H, D = 8, 64
    lam_init = 0.8 - 0.6 * math.exp(-0.3 * layer)
    with ExitStack() as own:
        sb = lambda name, shape: own.enter_context(nc.sbuf_tensor("df_" + name, shape, F32))
        U, qT, kT = sb("U", [P, NT, 3072]), sb("qT", [P, 8, T]), sb("kT", [P, 8, T])
        tmp, lv, gain = sb("tmp", [P, 4, NT, 32, 8]), sb("lv", [P, 4, D]), sb("gain", [P, 2 * D])
        pr, lam = sb("pr", [P, 2, D]), sb("lam", [P, 2])
        load(k, "df_load", [(lv[:], A["diff_lambda_2"][0].partition_broadcast(P)),
                            (gain[:], rows(A["diff_norm_2"][0]))])
        gemm(k, "df_in", k.hT, 8, A["diff_w_in_2"][0], 3072, tokens_to(k, U))
        rotate(k, "df_rope", U[:, :, 0:2048], 32, cos, sin, tmp)

        def dots(dve, after):
            dve.tensor_tensor(pr[:, 0], lv[:, 0], lv[:, 1], ALU.mult)
            after(dve.tensor_tensor(pr[:, 1], lv[:, 2], lv[:, 3], ALU.mult))
            after(dve.tensor_reduce(lam[:], pr[:], AX.X, ALU.add))
        on_vector(k, "df_l1", dots)
        on_scalar(k, "df_l2", lambda act, after: act.activation(lam[:], lam[:], ACT.Exp))

        def lam_of(dve, after):
            after(dve.tensor_tensor(lam[:, 0:1], lam[:, 1:2], lam[:, 0:1], ALU.subtract))
            after(dve.tensor_scalar(lam[:, 0:1], lam[:, 0:1], -lam_init, None, ALU.add))
        on_vector(k, "df_l3", lam_of)
        transpose_in(k, "df_qT", U, qT, 8, factor=D ** -0.5)
        transpose_in(k, "df_kT", U[:, :, 1024:2048], kT, 8)
        half = lambda h: slice((h % 2) * D, (h % 2 + 1) * D)
        attention(k, "df_a", [(list(range(h, h + 4)), t) for t in range(NT) for h in range(0, 2 * H, 4)],
                  q_of=lambda h, t: qT[half(h), h // 2, t * P:(t + 1) * P],
                  k_of=lambda h, kt: kT[half(h), h // 2, kt * P:(kt + 1) * P],
                  v_of=lambda h, kt: U[:, kt, 2048 + (h // 2) * 2 * D:2048 + (h // 2 + 1) * 2 * D],
                  bias_of=lambda hs, t: k.causal[:, t, :(t + 1) * P].unsqueeze(1).to_broadcast([P, 4, (t + 1) * P]),
                  out_of=lambda hs, t: y[:, t, hs[0] * D:(hs[-1] + 1) * D].rearrange("p (g d) -> p g d", d=2 * D),
                  dv=2 * D, minus=lambda g: lam[:, 0:1])
        rms_rows(k, "df_n", y[:], y[:], gain[:], groups=H, factor=1.0 - lam_init)


def second_block(k, A, masks):
    nc, T, NT = k.nc, k.T, k.NT
    with ExitStack() as own:
        sb = lambda name, shape: own.enter_context(nc.sbuf_tensor("sb_" + name, shape, F32))
        k.cond, c = sb("cond", [P, 8, P]), sb("c", [P, 8])
        k.onesT = sb("onesT", [P, T])
        k.causal = sb("causal", [P, NT, T])
        cos, sin = sb("cos", [P, NT, 8]), sb("sin", [P, NT, 8])
        y = sb("y", [P, NT, 1024])
        load(k, "sb_load", [(c[:], column(A["c_2"][0]))])
        on_scalar(k, "sb_silu", lambda act, after: act.activation(c[:], c[:], ACT.Silu))
        on_vector(k, "sb_cond", lambda dve, after: [
            dve.tensor_copy(k.cond[:], c[:].unsqueeze(2).to_broadcast([P, 8, P])), dve.memset(k.onesT[:], 1.0)])

        def mask(pool, after):
            after(pool.memset(k.causal[:], 0.0))
            for t in range(NT):
                pool.affine_select(out=k.causal[:, t, :], in_=k.causal[:, t, :], compare_op=ALU.is_ge, fill=NEG,
                                   base=t * P, pattern=[[-1, T]], channel_multiplier=1)
        on_gpsimd(k, "sb_causal", mask)
        rope_tables(k, A["positions_2"][0], cos, sin)
        mixers = [lambda: mlstm(k, A, y), lambda: windowed(k, A, cos, sin, y),
                  lambda: hgrn(k, A, masks, 2, y), lambda: differential(k, A, cos, sin, 3, y)]
        outs = ["mlstm_w_out_2", "swa_w_out_2", "hgrn_w_out_2", "diff_w_out_2"]
        for i in range(4):
            modulation(k, f"l{i}_ada0", A["ada_w_2"][i, 0], A["ada_b_2"][i, 0])
            modulate(k, f"l{i}_m0", y)
            mixers[i]()
            transpose_in(k, f"l{i}_yT", y, k.hT)
            gemm(k, f"l{i}_out", k.hT, 8, A[outs[i]][0], 1024, tokens_to(k, y))
            residual_norm(k, f"l{i}_n0", y, A["ln_g_2"][i, 0], A["ln_b_2"][i, 0])
            if k.stop == (i, 0):
                return
            modulation(k, f"l{i}_ada1", A["ada_w_2"][i, 1], A["ada_b_2"][i, 1])
            modulate(k, f"l{i}_m1", y)
            w, wd = A["ffn_w_in_2"][i], A["ffn_w_out_2"][i]
            HID = 2816

            def source(j, u, w=w, wd=wd):
                b = j * 2 + u
                return (w[:, bass.ds(b * 256, 256)], w[:, bass.ds(b * 256 + HID, 256)],
                        wd[bass.ds(b * 256, 256), :], None)
            swiglu(k, f"l{i}_ffn", HID // 256, source, k.zero[:],
                   lambda dve, psum, t: dve.tensor_copy(y[:, t, :], psum))
            residual_norm(k, f"l{i}_n1", y, A["ln_g_2"][i, 1], A["ln_b_2"][i, 1])
            if k.stop == (i, 1):
                return


def program(nc, A, out):
    T = A["x"].shape[1]
    scratch = nc.dram_tensor("compress_rows", [2, 2, T, 64], F32, kind="Internal").ap()
    table = nc.dram_tensor("expert_factors", [32, T], F32, kind="Internal").ap()
    with ExitStack() as ctx:
        k = persistent(nc, ctx, T)
        masks = ctx.enter_context(nc.sbuf_tensor("masks", [P, 7, P], F32))
        level_masks(k, masks)
        first_block(k, A, masks, scratch, table)
        second_block(k, A, masks)
        dump(k, "store", [(out[0].rearrange("(t p) n -> p t n", p=P), k.X[:])])


def kernel(**inputs):
    import numpy as _np
    import concourse.bacc as _bacc
    from concourse import mybir as _mybir
    from concourse.bass_utils import run_bass_kernel_spmd as _run

    nc = _bacc.Bacc("TRN2", target_bir_lowering=False, num_devices=1)
    arrays, aps = {}, {}
    for name, value in inputs.items():
        a = _np.ascontiguousarray(value)
        arrays[f"in_{name}_dram"] = a
        aps[name] = nc.dram_tensor(f"in_{name}_dram", a.shape, _mybir.dt.from_np(a.dtype), kind="ExternalInput").ap()
    shape = tuple(inputs["x"].shape)
    out = nc.dram_tensor("out_0_dram", shape, _mybir.dt.float32, kind="ExternalOutput").ap()
    program(nc, aps, out)
    r = _run(nc, [arrays], core_ids=[0])
    return r.results[0]["out_0_dram"]
```

```python
import math
from contextlib import ExitStack

import numpy as np

import concourse.bass as bass
from concourse import mybir

F32 = mybir.dt.float32
F32R = mybir.dt.float32r
I32 = mybir.dt.int32
ALU = mybir.AluOpType
ACT = mybir.ActivationFunctionType
AX = mybir.AxisListType
P = 128
BANK = 512
NEG = -1e30


class Kept:
    pass


class Chain:

    def __init__(self, eng, sem):
        self.eng, self.sem, self.n = eng, sem, 0

    def __call__(self, ins):
        self.n += 1
        ins.then_inc(self.sem, 1)
        self.eng.wait_ge(self.sem, self.n)


class Stage:

    def __init__(self, nc, name):
        self.nc, self.name, self.ctx, self.sems = nc, name, ExitStack(), []

    def __enter__(self):
        self.ctx.__enter__()
        return self

    def __exit__(self, *a):
        out = self.ctx.__exit__(*a)
        if a[0] is None and self.sems:
            for sem in self.sems:
                self.nc.gpsimd.sem_clear(sem)
                self.nc.release_semaphore(sem)
        return out

    def sem(self, name):
        self.sems.append(self.nc.alloc_semaphore(f"{self.name}_{name}"))
        return self.sems[-1]

    def sb(self, name, shape, dt=F32):
        return self.ctx.enter_context(self.nc.sbuf_tensor(f"{self.name}_{name}", shape, dt))

    def block(self):
        return self.ctx.enter_context(self.nc.Block())


def persistent(nc, ctx, T):
    k = Kept()
    k.nc, k.T, k.NT, k.stop = nc, T, T // P, None
    sb = lambda name, shape: ctx.enter_context(nc.sbuf_tensor(name, shape, F32))
    k.X = sb("X", [P, k.NT, 1024])
    k.hT = sb("hT", [P, 8, T])
    k.ident = sb("ident", [P, P])
    k.ones = sb("ones", [P, P])
    k.zero = sb("zero", [P, P])
    k.upto = sb("upto", [P, P])
    k.nhalf = sb("nhalf", [P, 64])
    k.wring = sb("wring", [P, 3, 4096])
    k.c = sb("c", [P, 8])
    k.ps = ctx.enter_context(nc.psum_tensor("ps", [P, 8, BANK], F32))
    with Stage(nc, "const") as st:
        filled = st.sem("filled")
        block = st.block()

        @block.gpsimd
        def _(pool):
            pool.memset(k.ident[:], 0.0).then_inc(filled, 1)
            pool.memset(k.ones[:], 1.0).then_inc(filled, 1)
            pool.memset(k.nhalf[:], -0.5)
            pool.memset(k.zero[:], 0.0)
            pool.wait_ge(filled, 2)
            pool.affine_select(out=k.ident[:], in_=k.ident[:], compare_op=ALU.not_equal, fill=1.0,
                               base=0, pattern=[[-1, P]], channel_multiplier=1)
            pool.affine_select(out=k.upto[:], in_=k.ones[:], compare_op=ALU.is_ge, fill=0.0,
                               base=0, pattern=[[1, P]], channel_multiplier=-1)
    return k


def load(k, name, pairs):
    nc = k.nc
    with Stage(nc, name) as st:
        landed = st.sem("landed")
        block = st.block()

        @block.sync
        def _(sp):
            with nc.allow_non_contiguous_dma("small vectors"):
                for dst, src in pairs:
                    sp.dma_start(dst, src).then_inc(landed, 16)
            sp.wait_ge(landed, 16 * len(pairs))


def rows(src, n=P):
    return src.partition_broadcast(n)


def gemm(k, name, xT, KT, w, N, finish, feature_major=False, bias=None):
    nc, T, ring, ps = k.nc, k.T, k.wring, k.ps
    chunks = [(n0, min(n0 + BANK, N)) for n0 in range(0, N, BANK)]
    R = 3
    with Stage(nc, name) as st:
        landed = [st.sem(f"landed{i}") for i in range(R)]
        filled = [st.sem(f"filled{j}") for j in range(2)]
        drained = [st.sem(f"drained{j}") for j in range(2)]
        block = st.block()

        def slot(c):
            n = chunks[c][1] - chunks[c][0]
            return ring[:, c % R, :KT * n].rearrange("p (k n) -> p k n", k=KT)

        def halves(c):
            n = chunks[c][1] - chunks[c][0]
            return [0, 1] if not feature_major or n > 2 * P else [0]

        @block.sync
        def _(sp):
            for c, (n0, n1) in enumerate(chunks):
                if c >= R:
                    sp.wait_ge(filled[1], c - R + 1)
                with nc.allow_non_contiguous_dma("narrow chunk"):
                    sp.dma_start(slot(c), w[:, n0:n1].rearrange("(k p) n -> p k n", p=P)
                                 ).then_inc(landed[c % R], 16)

        @block.tensor
        def _(pe):
            count = [0, 0]
            for c, (n0, n1) in enumerate(chunks):
                n = n1 - n0
                pe.wait_ge(landed[c % R], 16 * (c // R + 1))
                for j in halves(c):
                    if count[j] >= 2:
                        pe.wait_ge(drained[j], count[j] - 1)
                    bank = ps[:, 2 * j + count[j] % 2, :]
                    count[j] += 1
                    if feature_major:
                        for i in range(2 * j, min(2 * j + 2, -(-n // P))):
                            m = min(P, n - i * P)
                            for kt in range(KT):
                                last = pe.matmul(bank[:m, (i % 2) * T:(i % 2 + 1) * T],
                                                 slot(c)[:, kt, i * P:i * P + m], xT[:, kt, :],
                                                 start=kt == 0, stop=kt == KT - 1)
                    else:
                        for kt in range(KT):
                            last = pe.matmul(bank[:, :n], xT[:, kt, j * P:(j + 1) * P], slot(c)[:, kt, :],
                                             start=kt == 0, stop=kt == KT - 1 and bias is None)
                        if bias is not None:
                            last = pe.matmul(bank[:, :n], k.ones[0:1, :], bias[0:1, n0:n1],
                                             start=False, stop=True)
                    last.then_inc(filled[j], 1)

        def drain(eng, j):
            seen = 0
            for c, (n0, n1) in enumerate(chunks):
                if j not in halves(c):
                    continue
                eng.wait_ge(filled[j], seen + 1)
                last = finish(eng, ps[:, 2 * j + seen % 2, :], j, n0, n1)
                last.then_inc(drained[j], 1)
                seen += 1

        @block.scalar
        def _(act):
            drain(act, 0)

        @block.vector
        def _(dve):
            drain(dve, 1)


def transpose_in(k, name, src, dst, n_tiles=8, scale=None, src_cols=None,
                 factor=1.0):
    nc, T, ps = k.nc, k.T, k.ps
    cols = src_cols or (lambda t, i: src[:, t, i * P:(i + 1) * P])
    with Stage(nc, name) as st:
        turned, copied = st.sem("turned"), st.sem("copied")
        block = st.block()

        @block.tensor
        def _(pe):
            for i in range(n_tiles):
                if i >= 8:
                    pe.wait_ge(copied, i - 7)
                for t in range(k.NT):
                    last = pe.transpose(ps[:, i % 8, t * P:(t + 1) * P], cols(t, i), k.ident[:])
                last.then_inc(turned, 1)

        @block.scalar
        def _(act):
            for i in range(n_tiles):
                act.wait_ge(turned, i + 1)
                act.activation(dst[:, i, :], ps[:, i % 8, :T], ACT.Copy if scale is None else ACT.Identity,
                               scale=factor if scale is None else scale[:, i:i + 1]).then_inc(copied, 1)


def rms_rows(k, name, src, dst, gain=None, groups=1, mean=True, factor=1.0):
    nc, NT = k.nc, k.NT
    d = src.shape[2] // groups
    shape = [P, NT, groups, d]
    with Stage(nc, name) as st:
        sq = st.sb("sq", shape)
        ss = st.sb("ss", [P, NT, groups])
        step, summed, rooted = st.sem("step"), st.sem("summed"), st.sem("rooted")
        block = st.block()
        v = src.rearrange("p t (g d) -> p t g d", g=groups)
        w = dst.rearrange("p t (g d) -> p t g d", g=groups)
        sf = ss[:].rearrange("p t g -> p (t g)")
        c = 1.0 / d if mean else 1.0

        @block.vector
        def _(dve):
            after = Chain(dve, step)
            after(dve.tensor_tensor(sq[:], v, v, ALU.mult))
            after(dve.tensor_reduce(ss[:], sq[:], AX.X, ALU.add))
            dve.tensor_scalar(ss[:], ss[:], c / factor ** 2, 1e-6 / factor ** 2, ALU.mult, ALU.add
                              ).then_inc(summed, 1)
            dve.wait_ge(rooted, 1)
            op = dve.tensor_tensor(w, v, ss[:].unsqueeze(3).to_broadcast(shape), ALU.mult)
            if gain is not None:
                after(op)
                dve.tensor_tensor(w, w, gain.unsqueeze(1).unsqueeze(1).to_broadcast(shape), ALU.mult)

        @block.gpsimd
        def _(pool):
            pool.wait_ge(summed, 1)
            pool.tensor_tensor(sf, sf, k.nhalf[:, :NT * groups], ALU.pow).then_inc(rooted, 1)


def attention(k, name, units, q_of, k_of, v_of, bias_of, out_of, dv, sink_of=None, minus=None,
              keys=None):
    nc, ps = k.nc, k.ps
    G = len(units[0][0])
    keys = keys or (lambda t: list(range(t + 1)))
    NK = max(len(keys(t)) for _, t in units) * P
    O = G // 2 if minus else G
    with Stage(nc, name) as st:
        S = st.sb("S", [P, 2, G, NK])
        PT = st.sb("PT", [P, 2, O, NK])
        mx = st.sb("mx", [P, 2, G])
        sm = st.sb("sm", [P, 2, G])
        es = st.sb("es", [P, 2, G])
        step = st.sem("step")
        scored, biased, shifted, raised = st.sem("scored"), st.sem("biased"), st.sem("shifted"), st.sem("raised")
        mixed, turned, turned_out = st.sem("mixed"), st.sem("turned"), st.sem("turned_out")
        applied, stored, sunk = st.sem("applied"), st.sem("stored"), st.sem("sunk")
        block = st.block()
        sc = lambda u: ps[:, 2 * (u % 2):2 * (u % 2) + 2, :].rearrange("p b (g n) -> p g b n", n=256)
        pairs = lambda ap: ap.rearrange("p (g b) n -> p g b n", b=2)
        tr = ps[:, 4:6, :].rearrange("p b (g n) -> p (b g) n", n=256)
        ob = lambda u: ps[:, 6 + u % 2, :O * dv].rearrange("p (g n) -> p g n", n=dv)

        @block.tensor
        def _(pe):
            def scores(u):
                heads, t = units[u]
                if u >= 2:
                    pe.wait_ge(biased, u - 1)
                for g, h in enumerate(heads):
                    for i, kt in enumerate(keys(t)):
                        last = pe.matmul(sc(u)[:, g // 2, g % 2, i * P:(i + 1) * P], q_of(h, t), k_of(h, kt),
                                         start=True, stop=True)
                last.then_inc(scored, 1)

            scores(0)
            for u, (heads, t) in enumerate(units):
                if u + 1 < len(units):
                    scores(u + 1)
                if minus:
                    pe.wait_ge(mixed, u + 1)
                else:
                    pe.wait_ge(raised, u + 1)
                if u >= 1:
                    pe.wait_ge(turned_out, u)
                for g in range(O):
                    for i, kt in enumerate(keys(t)):
                        last = pe.transpose(tr[:, g, i * P:(i + 1) * P],
                                            S[:, u % 2, 2 * g if minus else g, i * P:(i + 1) * P], k.ident[:])
                last.then_inc(turned, 1)
                pe.wait_ge(turned_out, u + 1)
                if u >= 2:
                    pe.wait_ge(stored, u - 1)
                for g in range(O):
                    h = heads[2 * g] if minus else heads[g]
                    for i, kt in enumerate(keys(t)):
                        last = pe.matmul(ob(u)[:, g, :], PT[:, u % 2, g, i * P:(i + 1) * P], v_of(h, kt),
                                         start=i == 0, stop=i == len(keys(t)) - 1)
                last.then_inc(applied, 1)

        @block.scalar
        def _(act):
            for u, (heads, t) in enumerate(units):
                n = len(keys(t)) * P
                act.wait_ge(shifted, u + 1)
                act.activation(S[:, u % 2, :, :n], S[:, u % 2, :, :n], ACT.Exp).then_inc(raised, 1)
                if sink_of:
                    act.activation(es[:, u % 2, :], es[:, u % 2, :], ACT.Exp).then_inc(sunk, 1)
                act.wait_ge(turned, u + 1)
                if u >= 2:
                    act.wait_ge(applied, u - 1)
                act.activation(PT[:, u % 2, :, :n], tr[:, :O, :n], ACT.Copy).then_inc(turned_out, 1)

        @block.vector
        def _(dve):
            after = Chain(dve, step)

            def shift(u):
                heads, t = units[u]
                n = len(keys(t)) * P
                s, m, b = S[:, u % 2, :, :n], mx[:, u % 2, :], u % 2
                dve.wait_ge(scored, u + 1)
                if u >= 2:
                    dve.wait_ge(turned, u - 1)
                dve.tensor_tensor(pairs(s), sc(u)[:, :G // 2, :, :n], pairs(bias_of(heads, t)), ALU.add
                                  ).then_inc(biased, 1)
                dve.wait_ge(biased, u + 1)
                after(dve.tensor_reduce(m, s, AX.X, ALU.max))
                if sink_of:
                    after(dve.tensor_tensor(m, m, sink_of(heads), ALU.max))
                    after(dve.tensor_tensor(es[:, b, :], sink_of(heads), m, ALU.subtract))
                dve.tensor_tensor(s, s, m.unsqueeze(2).to_broadcast([P, G, n]), ALU.subtract
                                  ).then_inc(shifted, 1)

            def finish(u):
                heads, t = units[u]
                n = len(keys(t)) * P
                s, l = S[:, u % 2, :, :n], sm[:, u % 2, :]
                dve.wait_ge(raised, u + 1)
                after(dve.tensor_reduce(l, s, AX.X, ALU.add))
                if sink_of:
                    dve.wait_ge(sunk, u + 1)
                    after(dve.tensor_tensor(l, l, es[:, u % 2, :], ALU.add))
                after(dve.reciprocal(l, l))
                if minus:
                    after(dve.tensor_tensor(s, s, l.unsqueeze(2).to_broadcast([P, G, n]), ALU.mult))
                    for g in range(O):
                        last = dve.scalar_tensor_tensor(S[:, u % 2, 2 * g, :n], S[:, u % 2, 2 * g + 1, :n],
                                                        minus(g), S[:, u % 2, 2 * g, :n], ALU.mult, ALU.add)
                    last.then_inc(mixed, 1)

            shift(0)
            for u, (heads, t) in enumerate(units):
                if u + 1 < len(units):
                    shift(u + 1)
                finish(u)
                dve.wait_ge(applied, u + 1)
                out = out_of(heads, t)
                if minus:
                    dve.tensor_copy(out, ob(u)).then_inc(stored, 1)
                else:
                    dve.tensor_tensor(out, ob(u), sm[:, u % 2, :].unsqueeze(2).to_broadcast([P, G, dv]),
                                      ALU.mult).then_inc(stored, 1)


def dump(k, name, pairs):
    with Stage(k.nc, name) as st:
        stored = st.sem("stored")
        block = st.block()

        @block.sync
        def _(sp):
            for dst, src in pairs:
                sp.dma_start(dst, src).then_inc(stored, 16)
            sp.wait_ge(stored, 16 * len(pairs))


def on_vector(k, name, body):
    with Stage(k.nc, name) as st:
        step = st.sem("step")
        block = st.block()

        @block.vector
        def _(dve):
            body(dve, Chain(dve, step))


def on_scalar(k, name, body):
    with Stage(k.nc, name) as st:
        step = st.sem("step")
        block = st.block()

        @block.scalar
        def _(act):
            body(act, Chain(act, step))


def on_gpsimd(k, name, body):
    with Stage(k.nc, name) as st:
        step = st.sem("step")
        block = st.block()

        @block.gpsimd
        def _(pool):
            body(pool, Chain(pool, step))


def on_tensor(k, name, body):
    with Stage(k.nc, name) as st:
        block = st.block()

        @block.tensor
        def _(pe):
            body(pe)


def level_masks(k, masks):
    def body(pool, after):
        after(pool.memset(masks[:], 0.0))
        for v in range(7):
            b = 2 ** v
            half = masks[:, v, :].rearrange("s (n h j) -> s n h j", h=2, j=b)[:, :, 1, :]
            after(pool.memset(half, 1.0))
            after(pool.affine_select(out=half, in_=half, compare_op=ALU.is_ge, fill=0.0, base=0,
                                     pattern=[[-2 * b, P // (2 * b)], [0, b]], channel_multiplier=1))
            after(pool.affine_select(out=half, in_=half, compare_op=ALU.is_ge, fill=0.0, base=b - 1,
                                     pattern=[[2 * b, P // (2 * b)], [0, b]], channel_multiplier=-1))
    on_gpsimd(k, "level_masks", body)


def copier(nc, eng):
    return eng.copy if eng is nc.scalar else eng.tensor_copy


def tokens_to(k, dst):
    return lambda eng, psum, j, n0, n1: copier(k.nc, eng)(dst[:, j, n0:n1], psum[:, :n1 - n0])


def features_to(k, dst):
    def finish(eng, psum, j, n0, n1):
        i = n0 // P + 2 * j
        return copier(k.nc, eng)(dst[:, i:i + 2, :], psum[:, :2 * k.T].rearrange("p (i t) -> p i t", i=2))
    return finish


def turn_out(k, name, src, dst, n_tiles):
    with Stage(k.nc, name) as st:
        turned, copied = st.sem("turned"), st.sem("copied")
        block = st.block()
        groups = [(t, i, min(i + 4, n_tiles)) for t in range(k.NT) for i in range(0, n_tiles, 4)]

        @block.tensor
        def _(pe):
            for n, (t, i0, i1) in enumerate(groups):
                if n >= 8:
                    pe.wait_ge(copied, n - 7)
                for i in range(i0, i1):
                    last = pe.transpose(k.ps[:, n % 8, (i - i0) * P:(i - i0 + 1) * P],
                                        src[:, i, t * P:(t + 1) * P], k.ident[:])
                last.then_inc(turned, 1)

        @block.scalar
        def _(act):
            for n, (t, i0, i1) in enumerate(groups):
                act.wait_ge(turned, n + 1)
                act.copy(dst[:, t, i0 * P:i1 * P], k.ps[:, n % 8, :(i1 - i0) * P]).then_inc(copied, 1)


def alibi(k, name, table, dist, heads, width, step, offset):
    def fill(pool, after):
        for t in range(k.NT):
            after(pool.iota(dist[:, t, :], pattern=[[step, width]], base=offset - t * P,
                            channel_multiplier=-1, allow_small_or_imprecise_dtypes=True))
            for h in range(heads):
                after(pool.tensor_scalar(table[:, t, h, :width], dist[:, t, :],
                                         2.0 ** (-8.0 * (h + 1) / heads), None, ALU.mult))
            after(pool.affine_select(out=table[:, t, :, :width], in_=table[:, t, :, :width],
                                     compare_op=ALU.is_ge, fill=NEG, base=t * P - offset,
                                     pattern=[[0, heads], [-step, width]], channel_multiplier=1))
    on_gpsimd(k, name, fill)


def sparse_attention(k, A, scratch, y, ctx):
    nc, T, NT, ps = k.nc, k.T, k.NT, k.ps
    D, H, G = 64, 8, 2
    NC = (T - 32) // 16 + 1
    with ExitStack() as own:
        sb = lambda name, shape: own.enter_context(nc.sbuf_tensor("nsa_" + name, shape, F32))
        U = sb("U", [P, NT, 1304])
        gains = sb("gains", [P, 4, D])
        qT, kT = sb("qT", [P, 4, T]), sb("kT", [P, 2, 2, T])
        KD = sb("KD", [P, 2, NT, 2, 2, D])
        bias, dist = sb("bias", [P, NT, H, T]), sb("dist", [P, NT, T])
        O = sb("O", [P, NT, 3, H * D])
        flat = sb("flat", [2 * NC, 2, 2048])
        flatT = sb("flatT", [P, 2, 16, 2 * NC])
        pe_c = sb("pe_c", [P, 2, 16])
        w2 = sb("w2", [P, 2, 2, D])
        hid, g1, g2 = (sb(n, [P, 2, 2, 2 * NC]) for n in ("hid", "g1", "g2"))
        kc, vc = sb("kc", [2 * NC, 2, D]), sb("vc", [2 * NC, D])
        kss = sb("kss", [2 * NC, 1])
        kcT = sb("kcT", [P, 2 * NC])
        vbd = sb("vbd", [P, H * D])
        cb = sb("cb", [P, NT, H, 16])
        pc, pcT = sb("pc", [P, NT, H, 16]), sb("pcT", [P, NT, P])
        cm, cl, seen = sb("cm", [P, NT, H]), sb("cl", [P, NT, H]), sb("seen", [P, NT, H])

        load(k, "nsa_load", [(gains[:], A["nsa_qk_gain"][0].partition_broadcast(P)),
                             (pe_c[:, 0, :], A["cmp_pe"][0, 0].rearrange("(j l) d -> (l d) j", l=2)),
                             (pe_c[:, 1, :], A["cmp_pe"][0, 1].rearrange("(j l) d -> (l d) j", l=2)),
                             (w2[:, 0], A["cmp_w2"][0, 0].rearrange("(j p) d -> p j d", p=P)),
                             (w2[:, 1], A["cmp_w2"][0, 1].rearrange("(j p) d -> p j d", p=P))])
        alibi(k, "nsa_alibi", bias, dist, H, T, 1, 0)
        alibi(k, "nsa_alibi_c", cb, dist[:, :, :NC], H, NC, 16, 31)
        gemm(k, "nsa_in", k.hT, 8, A["w_in"][0][:, 1536:2840], 1304, tokens_to(k, U))
        dump(k, "nsa_out", [(scratch[c, g, t * P:(t + 1) * P, :],
                             U[:, t, 512 + (2 * c + g) * D:512 + (2 * c + g + 1) * D])
                            for c in range(2) for g in range(G) for t in range(NT)])
        load(k, "nsa_flat", [(flat[g * NC:(g + 1) * NC, c, :],
                              bass.AP(tensor=scratch.tensor, offset=(c * G + g) * T * D,
                                      ap=[[16 * D, NC], [1, 32 * D]]))
                             for c in range(2) for g in range(G)])

        def turn_flat(pe):
            for c in range(2):
                for j in range(16):
                    pe.transpose(ps[:, c, j * 2 * NC:(j + 1) * 2 * NC], flat[:, c, j * P:(j + 1) * P],
                                 k.ident[:2 * NC, :2 * NC])
        on_tensor(k, "nsa_tf", turn_flat)

        def add_pe(dve, after):
            for c in range(2):
                dve.tensor_tensor(flatT[:, c], ps[:, c, :32 * NC].rearrange("p (j n) -> p j n", j=16),
                                  pe_c[:, c, :].unsqueeze(2).to_broadcast([P, 16, 2 * NC]), ALU.add)
        on_vector(k, "nsa_pe", add_pe)
        for c in range(2):
            compress_hidden(k, f"nsa_c{c}", A["cmp_w1"][0, c], flatT[:, c], hid[:, c])

        def gelu_a(dve, after):
            after(dve.tensor_tensor(g1[:], hid[:], hid[:], ALU.mult))
            after(dve.tensor_scalar(g1[:], g1[:], 0.044715, 1.0, ALU.mult, ALU.add))
            after(dve.tensor_tensor(g1[:], g1[:], hid[:], ALU.mult))
        on_vector(k, "nsa_ga", gelu_a)
        on_scalar(k, "nsa_gb", lambda act, after:
                  act.activation(g2[:], g1[:], ACT.Tanh, scale=math.sqrt(2 / math.pi)))

        def gelu_c(dve, after):
            after(dve.tensor_scalar(g2[:], g2[:], 1.0, 0.5, ALU.add, ALU.mult))
            after(dve.tensor_tensor(hid[:], hid[:], g2[:], ALU.mult))
        on_vector(k, "nsa_gc", gelu_c)

        def second(pe):
            for c in range(2):
                for j in range(2):
                    pe.matmul(ps[:2 * NC, c, :D], hid[:, c, j, :], w2[:, c, j, :], start=j == 0, stop=j == 1)
        on_tensor(k, "nsa_w2", second)

        def kc_norm(dve, after):
            after(dve.memset(vbd[:], 0.0))
            after(dve.tensor_copy(vc[:], ps[:2 * NC, 1, :D]))
            after(dve.tensor_copy(kc[:, 0, :], ps[:2 * NC, 0, :D]))
            after(dve.tensor_tensor(kc[:, 1, :], kc[:, 0, :], kc[:, 0, :], ALU.mult))
            after(dve.tensor_reduce(kss[:], kc[:, 1, :], AX.X, ALU.add))
            after(dve.tensor_scalar(kss[:], kss[:], 1.0 / D, 1e-6, ALU.mult, ALU.add))
        on_vector(k, "nsa_kn", kc_norm)
        on_gpsimd(k, "nsa_kr", lambda pool, after:
                  pool.tensor_tensor(kss[:], kss[:], k.nhalf[:2 * NC, :1], ALU.pow))

        def kc_scale(dve, after):
            after(dve.scalar_tensor_tensor(kc[:, 0, :], kc[:, 0, :], kss[:, 0:1], gains[:2 * NC, 1, :],
                                           ALU.mult, ALU.mult))
            dve.tensor_copy(kc[:, 1, :], kc[:, 0, :])
        on_vector(k, "nsa_ks", kc_scale)
        load(k, "nsa_vbd", [(vbd[16 * h:16 * h + NC, h * D:(h + 1) * D],
                             vc[(h // 4) * NC:(h // 4 + 1) * NC, :]) for h in range(H)])
        on_tensor(k, "nsa_kt", lambda pe: pe.transpose(
            ps[:, 0, :2 * NC], kc[:].rearrange("n u d -> n (u d)"), k.ident[:2 * NC, :2 * NC]))
        on_vector(k, "nsa_kv", lambda dve, after: dve.tensor_copy(kcT[:], ps[:, 0, :2 * NC]))

        rms_rows(k, "nsa_q", U[:, :, 0:512], U[:, :, 0:512], gains[:, 0, :], groups=H)
        for n, (a, gi) in enumerate(((768, 2), (1024, 3))):
            rms_rows(k, f"nsa_k{n}", U[:, :, a:a + 128], U[:, :, a:a + 128], gains[:, gi, :], groups=G)

        def twice(dve, after):
            for n, a in enumerate((768, 1024)):
                for u in range(2):
                    dve.tensor_copy(KD[:, n, :, :, u, :], U[:, :, a:a + 128].rearrange("p t (g d) -> p t g d", g=G))
        on_vector(k, "nsa_twice", twice)
        transpose_in(k, "nsa_qT", U, qT, 4, factor=D ** -0.5)
        for n in range(2):
            transpose_in(k, f"nsa_kT{n}", None, kT[:, n], 2,
                         src_cols=lambda t, i, n=n: KD[:, n, t, i].rearrange("p u d -> p (u d)"))
        half = lambda h: slice((h % 2) * D, (h % 2 + 1) * D)
        units = [(list(range(g * 4, g * 4 + 4)), t) for t in range(NT) for g in range(G)]
        for n, a in enumerate((896, 1152)):
            attention(k, f"nsa_a{n}", units,
                      q_of=lambda h, t: qT[half(h), h // 2, t * P:(t + 1) * P],
                      k_of=lambda h, kt, n=n: kT[half(h), n, h // 4, kt * P:(kt + 1) * P],
                      v_of=lambda h, kt, a=a: U[:, kt, a + (h // 4) * D:a + (h // 4 + 1) * D],
                      bias_of=lambda hs, t: bias[:, t, hs[0]:hs[-1] + 1, :(t + 1) * P],
                      out_of=lambda hs, t, n=n: O[:, t, 1 + n, hs[0] * D:(hs[-1] + 1) * D].rearrange(
                          "p (g d) -> p g d", d=D), dv=D)

        def c_scores(pe):
            for t in range(NT):
                for h in range(H):
                    pe.matmul(ps[:, 2 * t + h % 2, h // 2 * 16:h // 2 * 16 + NC], qT[half(h), h // 2, t * P:(t + 1) * P],
                              kcT[half(h), (h // 4) * NC:(h // 4 + 1) * NC], start=True, stop=True)
        on_tensor(k, "nsa_cs", c_scores)
        flat2 = lambda x: x[:].rearrange("p t h -> p (t h)")
        pcv = pc[:].rearrange("p t h n -> p (t h) n")

        def c_shift(dve, after):
            after(dve.memset(pc[:], 0.0))
            for t in range(NT):
                pair = lambda x: x[:, t].rearrange("p (g b) n -> p g b n", b=2)[:, :, :, :NC]
                after(dve.tensor_tensor(pair(pc), ps[:, 2 * t:2 * t + 2, :64].rearrange(
                    "p b (g n) -> p g b n", n=16)[:, :, :, :NC], pair(cb), ALU.add))
            after(dve.tensor_reduce(flat2(cm), pcv[:, :, :NC], AX.X, ALU.max))
            after(dve.tensor_tensor(pcv[:, :, :NC], pcv[:, :, :NC],
                                    flat2(cm).unsqueeze(2).to_broadcast([P, NT * H, NC]), ALU.subtract))
            after(dve.tensor_scalar(seen[:], cm[:], NEG / 2, None, ALU.is_gt))
        on_vector(k, "nsa_c1", c_shift)
        on_scalar(k, "nsa_c2", lambda act, after: act.activation(pcv[:, :, :NC], pcv[:, :, :NC], ACT.Exp))

        def c_norm(dve, after):
            after(dve.tensor_reduce(flat2(cl), pcv[:, :, :NC], AX.X, ALU.add))
            after(dve.reciprocal(cl[:], cl[:]))
            after(dve.tensor_tensor(cl[:], cl[:], seen[:], ALU.mult))
            dve.tensor_tensor(pcv[:, :, :NC], pcv[:, :, :NC],
                              flat2(cl).unsqueeze(2).to_broadcast([P, NT * H, NC]), ALU.mult)
        on_vector(k, "nsa_c3", c_norm)
        on_tensor(k, "nsa_c4", lambda pe: [pe.transpose(
            ps[:, t, :P], pc[:, t].rearrange("p h n -> p (h n)"), k.ident[:]) for t in range(NT)])
        on_vector(k, "nsa_c5", lambda dve, after: [dve.tensor_copy(pcT[:, t], ps[:, t, :P]) for t in range(NT)])
        on_tensor(k, "nsa_c6", lambda pe: [pe.matmul(ps[:, t, :], pcT[:, t], vbd[:], start=True, stop=True)
                                           for t in range(NT)])
        gates = U[:, :, 1280:1304]
        on_scalar(k, "nsa_g", lambda act, after: act.activation(gates, gates, ACT.Sigmoid))

        def combine(dve, after):
            for t in range(NT):
                after(dve.tensor_copy(O[:, t, 0, :], ps[:, t, :]))
                Ot = O[:, t].rearrange("p b (h d) -> p (b h) d", d=D)
                after(dve.tensor_tensor(Ot, Ot, U[:, t, 1280:1304].unsqueeze(2).to_broadcast([P, 24, D]), ALU.mult))
                after(dve.tensor_tensor(y[:, t, :], O[:, t, 0, :], O[:, t, 1, :], ALU.add))
                after(dve.tensor_tensor(y[:, t, :], y[:, t, :], O[:, t, 2, :], ALU.add))
        on_vector(k, "nsa_y", combine)


def compress_hidden(k, name, w1, xT, hid):
    nc, ps, N = k.nc, k.ps, xT.shape[2]
    w = k.wring[:, 0, :].rearrange("p (k n) -> p k n", k=16)
    with Stage(nc, name) as st:
        landed, filled = st.sem("landed"), st.sem("filled")
        block = st.block()

        @block.sync
        def _(sp):
            sp.dma_start(w, w1.rearrange("(k p) n -> p k n", p=P)).then_inc(landed, 16)

        @block.tensor
        def _(pe):
            pe.wait_ge(landed, 16)
            for j in range(2):
                for kt in range(16):
                    last = pe.matmul(ps[:, j, :N], w[:, kt, j * P:(j + 1) * P], xT[:, kt, :],
                                     start=kt == 0, stop=kt == 15)
                last.then_inc(filled, 1)

        @block.vector
        def _(dve):
            for j in range(2):
                dve.wait_ge(filled, j + 1)
                dve.tensor_copy(hid[:, j, :], ps[:, j, :N])


def column(v, n=None):
    return v.rearrange("(i p) -> p i", p=P)


def gated_delta(k, A, masks, y):
    nc, T, NT, ps = k.nc, k.T, k.NT, k.ps
    H, D = 4, 128
    assert NT == 2
    with ExitStack() as own:
        sb = lambda name, shape: own.enter_context(nc.sbuf_tensor("gdn_" + name, shape, F32))
        cw = sb("cw", [P, 4, 12])
        alog, dt, gain = sb("alog", [P, H]), sb("dt", [P, H]), sb("gain", [P, D])
        Z = sb("Z", [P, NT, 520])
        raw, conv = sb("raw", [P, 12, T + 3]), sb("conv", [P, 12, T])
        tok = sb("tok", [P, NT, 1536])
        load(k, "gdn_load", [(cw[:, j, :], column(A["gdn_conv_w"][0, j])) for j in range(4)]
             + [(alog[:], rows(A["gdn_a_log"][0])), (dt[:], rows(A["gdn_dt_bias"][0])),
                (gain[:], rows(A["gdn_out_gain"][0]))])
        gemm(k, "gdn_in", k.hT, 8, A["w_in"][0][:, 2840:4376], 1536, features_to(k, raw[:, :, 3:]),
             feature_major=True)
        gemm(k, "gdn_z", k.hT, 8, A["w_in"][0][:, 4376:4896], 520, tokens_to(k, Z))

        def convolve(dve, after):
            after(dve.memset(raw[:, :, 0:3], 0.0))
            for j in range(4):
                for i in range(12):
                    if j == 0:
                        op = dve.tensor_scalar(conv[:, i, :], raw[:, i, 0:T], cw[:, 0, i:i + 1], None, ALU.mult)
                    else:
                        op = dve.scalar_tensor_tensor(conv[:, i, :], raw[:, i, j:j + T], cw[:, j, i:i + 1],
                                                      conv[:, i, :], ALU.mult, ALU.add)
                after(op)
        on_vector(k, "gdn_conv", convolve)
        on_scalar(k, "gdn_silu", lambda act, after: act.activation(conv[:], conv[:], ACT.Silu))
        turn_out(k, "gdn_tok", conv, tok, 12)
        rms_rows(k, "gdn_q", tok[:, :, 0:512], tok[:, :, 0:512], groups=H, mean=False, factor=D ** -0.5)
        rms_rows(k, "gdn_k", tok[:, :, 512:1024], tok[:, :, 512:1024], groups=H, mean=False)
        beta, sp, ab, g = (sb(n, [P, NT, H]) for n in ("beta", "sp", "ab", "g"))
        gcs = sb("gcs", [P, NT, 2, H])
        e1, e2 = sb("e1", [P, NT, H]), sb("e2", [P, NT, H])

        def decay_in(dve, after):
            after(dve.tensor_tensor(sp[:], Z[:, :, 516:520], dt[:].unsqueeze(1).to_broadcast([P, NT, H]), ALU.add))
            after(dve.tensor_scalar(ab[:], sp[:], -1.0, None, ALU.mult))
            after(dve.tensor_tensor(ab[:], ab[:], sp[:], ALU.min))
        on_vector(k, "gdn_g1", decay_in)

        def soft(act, after):
            after(act.activation(ab[:], ab[:], ACT.Exp))
            after(act.activation(ab[:], ab[:], ACT.Ln, bias=1.0))
            act.activation(alog[:], alog[:], ACT.Exp)
            act.activation(beta[:], Z[:, :, 512:516], ACT.Sigmoid)
            act.activation(Z[:, :, 0:512], Z[:, :, 0:512], ACT.Silu)
        on_scalar(k, "gdn_g2", soft)

        def decay(dve, after):
            after(dve.scalar_tensor_tensor(g[:], sp[:], 0.0, ab[:], ALU.max, ALU.add))
            after(dve.scalar_tensor_tensor(g[:], g[:], -1.0, alog[:].unsqueeze(1).to_broadcast([P, NT, H]),
                                           ALU.mult, ALU.mult))
        on_vector(k, "gdn_g3", decay)
        part = lambda x, i: x[:].rearrange("p a b -> p (a b)")[:, i * NT * H * P:(i + 1) * NT * H * P].rearrange(
            "p (t h c) -> p t h c", t=NT, h=H)
        grep, Ti, XX = (part(conv, i) for i in range(3))
        kb, kbg, CT = (part(raw, i) for i in range(3))
        on_vector(k, "gdn_g4", lambda dve, after: dve.tensor_copy(
            grep, g[:].unsqueeze(3).to_broadcast([P, NT, H, P])))

        def running(pe):
            for t in range(NT):
                pe.matmul(ps[:, t, 0:H], k.upto[:], g[:, t, :], start=True, stop=True)
                pe.matmul(ps[:, t, H:2 * H], k.ones[:], g[:, t, :], start=True, stop=True)
                for h in range(H):
                    pe.matmul(ps[:, 2 + t, h * P:(h + 1) * P], grep[:, t, h, :], k.upto[:], start=True, stop=True)
        on_tensor(k, "gdn_run", running)
        DT = sb("DT", [P, NT, H, P])

        def decays(dve, after):
            after(dve.tensor_copy(gcs[:].rearrange("p t u h -> p t (u h)"), ps[:, 0:2, :2 * H]))
            after(dve.tensor_copy(e1[:], gcs[:, :, 0, :]))
            after(dve.tensor_tensor(e2[:], gcs[:, :, 1, :], gcs[:, :, 0, :], ALU.subtract))
            after(dve.tensor_tensor(DT[:], ps[:, 2:4, :].rearrange("p t (h c) -> p t h c", h=H),
                                    e1[:].unsqueeze(3).to_broadcast([P, NT, H, P]), ALU.subtract))
            after(dve.tensor_scalar(DT[:], DT[:], 0.0, None, ALU.min))
        on_vector(k, "gdn_d1", decays)

        el = sb("el", [P, NT, H])

        def exps(act, after):
            act.activation(DT[:], DT[:], ACT.Exp)
            act.activation(el[:], gcs[:, :, 1, :], ACT.Exp)
            act.activation(e1[:], e1[:], ACT.Exp)
            act.activation(e2[:], e2[:], ACT.Exp)
        on_scalar(k, "gdn_d2", exps)
        vb, kd = (sb(n, [P, NT, H, D]) for n in ("vb", "kd"))
        qd = sb("qd", [P, H, D])
        q4, k4, v4 = (tok[:, :, a:a + 512].rearrange("p t (h d) -> p t h d", h=H) for a in (0, 512, 1024))
        by = lambda x: x.unsqueeze(3).to_broadcast([P, NT, H, D])

        def weigh(dve, after):
            dve.tensor_tensor(DT[:], DT[:], k.upto[:].unsqueeze(1).unsqueeze(1).to_broadcast([P, NT, H, P]), ALU.mult)
            dve.tensor_tensor(vb[:], v4, by(beta[:]), ALU.mult)
            dve.tensor_tensor(kd[:], k4, by(e2[:]), ALU.mult)
            dve.tensor_tensor(qd[:], q4[:, 1], e1[:, 1].unsqueeze(2).to_broadcast([P, H, D]), ALU.mult)
            after(dve.tensor_tensor(kb, k4, by(beta[:]), ALU.mult))
            dve.tensor_tensor(kbg, kb, by(e1[:]), ALU.mult)
        on_vector(k, "gdn_w", weigh)
        qT, kT, kbT, qdT = (sb(n, [P, H, T]) for n in ("qT", "kT", "kbT", "qdT"))
        for n, (src, dst) in enumerate(((tok[:, :, 0:512], qT), (tok[:, :, 512:1024], kT),
                                        (kb.rearrange("p t h d -> p t (h d)"), kbT))):
            transpose_in(k, f"gdn_t{n}", src, dst, H)
        transpose_in(k, "gdn_t3", None, qdT, H, src_cols=lambda t, i: qd[:, i, :])
        MT, AT = sb("MT", [P, NT, H, P]), sb("AT", [P, NT, H, P])

        def products(pe):
            for t in range(NT):
                for h in range(H):
                    kh = kT[:, h, t * P:(t + 1) * P]
                    pe.matmul(ps[:, t, h * P:(h + 1) * P], kh, kbT[:, h, t * P:(t + 1) * P], start=True, stop=True)
                    pe.matmul(ps[:, 2 + t, h * P:(h + 1) * P], kh, qT[:, h, t * P:(t + 1) * P], start=True, stop=True)
        on_tensor(k, "gdn_kk", products)
        bank = lambda i: ps[:, i:i + 2, :].rearrange("p t (h c) -> p t h c", h=H)
        on_vector(k, "gdn_m", lambda dve, after: [
            dve.tensor_tensor(MT[:], bank(0), DT[:], ALU.mult), dve.tensor_tensor(AT[:], bank(2), DT[:], ALU.mult)])
        TT = sb("TT", [P, NT, H, P])
        solve_unit_triangle(k, "gdn_s", MT, masks, Ti, TT[:], CT, XX, NT, H)

        vn, S = vb, sb("S", [P, H, D])
        wT = sb("wT", [P, H, P])

        def uw(pe):
            for h in range(H):
                for t in range(NT):
                    pe.matmul(ps[:, t, h * D:(h + 1) * D], TT[:, t, h, :], vb[:, t, h, :], start=True, stop=True)
                pe.matmul(ps[:, 2, h * P:(h + 1) * P], kbg[:, 1, h, :], TT[:, 1, h, :], start=True, stop=True)
        on_tensor(k, "gdn_uw", uw)
        on_vector(k, "gdn_u", lambda dve, after: [
            dve.tensor_copy(vn[:], bank(0)),
            dve.tensor_copy(wT[:], ps[:, 2, :].rearrange("p (h c) -> p h c", h=H))])

        def first_chunk(pe):
            for h in range(H):
                pe.matmul(ps[:, 0, h * D:(h + 1) * D], AT[:, 0, h, :], vn[:, 0, h, :], start=True, stop=True)
                pe.matmul(ps[:, 1, h * D:(h + 1) * D], kd[:, 0, h, :], vn[:, 0, h, :], start=True, stop=True)
        on_tensor(k, "gdn_c0", first_chunk)
        on_vector(k, "gdn_s0", lambda dve, after: [
            dve.tensor_copy(tok[:, 0, 0:512], ps[:, 0, :]),
            dve.tensor_copy(S[:], ps[:, 1, :].rearrange("p (h c) -> p h c", h=H))])
        on_tensor(k, "gdn_ws", lambda pe: [pe.matmul(ps[:, 0, h * D:(h + 1) * D], wT[:, h, :], S[:, h, :],
                                                     start=True, stop=True) for h in range(H)])
        on_vector(k, "gdn_v1", lambda dve, after: dve.tensor_tensor(
            vn[:, 1], vn[:, 1], ps[:, 0, :].rearrange("p (h c) -> p h c", h=H), ALU.subtract))

        def second_chunk(pe):
            for h in range(H):
                pe.matmul(ps[:, 1, h * D:(h + 1) * D], qdT[:, h, P:2 * P], S[:, h, :], start=True, stop=False)
                pe.matmul(ps[:, 1, h * D:(h + 1) * D], AT[:, 1, h, :], vn[:, 1, h, :], start=False, stop=True)
        on_tensor(k, "gdn_c1", second_chunk)
        on_vector(k, "gdn_o1", lambda dve, after: dve.tensor_copy(tok[:, 1, 0:512], ps[:, 1, :]))
        rms_rows(k, "gdn_o", tok[:, :, 0:512], tok[:, :, 512:1024], gain[:], groups=H)
        on_vector(k, "gdn_y", lambda dve, after: dve.tensor_tensor(
            y[:], tok[:, :, 512:1024], Z[:, :, 0:512], ALU.mult))


def solve_unit_triangle(k, name, MT, masks, Ti, TT, CT, XX, NT, H):
    ps, nc = k.ps, k.nc
    b = lambda i: ps[:, i, :].rearrange("p (h c) -> p h c", h=H)
    with Stage(nc, name) as st:
        step = st.sem("step")
        joined = [st.sem(f"joined{t}") for t in range(NT)]
        crossed = [st.sem(f"crossed{t}") for t in range(NT)]
        held = [st.sem(f"held{t}") for t in range(NT)]
        closed = [st.sem(f"closed{t}") for t in range(NT)]
        block = st.block()
        L = masks.shape[1]

        @block.vector
        def _(dve):
            after = Chain(dve, step)
            for x in (Ti, TT):
                op = dve.tensor_copy(x, k.ident[:].unsqueeze(1).unsqueeze(1).to_broadcast([P, NT, H, P]))
            after(op)
            for v in range(L):
                for t in range(NT):
                    dve.tensor_tensor(CT[:, t], MT[:, t], masks[:, v, :].unsqueeze(1).to_broadcast([P, H, P]),
                                      ALU.mult).then_inc(joined[t], 1)
                for t in range(NT):
                    dve.wait_ge(crossed[t], v + 1)
                    dve.tensor_copy(XX[:, t], b(t)).then_inc(held[t], 1)
                for t in range(NT):
                    dve.wait_ge(closed[t], v + 1)
                    dve.tensor_tensor(Ti[:, t], Ti[:, t], b(2 + t), ALU.subtract)
                    op = dve.tensor_tensor(TT[:, t], TT[:, t], b(4 + t), ALU.subtract)
                after(op)

        @block.tensor
        def _(pe):
            for v in range(L):
                for t in range(NT):
                    pe.wait_ge(joined[t], v + 1)
                    for h in range(H):
                        last = pe.matmul(b(t)[:, h], CT[:, t, h], Ti[:, t, h], start=True, stop=True)
                    last.then_inc(crossed[t], 1)
                for t in range(NT):
                    pe.wait_ge(held[t], v + 1)
                    for h in range(H):
                        pe.matmul(b(2 + t)[:, h], TT[:, t, h], XX[:, t, h], start=True, stop=True)
                        last = pe.matmul(b(4 + t)[:, h], XX[:, t, h], TT[:, t, h], start=True, stop=True)
                    last.then_inc(closed[t], 1)


def short_conv(k, A, y):
    nc, T = k.nc, k.T
    with ExitStack() as own:
        sb = lambda name, shape: own.enter_context(nc.sbuf_tensor("sc_" + name, shape, F32))
        cw, u, cx = sb("cw", [P, 3, 4]), sb("u", [P, 12, T]), sb("cx", [P, 4, T + 2])
        load(k, "sc_load", [(cw[:, j, :], column(A["conv_a_w"][0, j])) for j in range(3)])
        gemm(k, "sc_in", k.hT, 8, A["w_in"][0][:, 0:1536], 1536, features_to(k, u), feature_major=True)

        def body(dve, after):
            after(dve.memset(cx[:, :, 0:2], 0.0))
            after(dve.tensor_tensor(cx[:, :, 2:], u[:, 4:8, :], u[:, 8:12, :], ALU.mult))
            for j in range(3):
                for i in range(4):
                    if j == 0:
                        op = dve.tensor_scalar(y[:, i, :], cx[:, i, 0:T], cw[:, 0, i:i + 1], None, ALU.mult)
                    else:
                        op = dve.scalar_tensor_tensor(y[:, i, :], cx[:, i, j:j + T], cw[:, j, i:i + 1],
                                                      y[:, i, :], ALU.mult, ALU.add)
                after(op)
            dve.tensor_tensor(y[:], y[:], u[:, 0:4, :], ALU.mult)
        on_vector(k, "sc_conv", body)


def merge_branches(k, A, yT):
    nc, NT = k.nc, k.NT
    with ExitStack() as own:
        sb = lambda name, shape: own.enter_context(nc.sbuf_tensor("mb_" + name, shape, F32))
        gates, tmp, merged = sb("gates", [P, NT, 3072]), sb("tmp", [P, NT, BANK]), sb("merged", [P, NT, 1024])
        bias = sb("bias", [1, 3072])
        load(k, "mb_load", [(bias[:], A["b_gate"])])
        gemm(k, "mb_gates", k.hT, 8, A["w_gate"][0], 3072, tokens_to(k, gates), bias=bias)
        on_scalar(k, "mb_sig", lambda act, after: act.activation(gates[:], gates[:], ACT.Sigmoid))
        for r in range(3):
            branch = sb(f"branch{r}", [P, NT, 1024]) if r == 0 else branch
            gemm(k, f"mb_branch{r}", yT[r], 4, A["w_branch"][0, r], 1024, tokens_to(k, branch))

            def weigh(dve, after, r=r):
                g = gates[:, :, r * 1024:(r + 1) * 1024]
                after(dve.tensor_tensor(merged[:] if r == 0 else branch[:], branch[:], g, ALU.mult))
                if r:
                    dve.tensor_tensor(merged[:], merged[:], branch[:], ALU.add)
            on_vector(k, f"mb_w{r}", weigh)
        transpose_in(k, "mb_t", merged, k.hT)
        gemm(k, "mb_out", k.hT, 8, A["w_out"][0], 1024, tokens_to(k, branch))
        on_vector(k, "mb_x", lambda dve, after: dve.tensor_tensor(k.X[:], k.X[:], branch[:], ALU.add))


def swiglu(k, name, w_in, w_out, HID, y, ada=None):
    nc, T, NT, ps = k.nc, k.T, k.NT, k.ps
    U, FT, KIND = 2, 2, 3
    n_blocks = HID // (FT * P)
    whole, rest = divmod(n_blocks, U)
    G, UP, D = range(KIND)
    raw_all = k.wring[:].rearrange("p a b -> p (a b)").rearrange("p (u j n) -> p u j n", u=U, j=KIND)
    AH = 1536
    with Stage(nc, name) as st:
        hi, lo = (st.sb(n, [P, KIND, 2048], F32R) for n in ("hi", "lo"))
        h_hi, h_lo = (st.sb(n, [P, 8, T], F32R) for n in ("h_hi", "h_lo"))
        silu, hidden = st.sb("silu", [P, FT, T]), st.sb("hidden", [P, FT, T])
        hid_hi, hid_lo = (st.sb(n, [P, U, FT, T], F32R) for n in ("hid_hi", "hid_lo"))
        landed = [[st.sem(f"landed{j}{u}") for u in range(U)] for j in range(KIND)]
        high = [st.sem(f"high{j}") for j in range(KIND)]
        split = [st.sem(f"split{j}") for j in range(KIND)]
        h_high, h_split = st.sem("h_high"), st.sem("h_split")
        gate_read, down_read = st.sem("gate_read"), st.sem("down_read")
        filled = [st.sem(f"filled{f}") for f in range(FT)]
        silued = [st.sem(f"silued{f}") for f in range(FT)]
        made = [st.sem(f"made{f}") for f in range(FT)]
        hid_high = [st.sem(f"hid_high{f}") for f in range(FT)]
        hid_split = [st.sem(f"hid_split{f}") for f in range(FT)]
        summed = st.sem("summed")
        if ada is not None:
            aw = st.sb("aw", [P, 2, AH])
            ada_landed, ada_base = k.ada_landed, k.ada_base
            k.ada_base += 256
            ada_zeroed, ada_added = st.sem("ada_zeroed"), st.sem("ada_added")
        block = st.block()

        def steps(eng, step, n_ada=0):
            for u in range(U):
                step(0, u, u == 0, u == 1, n_ada > 0)
            for a, z in ((1, n_ada // U), (max(1, n_ada // U), whole)):
                if a < z:
                    with eng.Fori(a, z) as i:
                        for u in range(U):
                            step(i, u, False, False, a < n_ada // U)
            for u in range(rest):
                step(whole, u, False, False, False)
        N_ADA = 8 if ada is not None else 0

        @block.sync
        def _(sp):
            def fetch(i, u, first, second, _a):
                b = i * U + u
                for j in range(KIND):
                    if not (first or second):
                        sp.wait_ge(split[j], b - 1)
                    if j == D:
                        src = w_out[bass.ds(b * FT * P, FT * P), :]
                    else:
                        src = w_in[:, bass.ds(b * FT * P + j * HID, FT * P)]
                    sp.dma_start(raw_all[:, u, j, :].rearrange("p (k n) -> p k n", k=8 if j < D else FT),
                                 src.rearrange("(k p) n -> p k n", p=P)).then_inc(landed[j][u], 16)
            steps(sp, fetch)

        @block.gpsimd
        def _(pool):
            if ada is None:
                return
            pool.memset(k.ada[:], 0.0).then_inc(ada_zeroed, 1)

            def fetch(b, first):
                for q in range(4):
                    s, half = divmod(q, 2)
                    if not (first and q < 2):
                        pool.wait_ge(ada_added, b * 4 + q - 1)
                    pool.dma_start(aw[:, q % 2, :], ada[s][bass.ds(b * P, P), half * AH:(half + 1) * AH]
                                   ).then_inc(ada_landed[q % 2], 16)
            fetch(0, True)
            with pool.Fori(1, 8) as b:
                fetch(b, False)

        def product(pe, out, a_hi, a_lo, b_hi, b_lo, start, stop):
            pe.matmul(out, a_hi, b_hi, start=start, stop=False, skip_group_check=True)
            pe.matmul(out, a_hi, b_lo, start=False, stop=False, skip_group_check=True)
            return pe.matmul(out, a_lo, b_hi, start=False, stop=stop, skip_group_check=True)

        @block.tensor
        def _(pe):
            def gate_up(b, u, early):
                for f in range(FT):
                    bank = u * FT + f
                    if not early:
                        pe.wait_ge(made[f], b - 1)
                    for j in (G, UP):
                        if f == 0:
                            pe.wait_ge(split[j], b + 1)
                        for kt in range(8):
                            at = slice(kt * FT * P + f * P, kt * FT * P + (f + 1) * P)
                            last = product(pe, ps[:, bank, j * T:(j + 1) * T], hi[:, j, at], lo[:, j, at],
                                           h_hi[:, kt, :], h_lo[:, kt, :], kt == 0, kt == 7)
                        if j == G and f == FT - 1:
                            last.then_inc(gate_read, 1)
                    last.then_inc(filled[f], 1)

            def down(b, u, first, final):
                pe.wait_ge(split[D], b + 1)
                for f in range(FT):
                    pe.wait_ge(hid_split[f], b + 1)
                    for t in range(NT):
                        at = slice(t * P, (t + 1) * P)
                        for n in range(2):
                            cols = slice(f * 1024 + n * BANK, f * 1024 + (n + 1) * BANK)
                            last = product(pe, ps[:, 4 + 2 * t + n, :], hid_hi[:, u, f, at], hid_lo[:, u, f, at],
                                           hi[:, D, cols], lo[:, D, cols], first and f == 0,
                                           final and f == FT - 1)
                last.then_inc(down_read, 1)

            def step(i, u, first, second, _a):
                b = i * U + u
                gate_up(b, u, first or second)
                if not first:
                    down(b - 1, 1 - u, second, False)
            pe.wait_ge(h_split, 1)
            steps(pe, step)
            down(n_blocks - 1, (n_blocks - 1) % U, False, True)
            pe.matmul(ps[:, 0, :P], k.zero[:], k.ident[:], start=True, stop=True).then_inc(summed, 1)

        @block.scalar
        def _(act):
            def take(i, u, j):
                act.wait_ge(landed[j][u], i * 16 + 16)
                act.copy(hi[:, j, :], raw_all[:, u, j, :]).then_inc(high[j], 1)

            def last_down(i, u, first, second):
                if first:
                    return
                if not second:
                    act.wait_ge(down_read, i * U + u - 1)
                take(i if u else i - 1, 1 - u, D)

            def ahead(i, u):
                b = i * U + u
                act.wait_ge(gate_read, b + 1)
                take(i + u, 1 - u, G)
                act.wait_ge(filled[FT - 1], b + 1)
                take(i + u, 1 - u, UP)

            def make(i, u):
                b = i * U + u
                for f in range(FT):
                    act.wait_ge(filled[f], b + 1)
                    act.activation(silu[:, f, :], ps[:, u * FT + f, 0:T], ACT.Silu).then_inc(silued[f], 1)
                for f in range(FT):
                    act.wait_ge(made[f], b + 1)
                    act.copy(hid_hi[:, u, f, :], hidden[:, f, :]).then_inc(hid_high[f], 1)

            def step(i, u, first, second, _a, final=False):
                last_down(i, u, first, second)
                if not final:
                    ahead(i, u)
                make(i, u)
            act.copy(h_hi[:].rearrange("p k t -> p (k t)"), k.hT[:].rearrange("p k t -> p (k t)")
                     ).then_inc(h_high, 1)
            take(0, 0, G)
            take(0, 0, UP)
            assert rest == 1
            for u in range(U):
                step(0, u, u == 0, u == 1, False)
            with act.Fori(1, whole) as i:
                for u in range(U):
                    step(i, u, False, False, False)
            step(whole, 0, False, False, False, final=True)
            act.wait_ge(down_read, n_blocks - 1)
            take(whole, 0, D)

        @block.vector
        def _(dve):
            def take(b, u, j):
                dve.wait_ge(high[j], b + 1)
                dve.tensor_tensor(lo[:, j, :], raw_all[:, u, j, :], hi[:, j, :].bitcast(F32), ALU.subtract
                                  ).then_inc(split[j], 1)

            def modulation_rows(b, first):
                for q in range(4):
                    s, half = divmod(q, 2)
                    dve.wait_ge(ada_landed[q % 2], ada_base + b * 32 + (q // 2 + 1) * 16)
                    if not (first and q == 0):
                        dve.wait_ge(ada_added, b * 4 + q)
                    part = k.ada[:, s, half * AH:(half + 1) * AH]
                    dve.scalar_tensor_tensor(part, aw[:, q % 2, :], k.c[:, bass.ds(b, 1)], part,
                                             ALU.mult, ALU.add).then_inc(ada_added, 1)

            def step(i, u, first, second, with_ada, final=False):
                b = i * U + u
                if not first:
                    take(b - 1, 1 - u, D)
                if with_ada:
                    modulation_rows(b, first)
                if not final:
                    take(b + 1, 1 - u, G)
                    take(b + 1, 1 - u, UP)
                for f in range(FT):
                    dve.wait_ge(silued[f], b + 1)
                    if not first:
                        dve.wait_ge(hid_split[f], b)
                    dve.tensor_tensor(hidden[:, f, :], silu[:, f, :], ps[:, u * FT + f, T:2 * T], ALU.mult
                                      ).then_inc(made[f], 1)
                for f in range(FT):
                    dve.wait_ge(hid_high[f], b + 1)
                    dve.tensor_tensor(hid_lo[:, u, f, :], hidden[:, f, :], hid_hi[:, u, f, :].bitcast(F32),
                                      ALU.subtract).then_inc(hid_split[f], 1)
            dve.wait_ge(h_high, 1)
            dve.tensor_tensor(h_lo[:].rearrange("p k t -> p (k t)"), k.hT[:].rearrange("p k t -> p (k t)"),
                              h_hi[:].rearrange("p k t -> p (k t)").bitcast(F32), ALU.subtract).then_inc(h_split, 1)
            take(0, 0, G)
            take(0, 0, UP)
            if ada is not None:
                dve.wait_ge(ada_zeroed, 1)
            for u in range(U):
                step(0, u, u == 0, u == 1, N_ADA > 0)
            split_at = max(1, N_ADA // U)
            if split_at > 1:
                with dve.Fori(1, split_at) as i:
                    for u in range(U):
                        step(i, u, False, False, True)
            with dve.Fori(split_at, whole) as i:
                for u in range(U):
                    step(i, u, False, False, False)
            step(whole, 0, False, False, False, final=True)
            take(n_blocks - 1, 0, D)
            dve.wait_ge(summed, 1)
            dve.tensor_copy(y[:].rearrange("p t n -> p (t n)"), ps[:, 4:8, :].rearrange("p b n -> p (b n)"))


def route(k, A, h, one, pick, perm, permT, fac, hg, flags):
    nc, T, NT, ps = k.nc, k.T, k.NT, k.ps
    NG, NE = 4, 8
    assert T <= 2 * P
    with ExitStack() as own:
        sb = lambda name, shape: own.enter_context(nc.sbuf_tensor("rt_" + name, shape, F32))
        lg, le = sb("lg", [P, NT, NG]), sb("le", [P, NT, NG * NE])
        bg, be = sb("bg", [P, NG]), sb("be", [P, NG * NE])
        mg, zg, d2, w1, w2 = (sb(n, [P, NT]) for n in ("mg", "zg", "d2", "w1", "w2"))
        m1, m2 = sb("m1", [P, NT]), sb("m2", [P, NT])
        cum = sb("cum", [P, NT, NE])
        ex = sb("ex", [P, NT, NG])
        mine, two = (sb(n, [P, NT, NE]) for n in ("mine", "two"))
        rank, late = sb("rank", [P, NT]), sb("late", [P, NT])
        count, slots, fl = sb("count", [P, NG]), sb("slots", [P, P]), sb("fl", [P, 2])
        load(k, "rt_load", [(bg[:], rows(A["b_router_group"][0])), (be[:], rows(A["b_router_expert"][0]))])
        gemm(k, "rt_g", k.hT, 8, A["w_router_group"][0], NG, tokens_to(k, lg))
        gemm(k, "rt_e", k.hT, 8, A["w_router_expert"][0], NG * NE, tokens_to(k, le))

        def first(dve, after, x, best, mask, n):
            for t in range(NT):
                after(dve.tensor_scalar(mask[:, t, :], x[:, t, :], best[:, t:t + 1], None, ALU.is_equal))
                after(dve.tensor_tensor_scan(cum[:, t, :n], k.ones[:, :n], mask[:, t, :], 0.0, ALU.mult, ALU.add))
                after(dve.scalar_tensor_tensor(mask[:, t, :], cum[:, t, :n], 1.0, mask[:, t, :],
                                               ALU.is_equal, ALU.mult))

        def choose(dve, after):
            after(dve.tensor_tensor(lg[:], lg[:], bg[:].unsqueeze(1).to_broadcast([P, NT, NG]), ALU.add))
            after(dve.tensor_tensor(le[:], le[:], be[:].unsqueeze(1).to_broadcast([P, NT, NG * NE]), ALU.add))
            after(dve.tensor_reduce(mg[:], lg[:], AX.X, ALU.max))
            first(dve, after, lg, mg, pick, NG)
            after(dve.tensor_tensor(ex[:], lg[:], mg[:].unsqueeze(2).to_broadcast([P, NT, NG]), ALU.subtract))
            for g in range(NG):
                for t in range(NT):
                    lt, pt = le[:, t, g * NE:(g + 1) * NE], pick[:, t, g:g + 1]
                    if g == 0:
                        op = dve.tensor_scalar(mine[:, t, :], lt, pt, None, ALU.mult)
                    else:
                        op = dve.scalar_tensor_tensor(mine[:, t, :], lt, pt, mine[:, t, :], ALU.mult, ALU.add)
                after(op)
            after(dve.tensor_reduce(m1[:], mine[:], AX.X, ALU.max))
            first(dve, after, mine, m1, one, NE)
            after(dve.scalar_tensor_tensor(mine[:], one[:], NEG, mine[:], ALU.mult, ALU.add))
            after(dve.tensor_reduce(m2[:], mine[:], AX.X, ALU.max))
            first(dve, after, mine, m2, two, NE)
            after(dve.tensor_tensor(d2[:], m2[:], m1[:], ALU.subtract))
        on_vector(k, "rt_choose", choose)

        def exps(act, after):
            act.activation(ex[:], ex[:], ACT.Exp)
            act.activation(d2[:], d2[:], ACT.Exp)
        on_scalar(k, "rt_exp", exps)

        def positions(pe):
            for t in range(NT):
                for r in range(t + 1):
                    pe.matmul(ps[:, 0, t * NG:(t + 1) * NG], k.upto[:] if r == t else k.ones[:], pick[:, r, :],
                              start=r == 0, stop=r == t)
                pe.matmul(ps[:, 1, :NG], k.ones[:], pick[:, t, :], start=t == 0, stop=t == NT - 1)
        on_tensor(k, "rt_pos", positions)
        on_gpsimd(k, "rt_slots", lambda pool, after: pool.iota(
            slots[:], pattern=[[1, P]], base=0, channel_multiplier=0, allow_small_or_imprecise_dtypes=True))

        def weights(dve, after):
            after(dve.tensor_reduce(zg[:], ex[:], AX.X, ALU.add))
            after(dve.scalar_tensor_tensor(w1[:], d2[:], 1.0, zg[:], ALU.add, ALU.mult))
            after(dve.reciprocal(w1[:], w1[:]))
            after(dve.tensor_tensor(w2[:], w1[:], d2[:], ALU.mult))
            by = lambda x: x[:].unsqueeze(2).to_broadcast([P, NT, NE])
            after(dve.tensor_tensor(one[:], one[:], by(w1), ALU.mult))
            after(dve.tensor_tensor(two[:], two[:], by(w2), ALU.mult))
            after(dve.tensor_tensor(one[:], one[:], two[:], ALU.add))
            after(dve.tensor_tensor(ex[:], ps[:, 0, :NT * NG].rearrange("p (t g) -> p t g", t=NT), pick[:], ALU.mult))
            after(dve.tensor_reduce(rank[:], ex[:], AX.X, ALU.add))
            after(dve.tensor_scalar(rank[:], rank[:], -1.0, None, ALU.add))
            after(dve.tensor_scalar(late[:], rank[:], -float(P), None, ALU.add))
            for t in range(NT):
                for j in range(NG):
                    dve.tensor_scalar(perm[:, t, j, :], slots[:], rank[:, t:t + 1], pick[:, t, j:j + 1],
                                      ALU.is_equal, ALU.mult)
                dve.tensor_scalar(perm[:, t, NG, :], slots[:], late[:, t:t + 1], None, ALU.is_equal)
            after(dve.tensor_scalar(count[:], ps[:, 1, :NG], float(P), None, ALU.is_gt))
            after(dve.tensor_reduce(fl[:, 0:1], count[:], AX.X, ALU.add))
            after(dve.tensor_tensor(count[:], count[:], slots[:, 0:NG], ALU.mult))
            after(dve.tensor_reduce(fl[:, 1:2], count[:], AX.X, ALU.add))
            after(dve.tensor_scalar(fl[:, 1:2], fl[:, 1:2], float(NE), None, ALU.mult))
            dve.tensor_copy(flags[:], fl[:])
        on_vector(k, "rt_weights", weights)

        def turn(pe):
            for j in range(NG + 1):
                for t in range(NT):
                    pe.transpose(ps[:, j // 2, j % 2 * T + t * P:j % 2 * T + (t + 1) * P], perm[:, t, j, :], k.ident[:])
                    pe.matmul(ps[:, 3, j * NE:(j + 1) * NE], perm[:, t, j, :], one[:, t, :],
                              start=t == 0, stop=t == NT - 1)
        on_tensor(k, "rt_turn", turn)
        on_vector(k, "rt_copy", lambda dve, after: [
            dve.tensor_copy(permT[:].rearrange("p j t -> p (j t)"),
                            ps[:, 0:3, :].rearrange("p b n -> p (b n)")[:, :(NG + 1) * T]),
            dve.tensor_copy(fac[:].rearrange("p j e -> p (j e)"), ps[:, 3, :(NG + 1) * NE])])
        with Stage(nc, "rt_gather") as st:
            filled, drained = [[st.sem(f"{n}{i}") for i in range(2)] for n in ("filled", "drained")]
            block = st.block()
            parts = [(j, q) for j in range(NG + 1) for q in range(2)]

            @block.tensor
            def _(pe):
                for n, (j, q) in enumerate(parts):
                    if n >= 8:
                        pe.wait_ge(drained[n % 2], (n - 8) // 2 + 1)
                    for i in range(4):
                        kt = 4 * q + i
                        for t in range(NT):
                            last = pe.matmul(ps[:, n % 8, i * P:(i + 1) * P], h[:, t, kt * P:(kt + 1) * P],
                                             perm[:, t, j, :], start=t == 0, stop=t == NT - 1)
                    last.then_inc(filled[n % 2], 1)

            def drain(eng, odd):
                for n, (j, q) in enumerate(parts):
                    if n % 2 == odd:
                        eng.wait_ge(filled[odd], n // 2 + 1)
                        copier(nc, eng)(hg[:, j, 4 * q:4 * q + 4, :].rearrange("p k s -> p (k s)"),
                                        ps[:, n % 8, :]).then_inc(drained[odd], 1)

            @block.scalar
            def _(act):
                drain(act, 0)

            @block.vector
            def _(dve):
                drain(dve, 1)


def experts(k, name, A, tiles, fac, hg, sums, ada=None, flags=None):
    nc, NT, ps = k.nc, k.NT, k.ps
    U, FT, NE, HB = 2, 2, 8, 256
    wg, wu, wd = (A[f"w_expert_{n}"][0] for n in ("gate", "up", "down"))
    W = k.wring[:].rearrange("p a b -> p (a b)")[:, :U * 6144].rearrange("p (u n) -> p u n", u=U)
    gate = lambda u: W[:, u, 0:2048].rearrange("p (k n) -> p k n", k=8)
    up = lambda u: W[:, u, 2048:4096].rearrange("p (k n) -> p k n", k=8)
    down = lambda u: W[:, u, 4096:6144].rearrange("p (f n) -> p f n", f=FT)
    with Stage(nc, name) as st:
        silu = st.sb("silu", [P, U, HB])
        prod = st.sb("prod", [P, U, HB])
        hidT = st.sb("hidT", [P, U, FT, P])
        landed_in = [st.sem(f"landed_in{u}") for u in range(U)]
        landed_out = [st.sem(f"landed_out{u}") for u in range(U)]
        filled_g = [st.sem(f"filled_g{u}") for u in range(U)]
        filled = [st.sem(f"filled{u}") for u in range(U)]
        silued = [st.sem(f"silued{u}") for u in range(U)]
        made = [st.sem(f"made{u}") for u in range(U)]
        turned = [st.sem(f"turned{u}") for u in range(U)]
        copied = [st.sem(f"copied{u}") for u in range(U)]
        applied = [st.sem(f"applied{u}") for u in range(U)]
        summed, kept = st.sem("summed"), st.sem("kept")
        if ada:
            aw = st.sb("ada", [P, 2, 1536])
            ada_landed, ada_base = k.ada_landed, k.ada_base
            k.ada_base += 256
            ada_added = st.sem("ada_added")
            ada_w, cond, ada_sums = ada
        block = st.block()

        def guarded(eng, body):
            if flags is None:
                body(0)
                return
            any_late = eng.value_load(flags[0:1, 0:1], min_val=0, max_val=1)
            base = eng.value_load(flags[0:1, 1:2], min_val=0, max_val=24) if eng is nc.sync else 0
            with eng.If(any_late > 0):
                body(base)

        @block.sync
        def _(sp):
            def fetch(e, n, u, first):
                one = bass.ds(e, 1)
                flat = lambda x: x.rearrange("a k n -> (a k) n")
                if not first:
                    sp.wait_ge(filled[u], n)
                sp.dma_start(gate(u), flat(wg[one, :, u * HB:(u + 1) * HB]).rearrange("(k p) n -> p k n", p=P)
                             ).then_inc(landed_in[u], 16)
                sp.dma_start(up(u), flat(wu[one, :, u * HB:(u + 1) * HB]).rearrange("(k p) n -> p k n", p=P)
                             ).then_inc(landed_in[u], 16)
                if not first:
                    sp.wait_ge(applied[u], n)
                sp.dma_start(down(u), flat(wd[one, u * HB:(u + 1) * HB, :]).rearrange("(f p) n -> p f n", p=P)
                             ).then_inc(landed_out[u], 16)

            def program(base):
                for m, j in enumerate(tiles):
                    start = 1 if m == 0 else 0
                    if m == 0:
                        for u in range(U):
                            fetch(j * NE if flags is None else base, 0, u, True)
                    with sp.Fori(start, NE) as i:
                        for u in range(U):
                            fetch(i + (j * NE if flags is None else base), i + m * NE, u, False)
            guarded(sp, program)

        @block.gpsimd
        def _(pool):
            if not ada:
                return
            def fetch(i, n, j, b, first):
                if not first:
                    pool.wait_ge(ada_added, n - 1)
                pool.dma_start(aw[:, b, :], ada_w[j // 2][bass.ds(i * P, P), (j % 2) * 1536:(j % 2 + 1) * 1536]
                               ).then_inc(ada_landed[b], 16)
            for m, j in enumerate(tiles):
                if m == 0:
                    for b in range(2):
                        fetch(b, b, j, b, True)
                with pool.Fori(1 if m == 0 else 0, NE // 2) as i:
                    for b in range(2):
                        fetch(i * 2 + b, i * 2 + b + m * NE, j, b, False)

        @block.tensor
        def _(pe):
            def body(n, u, j, first):
                pe.wait_ge(landed_in[u], (n + 1) * 32)
                if not first:
                    pe.wait_ge(made[u], n)
                for bank, w, done in ((2 * u, gate(u), filled_g[u]), (2 * u + 1, up(u), filled[u])):
                    for kt in range(8):
                        last = pe.matmul(ps[:, bank, :HB], hg[:, j, kt, :], w[:, kt, :],
                                         start=kt == 0, stop=kt == 7)
                    last.then_inc(done, 1)

            def finish(n, u, first):
                pe.wait_ge(made[u], n + 1)
                if not first:
                    pe.wait_ge(copied[u], n)
                for f in range(FT):
                    last = pe.transpose(ps[:, 6 + u, f * P:(f + 1) * P], prod[:, u, f * P:(f + 1) * P], k.ident[:])
                last.then_inc(turned[u], 1)

            def apply(n, u, fresh):
                pe.wait_ge(landed_out[u], (n + 1) * 16)
                pe.wait_ge(copied[u], n + 1)
                for f in range(FT):
                    for c in range(2):
                        last = pe.matmul(ps[:, 4 + c, :], hidT[:, u, f, :], down(u)[:, f, c * BANK:(c + 1) * BANK],
                                         start=fresh and u == 0 and f == 0, stop=False, skip_group_check=True)
                last.then_inc(applied[u], 1)

            def expert(n, j, first, fresh):
                body(n, 0, j, first)
                body(n, 1, j, first)
                finish(n, 0, first)
                finish(n, 1, first)
                apply(n, 0, fresh)
                apply(n, 1, fresh)

            def program(base):
                for m, j in enumerate(tiles):
                    if m > 0:
                        pe.wait_ge(kept, m)
                    expert(m * NE, j, m == 0, True)
                    with pe.Fori(1, NE) as i:
                        expert(i + m * NE, j, False, False)
                    for c in range(2):
                        last = pe.matmul(ps[:, 4 + c, :], k.zero[:], k.X[:, 0, c * BANK:(c + 1) * BANK],
                                         start=False, stop=True, skip_group_check=True)
                    last.then_inc(summed, 1)
            guarded(pe, program)

        @block.scalar
        def _(act):
            def expert(n, j):
                for u in range(U):
                    act.wait_ge(filled_g[u], n + 1)
                    act.activation(silu[:, u, :], ps[:, 2 * u, :HB], ACT.Silu).then_inc(silued[u], 1)
                for u in range(U):
                    act.wait_ge(turned[u], n + 1)
                    act.copy(hidT[:, u].rearrange("p f s -> p (f s)"), ps[:, 6 + u, :FT * P]).then_inc(copied[u], 1)

            def program(base):
                for m, j in enumerate(tiles):
                    if m == 0:
                        expert(0, j)
                    with act.Fori(1 if m == 0 else 0, NE) as i:
                        expert(i + m * NE, j)
            guarded(act, program)

        @block.vector
        def _(dve):
            def expert(i, n, j):
                for u in range(U):
                    dve.wait_ge(filled[u], n + 1)
                    dve.wait_ge(silued[u], n + 1)
                    dve.scalar_tensor_tensor(prod[:, u, :], silu[:, u, :], fac[:, j, bass.ds(i, 1)],
                                             ps[:, 2 * u + 1, :HB], ALU.mult, ALU.mult).then_inc(made[u], 1)

            def pair(i2, m, j, first):
                for b in range(2):
                    i = i2 * 2 + b
                    expert(i, i + m * NE, j)
                    if ada:
                        dve.wait_ge(ada_landed[b], ada_base + (i2 + m * NE // 2 + 1) * 16)
                        if not (first and b == 0):
                            dve.wait_ge(ada_added, i + m * NE)
                        part = ada_sums[:, j // 2, (j % 2) * 1536:(j % 2 + 1) * 1536]
                        dve.scalar_tensor_tensor(part, aw[:, b, :], cond[:, bass.ds(i, 1)], part,
                                                 ALU.mult, ALU.add).then_inc(ada_added, 1)

            def program(base):
                for m, j in enumerate(tiles):
                    if m == 0:
                        pair(0, m, j, True)
                    with dve.Fori(1 if m == 0 else 0, NE // 2) as i2:
                        pair(i2, m, j, False)
                    dve.wait_ge(summed, m + 1)
                    dve.tensor_copy(sums[:, j, :], ps[:, 4:6, :].rearrange("p c n -> p (c n)")).then_inc(kept, 1)
            guarded(dve, program)


def scatter(k, permT, sums, tiles):
    NT, ps = k.NT, k.ps

    def back(pe):
        for t in range(NT):
            for c in range(2):
                for j in range(tiles):
                    pe.matmul(ps[:, 2 * t + c, :], permT[:, j, t * P:(t + 1) * P], sums[:, j, c * BANK:(c + 1) * BANK],
                              start=j == 0, stop=j == tiles - 1)
    on_tensor(k, "scatter", back)
    on_vector(k, "scatter_add", lambda dve, after: dve.tensor_tensor(
        k.X[:].rearrange("p t n -> p (t n)"), k.X[:].rearrange("p t n -> p (t n)"),
        ps[:, 0:4, :].rearrange("p b n -> p (b n)"), ALU.add))


def hybrid_block(k, A, masks, scratch):
    nc, NT, T = k.nc, k.NT, k.T
    with ExitStack() as own:
        sb = lambda name, shape: own.enter_context(nc.sbuf_tensor("fb_" + name, shape, F32))
        gain = sb("gain", [P, 8])
        load(k, "fb_load", [(k.X[:], A["x"][0].rearrange("(t p) n -> p t n", p=P)),
                            (gain[:], column(A["norm_mix"][0])), (k.c[:], column(A["c_2"][0]))])
        on_scalar(k, "fb_cond", lambda act, after: act.activation(k.c[:], k.c[:], ACT.Silu))
        y = sb("y", [P, NT, 512])
        yT = [sb(f"yT{r}", [P, 4, T]) for r in range(3)]
        with nc.sbuf_tensor("fb_h", [P, NT, 1024], F32) as h:
            rms_rows(k, "fb_rms", k.X[:], h[:])
            transpose_in(k, "fb_hT", h, k.hT, scale=gain[:])
        short_conv(k, A, yT[0])
        sparse_attention(k, A, scratch, y, None)
        transpose_in(k, "fb_yn", y, yT[1], 4)
        gated_delta(k, A, masks, y)
        transpose_in(k, "fb_yg", y, yT[2], 4)
        merge_branches(k, A, yT)


def for_modulation(k, ctx):
    sb = lambda name, shape: ctx.enter_context(k.nc.sbuf_tensor(name, shape, F32))
    k.ada = sb("ada", [P, 2, 3072])
    k.ada_landed = [k.nc.alloc_semaphore(f"ada_landed{b}") for b in range(2)]
    k.ada_base = 0
    k.mod = sb("mod", [P, 3072])


def moe_block(k, A):
    nc, NT, T = k.nc, k.NT, k.T
    with ExitStack() as own:
        sb = lambda name, shape, dt=F32: own.enter_context(nc.sbuf_tensor("moe_" + name, shape, dt))
        perm, permT = sb("perm", [P, NT, 5, P]), sb("permT", [P, 5, T])
        fac, hg, sums = sb("fac", [P, 5, 8]), sb("hg", [P, 5, 8, P]), sb("sums", [P, 5, 1024])
        flags, pick, one = sb("flags", [P, 2], I32), sb("pick", [P, NT, 4]), sb("one", [P, NT, 8])
        with nc.sbuf_tensor("moe_h", [P, NT, 1024], F32) as h, nc.sbuf_tensor("moe_gain", [P, 1024], F32) as gain:
            load(k, "moe_load", [(gain[:], rows(A["norm_ffn"][0]))])
            rms_rows(k, "moe_rms", k.X[:], h[:], gain[:])
            transpose_in(k, "moe_hT", h, k.hT)
            route(k, A, h, one, pick, perm, permT, fac, hg, flags)
        on_vector(k, "moe_zero", lambda dve, after: [dve.memset(sums[:, 4, :], 0.0), dve.memset(k.ada[:], 0.0)])
        experts(k, "moe", A, [0, 1, 2, 3], fac, hg, sums,
                ada=[[A["ada_w_2"][0, s] for s in range(2)], k.c, k.ada])
        experts(k, "late", A, [4], fac, hg, sums, flags=flags)
        scatter(k, permT, sums, 5)


ALPHA = 8 ** 0.25
ROPE_THETA = 500000.0


def modulation(k, name, site, bias):
    nc, ps = k.nc, k.ps
    N = 6
    with Stage(nc, name) as st:
        biased, filled = st.sem("biased"), st.sem("filled")
        block = st.block()

        @block.sync
        def _(sp):
            sp.dma_start(k.mod[:], rows(bias)).then_inc(biased, 16)

        @block.tensor
        def _(pe):
            for c in range(N):
                pe.matmul(ps[:, c, :], k.ones[:], k.ada[:, site, c * BANK:(c + 1) * BANK],
                          start=True, stop=True).then_inc(filled, 1)

        @block.vector
        def _(dve):
            dve.wait_ge(biased, 16)
            for c in range(N):
                dve.wait_ge(filled, c + 1)
                m = k.mod[:, c * BANK:(c + 1) * BANK]
                dve.scalar_tensor_tensor(m, ps[:, c, :], 0.0 if c < 2 else 1.0, m, ALU.add, ALU.add)


def modulate(k, name, h):
    shape = [P, k.NT, 1024]
    row = lambda i: k.mod[:, i * 1024:(i + 1) * 1024].unsqueeze(1).to_broadcast(shape)

    def body(dve, after):
        after(dve.tensor_tensor(h[:], k.X[:], row(1), ALU.mult))
        dve.tensor_tensor(h[:], h[:], row(0), ALU.add)
    on_vector(k, name + "_mod", body)
    transpose_in(k, name + "_hT", h, k.hT)


def residual_norm(k, name, y, g, b):
    nc, NT, X = k.nc, k.NT, k.X
    shape = [P, NT, 1024]
    with Stage(nc, name) as st:
        gr, br = st.sb("g", [P, 1024]), st.sb("b", [P, 1024])
        mean, var = st.sb("mean", [P, NT]), st.sb("var", [P, NT])
        landed, step, summed, rooted = st.sem("landed"), st.sem("step"), st.sem("summed"), st.sem("rooted")
        block = st.block()
        row = lambda r: r.unsqueeze(1).to_broadcast(shape)

        @block.sync
        def _(sp):
            sp.dma_start(gr[:], rows(g)).then_inc(landed, 16)
            sp.dma_start(br[:], rows(b)).then_inc(landed, 16)

        @block.vector
        def _(dve):
            after = Chain(dve, step)
            after(dve.tensor_tensor(y[:], y[:], row(k.mod[:, 2048:3072]), ALU.mult))
            after(dve.scalar_tensor_tensor(X[:], X[:], ALPHA, y[:], ALU.mult, ALU.add))
            after(dve.tensor_reduce(mean[:], X[:], AX.X, ALU.add))
            after(dve.tensor_scalar(mean[:], mean[:], 1.0 / 1024, None, ALU.mult))
            for t in range(NT):
                op = dve.tensor_scalar(X[:, t], X[:, t], mean[:, t:t + 1], None, ALU.subtract)
            after(op)
            after(dve.tensor_tensor(y[:], X[:], X[:], ALU.mult))
            after(dve.tensor_reduce(var[:], y[:], AX.X, ALU.add))
            dve.tensor_scalar(var[:], var[:], 1.0 / 1024, 1e-5, ALU.mult, ALU.add).then_inc(summed, 1)
            dve.wait_ge(landed, 32)
            dve.wait_ge(rooted, 1)
            for t in range(NT):
                op = dve.scalar_tensor_tensor(X[:, t], X[:, t], var[:, t:t + 1], gr[:], ALU.mult, ALU.mult)
            after(op)
            dve.tensor_tensor(X[:], X[:], row(br[:]), ALU.add)

        @block.gpsimd
        def _(pool):
            pool.wait_ge(summed, 1)
            pool.tensor_tensor(var[:], var[:], k.nhalf[:, :NT], ALU.pow).then_inc(rooted, 1)


def mlstm(k, A, y):
    nc, T, NT, ps = k.nc, k.T, k.NT, k.ps
    H, DK, DV = 4, 128, 256
    with ExitStack() as own:
        sb = lambda name, shape: own.enter_context(nc.sbuf_tensor("ml_" + name, shape, F32))
        qkT, VO = sb("qkT", [P, 8, T]), sb("VO", [P, NT, 2056])
        bg, norm = sb("bg", [P, 8]), sb("norm", [P, 1024])
        load(k, "ml_load", [(bg[:], rows(A["mlstm_b_gate_2"][0])), (norm[:], rows(A["mlstm_norm_2"][0]))])
        w = A["mlstm_w_in_2"][0]
        gemm(k, "ml_qk", k.hT, 8, w[:, 0:1024], 1024, features_to(k, qkT), feature_major=True)
        gemm(k, "ml_vo", k.hT, 8, w[:, 1024:3080], 2056, tokens_to(k, VO))
        gt, ab, nf = sb("gt", [P, NT, 8]), sb("ab", [P, NT, H]), sb("nf", [P, NT, H])
        rep = sb("rep", [P, NT, 2, H, P])

        def pre(dve, after):
            after(dve.tensor_tensor(gt[:], VO[:, :, 2048:2056], bg[:].unsqueeze(1).to_broadcast([P, NT, 8]), ALU.add))
            after(dve.tensor_scalar(ab[:], gt[:, :, 4:8], -1.0, None, ALU.mult))
            after(dve.tensor_tensor(ab[:], ab[:], gt[:, :, 4:8], ALU.min))
        on_vector(k, "ml_p1", pre)

        def soft(act, after):
            after(act.activation(ab[:], ab[:], ACT.Exp))
            after(act.activation(ab[:], ab[:], ACT.Ln, bias=1.0))
            act.activation(VO[:, :, 1024:2048], VO[:, :, 1024:2048], ACT.Sigmoid)
        on_scalar(k, "ml_p2", soft)

        def repeat(dve, after):
            after(dve.tensor_scalar(nf[:], gt[:, :, 4:8], 0.0, None, ALU.min))
            after(dve.tensor_tensor(nf[:], ab[:], nf[:], ALU.subtract))
            dve.tensor_copy(rep[:, :, 0], gt[:, :, 0:4].unsqueeze(3).to_broadcast([P, NT, H, P]))
            dve.tensor_copy(rep[:, :, 1], nf[:].unsqueeze(3).to_broadcast([P, NT, H, P]))
        on_vector(k, "ml_p3", repeat)

        def rows_of_R(pe):
            for h in range(H):
                for t in range(NT):
                    out = ps[:, h // 2, (h % 2) * T + t * P:(h % 2) * T + (t + 1) * P]
                    pe.matmul(out, rep[:, t, 0, h], k.ident[:], start=True, stop=False)
                    for r in range(t):
                        pe.matmul(out, rep[:, r, 1, h], k.ones[:], start=False, stop=False)
                    pe.matmul(out, rep[:, t, 1, h], k.upto[:], start=False, stop=True)
            for t in range(NT):
                for r in range(t + 1):
                    pe.matmul(ps[:, 2, t * H:(t + 1) * H], k.upto[:] if r == t else k.ones[:], nf[:, r, :],
                              start=r == 0, stop=r == t)
        on_tensor(k, "ml_R", rows_of_R)
        W, c, em = sb("W", [P, NT, H, T]), sb("c", [P, NT, H]), sb("em", [P, NT, H])

        def weights(dve, after):
            for t in range(NT):
                after(dve.tensor_tensor(W[:, t], ps[:, 0:2, :].rearrange("p b (h s) -> p (b h) s", s=T),
                                        k.causal[:, t, :].unsqueeze(1).to_broadcast([P, H, T]), ALU.add))
            after(dve.tensor_reduce(c[:], W[:], AX.X, ALU.max))
            after(dve.tensor_scalar(c[:], c[:], 0.0, None, ALU.max))
            dve.tensor_tensor(W[:], W[:], c[:].unsqueeze(3).to_broadcast([P, NT, H, T]), ALU.subtract)
            dve.tensor_tensor(em[:], ps[:, 2, :NT * H].rearrange("p (t h) -> p t h", t=NT), c[:], ALU.subtract)
        on_vector(k, "ml_W", weights)
        on_scalar(k, "ml_E", lambda act, after: [act.activation(W[:], W[:], ACT.Exp),
                                                 act.activation(em[:], em[:], ACT.Exp)])
        den, PT = sb("den", [P, NT, H]), sb("PT", [P, H, T])
        for t in range(NT):
            n = (t + 1) * P
            on_tensor(k, f"ml_s{t}", lambda pe, t=t, n=n: [pe.matmul(
                ps[:, h // 2, (h % 2) * T:(h % 2) * T + n], qkT[:, h, t * P:(t + 1) * P], qkT[:, 4 + h, :n],
                start=True, stop=True) for h in range(H)])

            def weigh(dve, after, t=t, n=n):
                s = W[:, t, :, :n]
                after(dve.scalar_tensor_tensor(s, ps[:, 0:2, :].rearrange("p b (h s) -> p (b h) s", s=T)[:, :, :n],
                                               DK ** -0.5, s, ALU.mult, ALU.mult))
                after(dve.tensor_reduce(den[:, t], s, AX.X, ALU.add))
                after(dve.tensor_scalar(c[:, t], den[:, t], -1.0, None, ALU.mult))
                after(dve.tensor_tensor(den[:, t], den[:, t], c[:, t], ALU.max))
                after(dve.tensor_tensor(den[:, t], den[:, t], em[:, t], ALU.max))
                after(dve.reciprocal(den[:, t], den[:, t]))
            on_vector(k, f"ml_w{t}", weigh)
            on_tensor(k, f"ml_t{t}", lambda pe, t=t: [pe.transpose(
                ps[:, h // 2, (h % 2) * T + r * P:(h % 2) * T + (r + 1) * P], W[:, t, h, r * P:(r + 1) * P],
                k.ident[:]) for h in range(H) for r in range(t + 1)])
            on_vector(k, f"ml_c{t}", lambda dve, after, n=n: dve.tensor_copy(
                PT[:, :, :n], ps[:, 0:2, :].rearrange("p b (h s) -> p (b h) s", s=T)[:, :, :n]))

            def apply(pe, t=t):
                for h in range(H):
                    for r in range(t + 1):
                        pe.matmul(ps[:, 2 + h // 2, (h % 2) * DV:(h % 2 + 1) * DV], PT[:, h, r * P:(r + 1) * P],
                                  VO[:, r, h * DV:(h + 1) * DV], start=r == 0, stop=r == t)
            on_tensor(k, f"ml_a{t}", apply)
            on_vector(k, f"ml_o{t}", lambda dve, after, t=t: dve.tensor_tensor(
                y[:, t].rearrange("p (h d) -> p h d", h=H), ps[:, 2:4, :].rearrange("p b (h d) -> p (b h) d", d=DV),
                den[:, t].unsqueeze(2).to_broadcast([P, H, DV]), ALU.mult))
        rms_rows(k, "ml_n", y[:], y[:], groups=H)

        def gated(dve, after):
            after(dve.tensor_tensor(y[:], y[:], norm[:].unsqueeze(1).to_broadcast([P, NT, 1024]), ALU.mult))
            dve.tensor_tensor(y[:], y[:], VO[:, :, 1024:2048], ALU.mult)
        on_vector(k, "ml_y", gated)


def rope_tables(k, positions, cos, sin):
    nc, NT, half = k.nc, k.NT, 8
    with ExitStack() as own:
        sb = lambda name, shape, dt=F32: own.enter_context(nc.sbuf_tensor("rp_" + name, shape, dt))
        pi, pf = sb("pi", [P, NT], I32), sb("pf", [P, NT])
        ang, turns, whole = sb("ang", [P, NT, half]), sb("turns", [P, NT, half]), sb("whole", [P, NT, half], I32)
        load(k, "rp_load", [(pi[:], positions.rearrange("(t p) -> p t", p=P))])
        c1 = 6.28125
        c2 = float(np.float32(np.round((2 * math.pi - c1) * 2 ** 20) / 2 ** 20))
        c3 = 2 * math.pi - c1 - c2

        def body(dve, after):
            after(dve.tensor_copy(pf[:], pi[:]))
            for i in range(half):
                inv = float(np.float32(ROPE_THETA ** (-i * 2.0 / 16)))
                op = dve.tensor_scalar(ang[:, :, i], pf[:], inv, None, ALU.mult)
            after(op)
            for dst, quarter in ((cos, 0.25), (sin, 0.0)):
                after(dve.tensor_scalar(turns[:], ang[:], 1 / (2 * math.pi), quarter, ALU.mult, ALU.add))
                after(dve.tensor_copy(whole[:], turns[:]))
                after(dve.tensor_copy(turns[:], whole[:]))
                after(dve.scalar_tensor_tensor(dst[:], turns[:], -c1, ang[:], ALU.mult, ALU.add))
                after(dve.scalar_tensor_tensor(dst[:], turns[:], -c2, dst[:], ALU.mult, ALU.add))
                after(dve.scalar_tensor_tensor(dst[:], turns[:], -c3, dst[:], ALU.mult, ALU.add))
                after(dve.tensor_scalar(dst[:], dst[:], quarter * 2 * math.pi, math.pi, ALU.add, ALU.min))
                after(dve.tensor_scalar(dst[:], dst[:], -math.pi, None, ALU.max))
        on_vector(k, "rp_ang", body)
        on_scalar(k, "rp_sin", lambda act, after: [act.activation(cos[:], cos[:], ACT.Sin),
                                                   act.activation(sin[:], sin[:], ACT.Sin)])


def rotate(k, name, x, heads, cos, sin, tmp):
    shape = [P, k.NT, heads, 8]
    v = x.rearrange("p t (h d) -> p t h d", h=heads)
    x1, x2 = v[:, :, :, 0:8], v[:, :, :, 8:16]
    c, s = (z[:].unsqueeze(2).to_broadcast(shape) for z in (cos, sin))

    def body(dve, after):
        dve.tensor_tensor(tmp[:, 0], x1, c, ALU.mult)
        dve.tensor_tensor(tmp[:, 1], x2, s, ALU.mult)
        dve.tensor_tensor(tmp[:, 2], x2, c, ALU.mult)
        after(dve.tensor_tensor(tmp[:, 3], x1, s, ALU.mult))
        dve.tensor_tensor(x1, tmp[:, 0], tmp[:, 1], ALU.subtract)
        dve.tensor_tensor(x2, tmp[:, 2], tmp[:, 3], ALU.add)
    on_vector(k, name, body)


def windowed(k, A, cos, sin, y):
    nc, T, NT = k.nc, k.T, k.NT
    H, G, D = 16, 2, 64
    with ExitStack() as own:
        sb = lambda name, shape: own.enter_context(nc.sbuf_tensor("wa_" + name, shape, F32))
        U, KD = sb("U", [P, NT, 1280]), sb("KD", [P, NT, G, 2, D])
        qT, kT = sb("qT", [P, 8, T]), sb("kT", [P, G, T])
        band, sinks, tmp = sb("band", [P, NT, T]), sb("sinks", [P, H]), sb("tmp", [P, 4, NT, 18, 8])
        load(k, "wa_load", [(sinks[:], rows(A["swa_sinks_2"][0]))])
        gemm(k, "wa_in", k.hT, 8, A["swa_w_in_2"][0], 1280, tokens_to(k, U))
        rotate(k, "wa_rope", U[:, :, 0:1152], 18, cos, sin, tmp)

        def mask(pool, after):
            for t in range(NT):
                pool.affine_select(out=band[:, t, :], in_=k.causal[:, t, :], compare_op=ALU.is_gt, fill=NEG,
                                   base=P - t * P, pattern=[[1, T]], channel_multiplier=-1)
        on_gpsimd(k, "wa_mask", mask)
        on_vector(k, "wa_twice", lambda dve, after: [dve.tensor_copy(
            KD[:, :, :, u, :], U[:, :, 1024:1152].rearrange("p t (g d) -> p t g d", g=G)) for u in range(2)])
        transpose_in(k, "wa_qT", U, qT, 8, factor=D ** -0.5)
        transpose_in(k, "wa_kT", None, kT, G, src_cols=lambda t, i: KD[:, t, i].rearrange("p u d -> p (u d)"))
        half = lambda h: slice((h % 2) * D, (h % 2 + 1) * D)
        attention(k, "wa_a", [(list(range(h, h + 4)), t) for t in range(NT) for h in range(0, H, 4)],
                  q_of=lambda h, t: qT[half(h), h // 2, t * P:(t + 1) * P],
                  k_of=lambda h, kt: kT[half(h), h // 8, kt * P:(kt + 1) * P],
                  v_of=lambda h, kt: U[:, kt, 1152 + (h // 8) * D:1152 + (h // 8 + 1) * D],
                  bias_of=lambda hs, t: band[:, t, :(t + 1) * P].unsqueeze(1).to_broadcast([P, 4, (t + 1) * P]),
                  out_of=lambda hs, t: y[:, t, hs[0] * D:(hs[-1] + 1) * D].rearrange("p (g d) -> p g d", d=D),
                  dv=D, sink_of=lambda hs: sinks[:, hs[0]:hs[-1] + 1])


def hgrn(k, A, masks, layer, y):
    nc, T, NT, ps = k.nc, k.T, k.NT, k.ps
    H, D = 8, 128
    LV = 8
    with ExitStack() as own:
        sb = lambda name, shape: own.enter_context(nc.sbuf_tensor("hg_" + name, shape, F32))
        QF, IG = sb("QF", [P, 16, T]), sb("IG", [P, NT, 2048])
        lo, norm = sb("lo", [P, 4, 8]), sb("norm", [P, 1024])
        lb, lc, mx = sb("lb", [P, 8]), sb("lc", [P, 8]), sb("mx", [P, 8])
        K, cf = sb("K", [P, H, T]), sb("cf", [P, H, T])
        E = sb("E", [P, 2, H, T])
        QE, KE = (k.wring[:, 2, i * H * T:(i + 1) * H * T].rearrange("p (h t) -> p h t", h=H) for i in range(2))
        aT, aX = sb("aT", [P, NT, H, P]), sb("aX", [P, H, P])
        load(k, "hg_load", [(lo[:, i, :], column(A["hgrn_lower_bounds_2"][i])) for i in range(4)]
             + [(norm[:], rows(A["hgrn_norm_2"][0]))])
        w = A["hgrn_w_in_2"][0]
        gemm(k, "hg_qf", k.hT, 8, w[:, 0:2048], 2048, features_to(k, QF), feature_major=True)
        gemm(k, "hg_ig", k.hT, 8, w[:, 2048:4096], 2048, tokens_to(k, IG))
        on_vector(k, "hg_l1", lambda dve, after: [
            after(dve.tensor_reduce(mx[:], lo[:].rearrange("p l i -> p i l"), AX.X, ALU.max)),
            after(dve.tensor_tensor(lo[:], lo[:], mx[:].unsqueeze(1).to_broadcast([P, 4, 8]), ALU.subtract))])
        on_scalar(k, "hg_l2", lambda act, after: [
            act.activation(lo[:], lo[:], ACT.Exp),
            act.activation(K[:], QF[:, 8:16, :], ACT.Exp, scale=-1.0)])
        Q = QF[:, 0:8, :]
        wide_ = lambda x: x[:].unsqueeze(2).to_broadcast([P, H, T])
        F = QF[:, 8:16, :]

        def gates(dve, after):
            after(dve.tensor_reduce(mx[:], lo[:].rearrange("p l i -> p i l"), AX.X, ALU.add))
            after(dve.reciprocal(mx[:], mx[:]))
            after(dve.tensor_reduce(lb[:], lo[:, 1:layer + 1].rearrange("p l i -> p i l"), AX.X, ALU.add))
            after(dve.tensor_tensor(lb[:], lb[:], mx[:], ALU.mult))
            after(dve.tensor_scalar(lc[:], lb[:], -1.0, 1.0, ALU.mult, ALU.add))
            after(dve.tensor_scalar(K[:], K[:], 1e30, None, ALU.min))
            after(dve.tensor_scalar(F, K[:], 1.0, None, ALU.add))
            after(dve.reciprocal(F, F))
            after(dve.tensor_tensor(F, F, wide_(lc), ALU.mult))
            after(dve.tensor_tensor(K[:], K[:], F, ALU.mult))
            after(dve.tensor_tensor(F, F, wide_(lb), ALU.add))
            after(dve.memset(aT[:], 0.0))
        on_vector(k, "hg_g", gates)
        on_scalar(k, "hg_ln", lambda act, after: act.activation(F, F, ACT.Ln))

        def running(dve, after):
            for h in range(H):
                dve.tensor_tensor_scan(cf[:, h, :], k.onesT[:], F[:, h, :], 0.0, ALU.mult, ALU.add)
        on_vector(k, "hg_cf", running)

        with Stage(nc, "hg_lv") as st:
            step, ready = st.sem("step"), st.sem("ready")
            spread, raised = st.sem("spread"), st.sem("raised")
            scaled, multiplied, taken = st.sem("scaled"), st.sem("multiplied"), st.sem("taken")
            block = st.block()

            def cut(x, v):
                b = 2 ** v
                z = x.rearrange("p h (n u j) -> p h n u j", u=2, j=b)
                return z[:, :, :, 0, :], z[:, :, :, 1, :]

            @block.vector
            def _(dve):
                def exponents(v):
                    b, n = 2 ** v, T // 2 ** (v + 1)
                    c0, c1 = cut(cf[:], v)
                    e0, e1 = cut(E[:, v % 2], v)
                    mid = c0[:, :, :, b - 1:b]
                    if n == 1:
                        c0, c1, e0, e1, mid = (z[:, :, 0, :] for z in (c0, c1, e0, e1, mid))
                        mid = mid.to_broadcast([P, H, b])
                    else:
                        mid = mid.to_broadcast([P, H, n, b])
                    dve.tensor_tensor(e0, mid, c0, ALU.subtract)
                    dve.tensor_tensor(e1, c1, mid, ALU.subtract).then_inc(spread, 1)

                exponents(0)
                for v in range(LV + 1):
                    if v + 1 < LV:
                        if v >= 1:
                            dve.wait_ge(scaled, v)
                        exponents(v + 1)
                    if v >= 1:
                        dve.wait_ge(multiplied, v)
                    if v < LV:
                        dve.wait_ge(raised, v + 1)
                        dve.tensor_tensor(QE, Q, E[:, v % 2], ALU.mult)
                        dve.tensor_tensor(KE, K[:], E[:, v % 2], ALU.mult).then_inc(scaled, 1)
                        dve.wait_ge(multiplied, v + 1)
                        if v < LV - 1:
                            dve.copy_predicated(
                                aT[:].rearrange("p t h c -> p (t h) c"),
                                masks[:, v, :].bitcast(mybir.dt.uint32).unsqueeze(1).to_broadcast([P, NT * H, P]),
                                ps[:, 0:4, :].rearrange("p b (h c) -> p (b h) c", c=P)).then_inc(taken, 1)
                        else:
                            dve.tensor_copy(aX[:].rearrange("p h c -> p (h c)"),
                                            ps[:, 0:2, :].rearrange("p b n -> p (b n)")).then_inc(taken, 1)
                        dve.wait_ge(taken, v + 1)
                    else:
                        dve.copy_predicated(
                            aT[:].rearrange("p t h c -> p (t h) c"),
                            k.ident[:].bitcast(mybir.dt.uint32).unsqueeze(1).to_broadcast([P, NT * H, P]),
                            ps[:, 4:8, :].rearrange("p b (h c) -> p (b h) c", c=P))

            @block.scalar
            def _(act):
                for v in range(LV):
                    act.wait_ge(spread, v + 1)
                    act.activation(E[:, v % 2], E[:, v % 2], ACT.Exp).then_inc(raised, 1)

            @block.tensor
            def _(pe):
                for v in range(LV):
                    pe.wait_ge(scaled, v + 1)
                    if v >= 1:
                        pe.wait_ge(taken, v)
                    for h in range(H):
                        if v < LV - 1:
                            for t in range(NT):
                                i = t * H + h
                                last = pe.matmul(ps[:, i // 4, i % 4 * P:(i % 4 + 1) * P],
                                                 KE[:, h, t * P:(t + 1) * P], QE[:, h, t * P:(t + 1) * P],
                                                 start=True, stop=True)
                        else:
                            last = pe.matmul(ps[:, h // 4, h % 4 * P:(h % 4 + 1) * P], KE[:, h, 0:P], QE[:, h, P:T],
                                             start=True, stop=True)
                    if v == LV - 1:
                        for h in range(H):
                            for t in range(NT):
                                i = t * H + h
                                last = pe.matmul(ps[:, 4 + i // 4, i % 4 * P:(i % 4 + 1) * P],
                                                 K[:, h, t * P:(t + 1) * P], Q[:, h, t * P:(t + 1) * P],
                                                 start=True, stop=True)
                    last.then_inc(multiplied, 1)

        def apply(pe):
            for h in range(H):
                v = lambda t: IG[:, t, h * D:(h + 1) * D]
                o = lambda t: ps[:, 2 * t + h // 4, h % 4 * D:(h % 4 + 1) * D]
                pe.matmul(o(0), aT[:, 0, h], v(0), start=True, stop=True)
                pe.matmul(o(1), aX[:, h], v(0), start=True, stop=False)
                pe.matmul(o(1), aT[:, 1, h], v(1), start=False, stop=True)
        on_tensor(k, "hg_pv", apply)
        on_scalar(k, "hg_silu", lambda act, after: [
            act.activation(IG[:, :, 1024:2048], IG[:, :, 1024:2048], ACT.Silu)])
        on_vector(k, "hg_o", lambda dve, after: dve.tensor_copy(
            y[:].rearrange("p t n -> p (t n)"), ps[:, 0:4, :].rearrange("p b n -> p (b n)")))
        rms_rows(k, "hg_n", y[:], y[:], groups=H)

        def gated(dve, after):
            after(dve.tensor_tensor(y[:], y[:], norm[:].unsqueeze(1).to_broadcast([P, NT, 1024]), ALU.mult))
            dve.tensor_tensor(y[:], y[:], IG[:, :, 1024:2048], ALU.mult)
        on_vector(k, "hg_y", gated)


def differential(k, A, cos, sin, layer, y):
    nc, T, NT = k.nc, k.T, k.NT
    H, D = 8, 64
    lam_init = 0.8 - 0.6 * math.exp(-0.3 * layer)
    with ExitStack() as own:
        sb = lambda name, shape: own.enter_context(nc.sbuf_tensor("df_" + name, shape, F32))
        U, qT, kT = sb("U", [P, NT, 3072]), sb("qT", [P, 8, T]), sb("kT", [P, 8, T])
        tmp, lv, gain = sb("tmp", [P, 4, NT, 32, 8]), sb("lv", [P, 4, D]), sb("gain", [P, 2 * D])
        pr, lam = sb("pr", [P, 2, D]), sb("lam", [P, 2])
        load(k, "df_load", [(lv[:], A["diff_lambda_2"][0].partition_broadcast(P)),
                            (gain[:], rows(A["diff_norm_2"][0]))])
        gemm(k, "df_in", k.hT, 8, A["diff_w_in_2"][0], 3072, tokens_to(k, U))
        rotate(k, "df_rope", U[:, :, 0:2048], 32, cos, sin, tmp)

        def dots(dve, after):
            dve.tensor_tensor(pr[:, 0], lv[:, 0], lv[:, 1], ALU.mult)
            after(dve.tensor_tensor(pr[:, 1], lv[:, 2], lv[:, 3], ALU.mult))
            after(dve.tensor_reduce(lam[:], pr[:], AX.X, ALU.add))
        on_vector(k, "df_l1", dots)
        on_scalar(k, "df_l2", lambda act, after: act.activation(lam[:], lam[:], ACT.Exp))

        def lam_of(dve, after):
            after(dve.tensor_tensor(lam[:, 0:1], lam[:, 1:2], lam[:, 0:1], ALU.subtract))
            after(dve.tensor_scalar(lam[:, 0:1], lam[:, 0:1], -lam_init, None, ALU.add))
        on_vector(k, "df_l3", lam_of)
        transpose_in(k, "df_qT", U, qT, 8, factor=D ** -0.5)
        transpose_in(k, "df_kT", U[:, :, 1024:2048], kT, 8)
        half = lambda h: slice((h % 2) * D, (h % 2 + 1) * D)
        attention(k, "df_a", [(list(range(h, h + 4)), t) for t in range(NT) for h in range(0, 2 * H, 4)],
                  q_of=lambda h, t: qT[half(h), h // 2, t * P:(t + 1) * P],
                  k_of=lambda h, kt: kT[half(h), h // 2, kt * P:(kt + 1) * P],
                  v_of=lambda h, kt: U[:, kt, 2048 + (h // 2) * 2 * D:2048 + (h // 2 + 1) * 2 * D],
                  bias_of=lambda hs, t: k.causal[:, t, :(t + 1) * P].unsqueeze(1).to_broadcast([P, 4, (t + 1) * P]),
                  out_of=lambda hs, t: y[:, t, hs[0] * D:(hs[-1] + 1) * D].rearrange("p (g d) -> p g d", d=2 * D),
                  dv=2 * D, minus=lambda g: lam[:, 0:1])
        rms_rows(k, "df_n", y[:], y[:], gain[:], groups=H, factor=1.0 - lam_init)


def second_block(k, A, masks):
    nc, T, NT = k.nc, k.T, k.NT
    with ExitStack() as own:
        sb = lambda name, shape: own.enter_context(nc.sbuf_tensor("sb_" + name, shape, F32))
        k.onesT = sb("onesT", [P, T])
        k.causal = sb("causal", [P, NT, T])
        cos, sin = sb("cos", [P, NT, 8]), sb("sin", [P, NT, 8])
        y = sb("y", [P, NT, 1024])
        on_vector(k, "sb_ones", lambda dve, after: dve.memset(k.onesT[:], 1.0))

        def mask(pool, after):
            after(pool.memset(k.causal[:], 0.0))
            for t in range(NT):
                pool.affine_select(out=k.causal[:, t, :], in_=k.causal[:, t, :], compare_op=ALU.is_ge, fill=NEG,
                                   base=t * P, pattern=[[-1, T]], channel_multiplier=1)
        on_gpsimd(k, "sb_causal", mask)
        rope_tables(k, A["positions_2"][0], cos, sin)
        mixers = [lambda: mlstm(k, A, y), lambda: windowed(k, A, cos, sin, y),
                  lambda: hgrn(k, A, masks, 2, y), lambda: differential(k, A, cos, sin, 3, y)]
        outs = ["mlstm_w_out_2", "swa_w_out_2", "hgrn_w_out_2", "diff_w_out_2"]
        for i in range(4):
            modulation(k, f"l{i}_ada0", 0, A["ada_b_2"][i, 0])
            modulate(k, f"l{i}_m0", y)
            mixers[i]()
            transpose_in(k, f"l{i}_yT", y, k.hT)
            gemm(k, f"l{i}_out", k.hT, 8, A[outs[i]][0], 1024, tokens_to(k, y))
            residual_norm(k, f"l{i}_n0", y, A["ln_g_2"][i, 0], A["ln_b_2"][i, 0])
            if k.stop == (i, 0):
                return
            modulation(k, f"l{i}_ada1", 1, A["ada_b_2"][i, 1])
            modulate(k, f"l{i}_m1", y)
            swiglu(k, f"l{i}_ffn", A["ffn_w_in_2"][i], A["ffn_w_out_2"][i], 2816, y,
                   ada=[A["ada_w_2"][i + 1, s] for s in range(2)] if i < 3 else None)
            residual_norm(k, f"l{i}_n1", y, A["ln_g_2"][i, 1], A["ln_b_2"][i, 1])
            if k.stop == (i, 1):
                return


def program(nc, A, out):
    T = A["x"].shape[1]
    scratch = nc.dram_tensor("compress_rows", [2, 2, T, 64], F32, kind="Internal").ap()
    with ExitStack() as ctx:
        k = persistent(nc, ctx, T)
        masks = ctx.enter_context(nc.sbuf_tensor("masks", [P, 7, P], F32))
        level_masks(k, masks)
        hybrid_block(k, A, masks, scratch)
        for_modulation(k, ctx)
        moe_block(k, A)
        second_block(k, A, masks)
        dump(k, "store", [(out[0].rearrange("(t p) n -> p t n", p=P), k.X[:])])


def kernel(**inputs):
    import numpy as _np
    import concourse.bacc as _bacc
    from concourse import mybir as _mybir
    from concourse.bass_utils import run_bass_kernel_spmd as _run

    nc = _bacc.Bacc("TRN2", target_bir_lowering=False, num_devices=1)
    arrays, aps = {}, {}
    for name, value in inputs.items():
        a = _np.ascontiguousarray(value)
        arrays[f"in_{name}_dram"] = a
        aps[name] = nc.dram_tensor(f"in_{name}_dram", a.shape, _mybir.dt.from_np(a.dtype), kind="ExternalInput").ap()
    shape = tuple(inputs["x"].shape)
    out = nc.dram_tensor("out_0_dram", shape, _mybir.dt.float32, kind="ExternalOutput").ap()
    program(nc, aps, out)
    r = _run(nc, [arrays], core_ids=[0])
    return r.results[0]["out_0_dram"]
```

```python
import math
from contextlib import ExitStack

import numpy as np

import concourse.bass as bass
from concourse import mybir

F32 = mybir.dt.float32
F32R = mybir.dt.float32r
I32 = mybir.dt.int32
ALU = mybir.AluOpType
ACT = mybir.ActivationFunctionType
AX = mybir.AxisListType
P = 128
BANK = 512
NEG = -1e30
RING, UNIT = 6, 2048


class Kept:
    pass


class Chain:

    def __init__(self, eng, sem):
        self.eng, self.sem, self.n = eng, sem, 0

    def __call__(self, ins):
        self.n += 1
        ins.then_inc(self.sem, 1)
        self.eng.wait_ge(self.sem, self.n)


class Stage:

    def __init__(self, nc, name):
        self.nc, self.name, self.ctx, self.sems = nc, name, ExitStack(), []

    def __enter__(self):
        self.ctx.__enter__()
        return self

    def __exit__(self, *a):
        out = self.ctx.__exit__(*a)
        if a[0] is None and self.sems:
            for sem in self.sems:
                self.nc.gpsimd.sem_clear(sem)
                self.nc.release_semaphore(sem)
        return out

    def sem(self, name):
        self.sems.append(self.nc.alloc_semaphore(f"{self.name}_{name}"))
        return self.sems[-1]

    def sb(self, name, shape, dt=F32):
        return self.ctx.enter_context(self.nc.sbuf_tensor(f"{self.name}_{name}", shape, dt))

    def block(self):
        return self.ctx.enter_context(self.nc.Block())


def persistent(nc, ctx, T):
    k = Kept()
    k.nc, k.T, k.NT, k.stop = nc, T, T // P, None
    sb = lambda name, shape: ctx.enter_context(nc.sbuf_tensor(name, shape, F32))
    k.X = sb("X", [P, k.NT, 1024])
    k.hT = sb("hT", [P, 8, T])
    k.ident = sb("ident", [P, P])
    k.ones = sb("ones", [P, P])
    k.zero = sb("zero", [P, P])
    k.upto = sb("upto", [P, P])
    k.nhalf = sb("nhalf", [P, 64])
    k.wring = sb("wring", [P, 3, 4096])
    k.ring = k.wring[:].rearrange("p a (b n) -> p (a b) n", n=UNIT)
    k.ring_landed = [nc.alloc_semaphore(f"ring_landed{i}") for i in range(RING)]
    k.sent = 0
    k.c = sb("c", [P, 8])
    k.ps = ctx.enter_context(nc.psum_tensor("ps", [P, 8, BANK], F32))
    with Stage(nc, "const") as st:
        filled = st.sem("filled")
        block = st.block()

        @block.gpsimd
        def _(pool):
            pool.memset(k.ident[:], 0.0).then_inc(filled, 1)
            pool.memset(k.ones[:], 1.0).then_inc(filled, 1)
            pool.memset(k.nhalf[:], -0.5)
            pool.memset(k.zero[:], 0.0)
            pool.wait_ge(filled, 2)
            pool.affine_select(out=k.ident[:], in_=k.ident[:], compare_op=ALU.not_equal, fill=1.0,
                               base=0, pattern=[[-1, P]], channel_multiplier=1)
            pool.affine_select(out=k.upto[:], in_=k.ones[:], compare_op=ALU.is_ge, fill=0.0,
                               base=0, pattern=[[1, P]], channel_multiplier=-1)
    return k


def load(k, name, pairs):
    nc = k.nc
    with Stage(nc, name) as st:
        landed = st.sem("landed")
        block = st.block()

        @block.sync
        def _(sp):
            with nc.allow_non_contiguous_dma("small vectors"):
                for dst, src in pairs:
                    sp.dma_start(dst, src).then_inc(landed, 16)
            sp.wait_ge(landed, 16 * len(pairs))


def rows(src, n=P):
    return src.partition_broadcast(n)


class Weights:

    def __init__(self, w, KT, N):
        self.w, self.KT, self.N, self.ahead = w, KT, N, 0
        self.chunks = [(n0, min(n0 + BANK, N)) for n0 in range(0, N, BANK)]
        self.units = []
        for c, (n0, n1) in enumerate(self.chunks):
            step = min(KT, 4 if n1 - n0 > 2 * P else 8)
            self.units += [(c, a, min(a + step, KT)) for a in range(0, KT, step)]


def view(weights, unit, buf):
    c, a, z = unit
    n0, n1 = weights.chunks[c]
    return buf[:, :(z - a) * (n1 - n0)].rearrange("p (k n) -> p k n", k=z - a)


def send(k, sp, weights):
    c, a, z = unit = weights.units[weights.ahead]
    n0, n1 = weights.chunks[c]
    weights.ahead += 1
    slot = k.sent % RING
    k.sent += 1
    with k.nc.allow_non_contiguous_dma("narrow chunk"):
        sp.dma_start(view(weights, unit, k.ring[:, slot, :]),
                     weights.w[a * P:z * P, n0:n1].rearrange("(k p) n -> p k n", p=P)
                     ).then_inc(k.ring_landed[slot], 16)


def ahead(k, name, weights):
    with Stage(k.nc, name) as st:
        block = st.block()

        @block.sync
        def _(sp):
            while weights.ahead < min(RING, len(weights.units)):
                send(k, sp, weights)
    return weights


def gemm(k, name, xT, weights, finish, feature_major=False, bias=None, then=None, also=(),
         beside=None):
    nc, T, ps = k.nc, k.T, k.ps
    KT, chunks, units = weights.KT, weights.chunks, weights.units
    first_sent = k.sent - weights.ahead
    slot = lambda n: (first_sent + n) % RING
    with Stage(nc, name) as st:
        x_hi, x_lo = (st.sb(n, [P, KT, T], F32R) for n in ("x_hi", "x_lo"))
        size = max((z - a) * (chunks[c][1] - chunks[c][0]) for c, a, z in units)
        hi, lo = (st.sb(n, [P, 2, size], F32R) for n in ("hi", "lo"))
        x_high, x_split = st.sem("x_high"), st.sem("x_split")
        high, split = st.sem("high"), st.sem("split")
        used = st.sem("used")
        filled = [st.sem(f"filled{j}") for j in range(2)]
        drained = [st.sem(f"drained{j}") for j in range(2)]
        also_landed, beside_step = st.sem("also_landed"), st.sem("beside_step")
        block = st.block()
        xparts = [(a, min(a + 4, KT)) for a in range(0, KT, 4)]

        def halves(c):
            n = chunks[c][1] - chunks[c][0]
            return [0, 1] if not feature_major or n > 2 * P else [0]

        def last_of(n):
            return n + 1 == len(units) or units[n + 1][0] != units[n][0]

        def wait_used(eng, n):
            if last_of(n):
                c = units[n][0]
                j = halves(c)[-1]
                eng.wait_ge(filled[j], sum(j in halves(d) for d in range(c + 1)))
            else:
                eng.wait_ge(used, sum(not last_of(m) for m in range(n + 1)))

        @block.sync
        def _(sp):
            for n in range(weights.ahead, len(units)):
                if n >= RING:
                    sp.wait_ge(split, n - RING + 1)
                send(k, sp, weights)
            with nc.allow_non_contiguous_dma("small vectors"):
                for dst, src in also:
                    sp.dma_start(dst, src).then_inc(also_landed, 16)
            if then is not None:
                for n in range(len(units), len(units) + min(RING, len(then.units))):
                    if n >= RING:
                        sp.wait_ge(split, n - RING + 1)
                    send(k, sp, then)
            if also:
                sp.wait_ge(also_landed, 16 * len(also))

        @block.gpsimd
        def _(pool):
            if beside is not None:
                beside(pool, Chain(pool, beside_step))

        @block.tensor
        def _(pe):
            count, seen_x = [0, 0], 0
            for n, unit in enumerate(units):
                c, a, z = unit
                n0, n1 = chunks[c]
                m = n1 - n0
                while seen_x < len(xparts) and xparts[seen_x][0] < z:
                    seen_x += 1
                    pe.wait_ge(x_split, seen_x)
                pe.wait_ge(split, n + 1)
                wh, wl = (view(weights, unit, b[:, n % 2, :]) for b in (hi, lo))
                start, stop = a == 0, last_of(n)
                for j in halves(c):
                    if start:
                        if count[j] >= 2:
                            pe.wait_ge(drained[j], count[j] - 1)
                        count[j] += 1
                    bank = ps[:, 2 * j + (count[j] - 1) % 2, :]
                    tiles = range(2 * j, min(2 * j + 2, -(-m // P))) if feature_major else [None]
                    for i in tiles:
                        for kt in range(a, z):
                            if feature_major:
                                w_ = min(P, m - i * P)
                                out = ps[:w_, 4 * ((count[j] - 1) % 2) + i, :T]
                                s = [b[:, kt - a, i * P:i * P + w_] for b in (wh, wl)]
                                r = [b[:, kt, :] for b in (x_hi, x_lo)]
                            else:
                                out = bank[:, :m]
                                s = [b[:, kt, j * P:(j + 1) * P] for b in (x_hi, x_lo)]
                                r = [b[:, kt - a, :] for b in (wh, wl)]
                            first, end = kt == 0, kt == KT - 1 and bias is None
                            pe.matmul(out, s[0], r[0], start=first, stop=False, skip_group_check=True)
                            pe.matmul(out, s[0], r[1], start=False, stop=False, skip_group_check=True)
                            last = pe.matmul(out, s[1], r[0], start=False, stop=end, skip_group_check=True)
                    if stop and bias is not None:
                        last = pe.matmul(bank[:, :m], k.ones[0:1, :], bias[0:1, n0:n1], start=False, stop=True,
                                         skip_group_check=True)
                    if stop:
                        last.then_inc(filled[j], 1)
                if not stop:
                    last.then_inc(used, 1)

        def program(eng, x_part, w_unit, j):
            seen, seen_x, waiting = 0, 0, []

            def drain():
                nonlocal seen
                c = waiting.pop(0)
                eng.wait_ge(filled[j], seen + 1)
                b = seen % 2
                psum = ps[:, 4 * b + 2 * j:4 * b + 2 * j + 2, :T] if feature_major else ps[:, 2 * j + b, :]
                finish(eng, psum, j, *chunks[c]).then_inc(drained[j], 1)
                seen += 1
            for n, unit in enumerate(units):
                while seen_x < len(xparts) and xparts[seen_x][0] < unit[2]:
                    x_part(seen_x)
                    seen_x += 1
                w_unit(n)
                if last_of(n):
                    if waiting:
                        drain()
                    if j in halves(unit[0]):
                        waiting.append(unit[0])
            while waiting:
                drain()

        @block.scalar
        def _(act):
            def x_part(i):
                a, z = xparts[i]
                act.copy(x_hi[:, a:z].rearrange("p k t -> p (k t)"), xT[:, a:z].rearrange("p k t -> p (k t)")
                         ).then_inc(x_high, 1)

            def w_unit(n):
                act.wait_ge(k.ring_landed[slot(n)], 16 * ((first_sent + n) // RING + 1))
                if n >= 2:
                    wait_used(act, n - 2)
                act.copy(view(weights, units[n], hi[:, n % 2, :]),
                         view(weights, units[n], k.ring[:, slot(n), :])).then_inc(high, 1)
            program(act, x_part, w_unit, 0)

        @block.vector
        def _(dve):
            def x_part(i):
                a, z = xparts[i]
                dve.wait_ge(x_high, i + 1)
                dve.tensor_tensor(x_lo[:, a:z], xT[:, a:z], x_hi[:, a:z].bitcast(F32), ALU.subtract
                                  ).then_inc(x_split, 1)

            def w_unit(n):
                dve.wait_ge(high, n + 1)
                at = lambda buf: view(weights, units[n], buf)
                dve.tensor_tensor(at(lo[:, n % 2, :]), at(k.ring[:, slot(n), :]),
                                  at(hi[:, n % 2, :].bitcast(F32)), ALU.subtract).then_inc(split, 1)
            program(dve, x_part, w_unit, 1)


def transpose_in(k, name, src, dst, n_tiles=8, scale=None, src_cols=None,
                 factor=1.0):
    nc, T, ps = k.nc, k.T, k.ps
    cols = src_cols or (lambda t, i: src[:, t, i * P:(i + 1) * P])
    with Stage(nc, name) as st:
        turned, copied = st.sem("turned"), st.sem("copied")
        block = st.block()

        @block.tensor
        def _(pe):
            for i in range(n_tiles):
                if i >= 8:
                    pe.wait_ge(copied, i - 7)
                for t in range(k.NT):
                    last = pe.transpose(ps[:, i % 8, t * P:(t + 1) * P], cols(t, i), k.ident[:])
                last.then_inc(turned, 1)

        @block.scalar
        def _(act):
            for i in range(n_tiles):
                act.wait_ge(turned, i + 1)
                act.activation(dst[:, i, :], ps[:, i % 8, :T], ACT.Copy if scale is None else ACT.Identity,
                               scale=factor if scale is None else scale[:, i:i + 1]).then_inc(copied, 1)


def rms_rows(k, name, src, dst, gain=None, groups=1, mean=True, factor=1.0, sq=None):
    nc, NT = k.nc, k.NT
    d = src.shape[2] // groups
    shape = [P, NT, groups, d]
    with Stage(nc, name) as st:
        sq = st.sb("sq", shape) if sq is None else sq
        ss = st.sb("ss", [P, NT, groups])
        step, summed, rooted = st.sem("step"), st.sem("summed"), st.sem("rooted")
        block = st.block()
        v = src.rearrange("p t (g d) -> p t g d", g=groups)
        w = dst.rearrange("p t (g d) -> p t g d", g=groups)
        sf = ss[:].rearrange("p t g -> p (t g)")
        c = 1.0 / d if mean else 1.0

        @block.vector
        def _(dve):
            after = Chain(dve, step)
            after(dve.tensor_tensor(sq[:], v, v, ALU.mult))
            after(dve.tensor_reduce(ss[:], sq[:], AX.X, ALU.add))
            dve.tensor_scalar(ss[:], ss[:], c / factor ** 2, 1e-6 / factor ** 2, ALU.mult, ALU.add
                              ).then_inc(summed, 1)
            dve.wait_ge(rooted, 1)
            op = dve.tensor_tensor(w, v, ss[:].unsqueeze(3).to_broadcast(shape), ALU.mult)
            if gain is not None:
                after(op)
                dve.tensor_tensor(w, w, gain.unsqueeze(1).unsqueeze(1).to_broadcast(shape), ALU.mult)

        @block.gpsimd
        def _(pool):
            pool.wait_ge(summed, 1)
            pool.tensor_tensor(sf, sf, k.nhalf[:, :NT * groups], ALU.pow).then_inc(rooted, 1)


def attention(k, name, units, q_of, k_of, v_of, bias_of, out_of, dv, sink_of=None, minus=None,
              keys=None):
    nc, ps = k.nc, k.ps
    G = len(units[0][0])
    keys = keys or (lambda t: list(range(t + 1)))
    NK = max(len(keys(t)) for _, t in units) * P
    O = G // 2 if minus else G
    with Stage(nc, name) as st:
        S = st.sb("S", [P, 2, G, NK])
        PT = st.sb("PT", [P, 2, O, NK])
        mx = st.sb("mx", [P, 2, G])
        sm = st.sb("sm", [P, 2, G])
        es = st.sb("es", [P, 2, G])
        step = st.sem("step")
        scored, biased, shifted, raised = st.sem("scored"), st.sem("biased"), st.sem("shifted"), st.sem("raised")
        mixed, turned, turned_out = st.sem("mixed"), st.sem("turned"), st.sem("turned_out")
        applied, stored, sunk = st.sem("applied"), st.sem("stored"), st.sem("sunk")
        block = st.block()
        sc = lambda u: ps[:, 2 * (u % 2):2 * (u % 2) + 2, :].rearrange("p b (g n) -> p g b n", n=256)
        pairs = lambda ap: ap.rearrange("p (g b) n -> p g b n", b=2)
        tr = ps[:, 4:6, :].rearrange("p b (g n) -> p (b g) n", n=256)
        ob = lambda u: ps[:, 6 + u % 2, :O * dv].rearrange("p (g n) -> p g n", n=dv)

        @block.tensor
        def _(pe):
            def scores(u):
                heads, t = units[u]
                if u >= 2:
                    pe.wait_ge(biased, u - 1)
                for g, h in enumerate(heads):
                    for i, kt in enumerate(keys(t)):
                        last = pe.matmul(sc(u)[:, g // 2, g % 2, i * P:(i + 1) * P], q_of(h, t), k_of(h, kt),
                                         start=True, stop=True)
                last.then_inc(scored, 1)

            def apply(u):
                heads, t = units[u]
                pe.wait_ge(turned_out, u + 1)
                if u >= 2:
                    pe.wait_ge(stored, u - 1)
                for g in range(O):
                    h = heads[2 * g] if minus else heads[g]
                    for i, kt in enumerate(keys(t)):
                        last = pe.matmul(ob(u)[:, g, :], PT[:, u % 2, g, i * P:(i + 1) * P], v_of(h, kt),
                                         start=i == 0, stop=i == len(keys(t)) - 1)
                last.then_inc(applied, 1)

            for u in range(min(2, len(units))):
                scores(u)
            for u, (heads, t) in enumerate(units):
                if u + 2 < len(units):
                    scores(u + 2)
                if u >= 1:
                    apply(u - 1)
                if minus:
                    pe.wait_ge(mixed, u + 1)
                else:
                    pe.wait_ge(raised, u + 1)
                if u >= 1:
                    pe.wait_ge(turned_out, u)
                for g in range(O):
                    for i, kt in enumerate(keys(t)):
                        last = pe.transpose(tr[:, g, i * P:(i + 1) * P],
                                            S[:, u % 2, 2 * g if minus else g, i * P:(i + 1) * P], k.ident[:])
                last.then_inc(turned, 1)
            apply(len(units) - 1)

        @block.scalar
        def _(act):
            for u, (heads, t) in enumerate(units):
                n = len(keys(t)) * P
                act.wait_ge(shifted, u + 1)
                act.activation(S[:, u % 2, :, :n], S[:, u % 2, :, :n], ACT.Exp).then_inc(raised, 1)
                if sink_of:
                    act.activation(es[:, u % 2, :], es[:, u % 2, :], ACT.Exp).then_inc(sunk, 1)
                act.wait_ge(turned, u + 1)
                if u >= 2:
                    act.wait_ge(applied, u - 1)
                act.activation(PT[:, u % 2, :, :n], tr[:, :O, :n], ACT.Copy).then_inc(turned_out, 1)

        @block.vector
        def _(dve):
            after = Chain(dve, step)

            def shift(u):
                heads, t = units[u]
                n = len(keys(t)) * P
                s, m, b = S[:, u % 2, :, :n], mx[:, u % 2, :], u % 2
                dve.wait_ge(scored, u + 1)
                if u >= 2:
                    dve.wait_ge(turned, u - 1)
                dve.tensor_tensor(pairs(s), sc(u)[:, :G // 2, :, :n], pairs(bias_of(heads, t)), ALU.add
                                  ).then_inc(biased, 1)
                dve.wait_ge(biased, u + 1)
                after(dve.tensor_reduce(m, s, AX.X, ALU.max))
                if sink_of:
                    after(dve.tensor_tensor(m, m, sink_of(heads), ALU.max))
                    after(dve.tensor_tensor(es[:, b, :], sink_of(heads), m, ALU.subtract))
                dve.tensor_tensor(s, s, m.unsqueeze(2).to_broadcast([P, G, n]), ALU.subtract
                                  ).then_inc(shifted, 1)

            def finish(u):
                heads, t = units[u]
                n = len(keys(t)) * P
                s, l = S[:, u % 2, :, :n], sm[:, u % 2, :]
                dve.wait_ge(raised, u + 1)
                if u >= 2:
                    dve.wait_ge(stored, u - 1)
                after(dve.tensor_reduce(l, s, AX.X, ALU.add))
                if sink_of:
                    dve.wait_ge(sunk, u + 1)
                    after(dve.tensor_tensor(l, l, es[:, u % 2, :], ALU.add))
                after(dve.reciprocal(l, l))
                if minus:
                    after(dve.tensor_tensor(s, s, l.unsqueeze(2).to_broadcast([P, G, n]), ALU.mult))
                    for g in range(O):
                        last = dve.scalar_tensor_tensor(S[:, u % 2, 2 * g, :n], S[:, u % 2, 2 * g + 1, :n],
                                                        minus(g), S[:, u % 2, 2 * g, :n], ALU.mult, ALU.add)
                    last.then_inc(mixed, 1)

            def store(u):
                heads, t = units[u]
                dve.wait_ge(applied, u + 1)
                out = out_of(heads, t)
                if minus:
                    dve.tensor_copy(out, ob(u)).then_inc(stored, 1)
                else:
                    dve.tensor_tensor(out, ob(u), sm[:, u % 2, :].unsqueeze(2).to_broadcast([P, G, dv]),
                                      ALU.mult).then_inc(stored, 1)

            shift(0)
            for u in range(len(units)):
                if u + 1 < len(units):
                    shift(u + 1)
                if u >= 1:
                    store(u - 1)
                finish(u)
            store(len(units) - 1)


def dump(k, name, pairs):
    with Stage(k.nc, name) as st:
        stored = st.sem("stored")
        block = st.block()

        @block.sync
        def _(sp):
            for dst, src in pairs:
                sp.dma_start(dst, src).then_inc(stored, 16)
            sp.wait_ge(stored, 16 * len(pairs))


def on_vector(k, name, body):
    with Stage(k.nc, name) as st:
        step = st.sem("step")
        block = st.block()

        @block.vector
        def _(dve):
            body(dve, Chain(dve, step))


def on_scalar(k, name, body):
    with Stage(k.nc, name) as st:
        step = st.sem("step")
        block = st.block()

        @block.scalar
        def _(act):
            body(act, Chain(act, step))


def on_gpsimd(k, name, body):
    with Stage(k.nc, name) as st:
        step = st.sem("step")
        block = st.block()

        @block.gpsimd
        def _(pool):
            body(pool, Chain(pool, step))


def on_tensor(k, name, body):
    with Stage(k.nc, name) as st:
        block = st.block()

        @block.tensor
        def _(pe):
            body(pe)


def level_masks(k, masks):
    def body(pool, after):
        after(pool.memset(masks[:], 0.0))
        for v in range(7):
            b = 2 ** v
            half = masks[:, v, :].rearrange("s (n h j) -> s n h j", h=2, j=b)[:, :, 1, :]
            after(pool.memset(half, 1.0))
            after(pool.affine_select(out=half, in_=half, compare_op=ALU.is_ge, fill=0.0, base=0,
                                     pattern=[[-2 * b, P // (2 * b)], [0, b]], channel_multiplier=1))
            after(pool.affine_select(out=half, in_=half, compare_op=ALU.is_ge, fill=0.0, base=b - 1,
                                     pattern=[[2 * b, P // (2 * b)], [0, b]], channel_multiplier=-1))
    on_gpsimd(k, "level_masks", body)


def copier(nc, eng):
    return eng.copy if eng is nc.scalar else eng.tensor_copy


def tokens_to(k, dst):
    return lambda eng, psum, j, n0, n1: copier(k.nc, eng)(dst[:, j, n0:n1], psum[:, :n1 - n0])


def features_to(k, dst):
    def finish(eng, psum, j, n0, n1):
        i = n0 // P + 2 * j
        return copier(k.nc, eng)(dst[:, i:i + 2, :], psum)
    return finish


def turn_out(k, name, src, dst, n_tiles):
    with Stage(k.nc, name) as st:
        turned, copied = st.sem("turned"), st.sem("copied")
        block = st.block()
        groups = [(t, i, min(i + 4, n_tiles)) for t in range(k.NT) for i in range(0, n_tiles, 4)]

        @block.tensor
        def _(pe):
            for n, (t, i0, i1) in enumerate(groups):
                if n >= 8:
                    pe.wait_ge(copied, n - 7)
                for i in range(i0, i1):
                    last = pe.transpose(k.ps[:, n % 8, (i - i0) * P:(i - i0 + 1) * P],
                                        src[:, i, t * P:(t + 1) * P], k.ident[:])
                last.then_inc(turned, 1)

        @block.scalar
        def _(act):
            for n, (t, i0, i1) in enumerate(groups):
                act.wait_ge(turned, n + 1)
                act.copy(dst[:, t, i0 * P:i1 * P], k.ps[:, n % 8, :(i1 - i0) * P]).then_inc(copied, 1)


def alibi(k, pool, after, table, dist, heads, width, step, offset):
    for t in range(k.NT):
        after(pool.iota(dist[:, t, :], pattern=[[step, width]], base=offset - t * P,
                        channel_multiplier=-1, allow_small_or_imprecise_dtypes=True))
        for h in range(heads):
            after(pool.tensor_scalar(table[:, t, h, :width], dist[:, t, :],
                                     2.0 ** (-8.0 * (h + 1) / heads), None, ALU.mult))
        after(pool.affine_select(out=table[:, t, :, :width], in_=table[:, t, :, :width],
                                 compare_op=ALU.is_ge, fill=NEG, base=t * P - offset,
                                 pattern=[[0, heads], [-step, width]], channel_multiplier=1))


def sparse_attention(k, A, scratch, y):
    nc, T, NT, ps = k.nc, k.T, k.NT, k.ps
    D, H, G = 64, 8, 2
    NC = (T - 32) // 16 + 1
    with ExitStack() as own:
        sb = lambda name, shape: own.enter_context(nc.sbuf_tensor("nsa_" + name, shape, F32))
        U = sb("U", [P, NT, 1304])
        pe_c, w2 = sb("pe_c", [P, 2, 16]), sb("w2", [P, 2, 2, D])
        bias, dist, cb = sb("bias", [P, NT, H, T]), sb("dist", [P, NT, T]), sb("cb", [P, NT, H, 16])
        gains = sb("gains", [P, 4, D])

        def tables(pool, after):
            alibi(k, pool, after, bias, dist, H, T, 1, 0)
            alibi(k, pool, after, cb, dist[:, :, :NC], H, NC, 16, 31)
        gemm(k, "nsa_in", k.hT, k.W["nsa_in"], tokens_to(k, U), beside=tables,
             also=[(gains[:], A["nsa_qk_gain"][0].partition_broadcast(P)), (pe_c[:, 0, :], A["cmp_pe"][0, 0].rearrange("(j l) d -> (l d) j", l=2)), (pe_c[:, 1, :], A["cmp_pe"][0, 1].rearrange("(j l) d -> (l d) j", l=2)), (w2[:, 0], A["cmp_w2"][0, 0].rearrange("(j p) d -> p j d", p=P)), (w2[:, 1], A["cmp_w2"][0, 1].rearrange("(j p) d -> p j d", p=P))])
        qT, kT = sb("qT", [P, 4, T]), sb("kT", [P, 2, 2, T])
        KD = sb("KD", [P, 2, NT, 2, 2, D])
        O = sb("O", [P, NT, 3, H * D])
        flat = sb("flat", [2 * NC, 2, 2048])
        flatT = sb("flatT", [P, 2, 16, 2 * NC])
        hid, g1, g2 = (sb(n, [P, 2, 2, 2 * NC]) for n in ("hid", "g1", "g2"))
        kc, vc = sb("kc", [2 * NC, 2, D]), sb("vc", [2 * NC, D])
        kss = sb("kss", [2 * NC, 1])
        kcT = sb("kcT", [P, 2 * NC])
        vbd = sb("vbd", [P, H * D])
        pc, pcT = sb("pc", [P, NT, H, 16]), sb("pcT", [P, NT, P])
        cm, cl, seen = sb("cm", [P, NT, H]), sb("cl", [P, NT, H]), sb("seen", [P, NT, H])

        dump(k, "nsa_out", [(scratch[c, g, t * P:(t + 1) * P, :],
                             U[:, t, 512 + (2 * c + g) * D:512 + (2 * c + g + 1) * D])
                            for c in range(2) for g in range(G) for t in range(NT)])
        load(k, "nsa_flat", [(flat[g * NC:(g + 1) * NC, c, :],
                              bass.AP(tensor=scratch.tensor, offset=(c * G + g) * T * D,
                                      ap=[[16 * D, NC], [1, 32 * D]]))
                             for c in range(2) for g in range(G)])

        def turn_flat(pe):
            for c in range(2):
                for j in range(16):
                    pe.transpose(ps[:, c, j * 2 * NC:(j + 1) * 2 * NC], flat[:, c, j * P:(j + 1) * P],
                                 k.ident[:2 * NC, :2 * NC])
        on_tensor(k, "nsa_tf", turn_flat)

        def add_pe(dve, after):
            for c in range(2):
                dve.tensor_tensor(flatT[:, c], ps[:, c, :32 * NC].rearrange("p (j n) -> p j n", j=16),
                                  pe_c[:, c, :].unsqueeze(2).to_broadcast([P, 16, 2 * NC]), ALU.add)
        on_vector(k, "nsa_pe", add_pe)
        compress_hidden(k, "nsa_hid", A["cmp_w1"][0], flatT[:], hid[:])

        def gelu_a(dve, after):
            after(dve.tensor_tensor(g1[:], hid[:], hid[:], ALU.mult))
            after(dve.tensor_scalar(g1[:], g1[:], 0.044715, 1.0, ALU.mult, ALU.add))
            after(dve.tensor_tensor(g1[:], g1[:], hid[:], ALU.mult))
        on_vector(k, "nsa_ga", gelu_a)
        on_scalar(k, "nsa_gb", lambda act, after:
                  act.activation(g2[:], g1[:], ACT.Tanh, scale=math.sqrt(2 / math.pi)))

        def gelu_c(dve, after):
            after(dve.tensor_scalar(g2[:], g2[:], 1.0, 0.5, ALU.add, ALU.mult))
            after(dve.tensor_tensor(hid[:], hid[:], g2[:], ALU.mult))
        on_vector(k, "nsa_gc", gelu_c)

        def second(pe):
            for c in range(2):
                for j in range(2):
                    pe.matmul(ps[:2 * NC, c, :D], hid[:, c, j, :], w2[:, c, j, :], start=j == 0, stop=j == 1)
        on_tensor(k, "nsa_w2", second)

        def kc_norm(dve, after):
            after(dve.memset(vbd[:], 0.0))
            after(dve.tensor_copy(vc[:], ps[:2 * NC, 1, :D]))
            after(dve.tensor_copy(kc[:, 0, :], ps[:2 * NC, 0, :D]))
            after(dve.tensor_tensor(kc[:, 1, :], kc[:, 0, :], kc[:, 0, :], ALU.mult))
            after(dve.tensor_reduce(kss[:], kc[:, 1, :], AX.X, ALU.add))
            after(dve.tensor_scalar(kss[:], kss[:], 1.0 / D, 1e-6, ALU.mult, ALU.add))
        on_vector(k, "nsa_kn", kc_norm)
        on_gpsimd(k, "nsa_kr", lambda pool, after:
                  pool.tensor_tensor(kss[:], kss[:], k.nhalf[:2 * NC, :1], ALU.pow))

        def kc_scale(dve, after):
            after(dve.scalar_tensor_tensor(kc[:, 0, :], kc[:, 0, :], kss[:, 0:1], gains[:2 * NC, 1, :],
                                           ALU.mult, ALU.mult))
            dve.tensor_copy(kc[:, 1, :], kc[:, 0, :])
        on_vector(k, "nsa_ks", kc_scale)
        load(k, "nsa_vbd", [(vbd[16 * h:16 * h + NC, h * D:(h + 1) * D],
                             vc[(h // 4) * NC:(h // 4 + 1) * NC, :]) for h in range(H)])
        ahead(k, "nsa_ahead", k.W["gdn_in"])
        on_tensor(k, "nsa_kt", lambda pe: pe.transpose(
            ps[:, 0, :2 * NC], kc[:].rearrange("n u d -> n (u d)"), k.ident[:2 * NC, :2 * NC]))
        on_vector(k, "nsa_kv", lambda dve, after: dve.tensor_copy(kcT[:], ps[:, 0, :2 * NC]))

        rms_rows(k, "nsa_q", U[:, :, 0:512], U[:, :, 0:512], gains[:, 0, :], groups=H)
        for n, (a, gi) in enumerate(((768, 2), (1024, 3))):
            rms_rows(k, f"nsa_k{n}", U[:, :, a:a + 128], U[:, :, a:a + 128], gains[:, gi, :], groups=G)

        def twice(dve, after):
            for n, a in enumerate((768, 1024)):
                for u in range(2):
                    dve.tensor_copy(KD[:, n, :, :, u, :], U[:, :, a:a + 128].rearrange("p t (g d) -> p t g d", g=G))
        on_vector(k, "nsa_twice", twice)
        transpose_in(k, "nsa_qT", U, qT, 4, factor=D ** -0.5)
        for n in range(2):
            transpose_in(k, f"nsa_kT{n}", None, kT[:, n], 2,
                         src_cols=lambda t, i, n=n: KD[:, n, t, i].rearrange("p u d -> p (u d)"))
        half = lambda h: slice((h % 2) * D, (h % 2 + 1) * D)
        units = [(list(range(g * 4, g * 4 + 4)), t) for t in range(NT) for g in range(G)]
        for n, a in enumerate((896, 1152)):
            attention(k, f"nsa_a{n}", units,
                      q_of=lambda h, t: qT[half(h), h // 2, t * P:(t + 1) * P],
                      k_of=lambda h, kt, n=n: kT[half(h), n, h // 4, kt * P:(kt + 1) * P],
                      v_of=lambda h, kt, a=a: U[:, kt, a + (h // 4) * D:a + (h // 4 + 1) * D],
                      bias_of=lambda hs, t: bias[:, t, hs[0]:hs[-1] + 1, :(t + 1) * P],
                      out_of=lambda hs, t, n=n: O[:, t, 1 + n, hs[0] * D:(hs[-1] + 1) * D].rearrange(
                          "p (g d) -> p g d", d=D), dv=D)

        def c_scores(pe):
            for t in range(NT):
                for h in range(H):
                    pe.matmul(ps[:, 2 * t + h % 2, h // 2 * 16:h // 2 * 16 + NC], qT[half(h), h // 2, t * P:(t + 1) * P],
                              kcT[half(h), (h // 4) * NC:(h // 4 + 1) * NC], start=True, stop=True)
        on_tensor(k, "nsa_cs", c_scores)
        flat2 = lambda x: x[:].rearrange("p t h -> p (t h)")
        pcv = pc[:].rearrange("p t h n -> p (t h) n")

        def c_shift(dve, after):
            after(dve.memset(pc[:], 0.0))
            for t in range(NT):
                pair = lambda x: x[:, t].rearrange("p (g b) n -> p g b n", b=2)[:, :, :, :NC]
                after(dve.tensor_tensor(pair(pc), ps[:, 2 * t:2 * t + 2, :64].rearrange(
                    "p b (g n) -> p g b n", n=16)[:, :, :, :NC], pair(cb), ALU.add))
            after(dve.tensor_reduce(flat2(cm), pcv[:, :, :NC], AX.X, ALU.max))
            after(dve.tensor_tensor(pcv[:, :, :NC], pcv[:, :, :NC],
                                    flat2(cm).unsqueeze(2).to_broadcast([P, NT * H, NC]), ALU.subtract))
            after(dve.tensor_scalar(seen[:], cm[:], NEG / 2, None, ALU.is_gt))
        on_vector(k, "nsa_c1", c_shift)
        on_scalar(k, "nsa_c2", lambda act, after: act.activation(pcv[:, :, :NC], pcv[:, :, :NC], ACT.Exp))

        def c_norm(dve, after):
            after(dve.tensor_reduce(flat2(cl), pcv[:, :, :NC], AX.X, ALU.add))
            after(dve.reciprocal(cl[:], cl[:]))
            after(dve.tensor_tensor(cl[:], cl[:], seen[:], ALU.mult))
            dve.tensor_tensor(pcv[:, :, :NC], pcv[:, :, :NC],
                              flat2(cl).unsqueeze(2).to_broadcast([P, NT * H, NC]), ALU.mult)
        on_vector(k, "nsa_c3", c_norm)
        on_tensor(k, "nsa_c4", lambda pe: [pe.transpose(
            ps[:, t, :P], pc[:, t].rearrange("p h n -> p (h n)"), k.ident[:]) for t in range(NT)])
        on_vector(k, "nsa_c5", lambda dve, after: [dve.tensor_copy(pcT[:, t], ps[:, t, :P]) for t in range(NT)])
        on_tensor(k, "nsa_c6", lambda pe: [pe.matmul(ps[:, t, :], pcT[:, t], vbd[:], start=True, stop=True)
                                           for t in range(NT)])
        gates = U[:, :, 1280:1304]
        on_scalar(k, "nsa_g", lambda act, after: act.activation(gates, gates, ACT.Sigmoid))

        def combine(dve, after):
            for t in range(NT):
                after(dve.tensor_copy(O[:, t, 0, :], ps[:, t, :]))
                Ot = O[:, t].rearrange("p b (h d) -> p (b h) d", d=D)
                after(dve.tensor_tensor(Ot, Ot, U[:, t, 1280:1304].unsqueeze(2).to_broadcast([P, 24, D]), ALU.mult))
                after(dve.tensor_tensor(y[:, t, :], O[:, t, 0, :], O[:, t, 1, :], ALU.add))
                after(dve.tensor_tensor(y[:, t, :], y[:, t, :], O[:, t, 2, :], ALU.add))
        on_vector(k, "nsa_y", combine)


def compress_hidden(k, name, w1, xT, hid):
    nc, ps, N = k.nc, k.ps, xT.shape[3]
    w = k.wring[:, 0:2, :].rearrange("p c (k n) -> p c k n", k=16)
    with Stage(nc, name) as st:
        landed, filled = [st.sem(f"landed{c}") for c in range(2)], st.sem("filled")
        block = st.block()

        @block.sync
        def _(sp):
            for c in range(2):
                sp.dma_start(w[:, c], w1[c].rearrange("(k p) n -> p k n", p=P)).then_inc(landed[c], 16)

        @block.tensor
        def _(pe):
            for c in range(2):
                pe.wait_ge(landed[c], 16)
                for j in range(2):
                    for kt in range(16):
                        last = pe.matmul(ps[:, 2 * c + j, :N], w[:, c, kt, j * P:(j + 1) * P], xT[:, c, kt, :],
                                         start=kt == 0, stop=kt == 15)
                    last.then_inc(filled, 1)

        @block.vector
        def _(dve):
            for n in range(4):
                dve.wait_ge(filled, n + 1)
                dve.tensor_copy(hid[:, n // 2, n % 2, :], ps[:, n, :N])


def column(v, n=None):
    return v.rearrange("(i p) -> p i", p=P)


def gated_delta(k, A, masks, y):
    nc, T, NT, ps = k.nc, k.T, k.NT, k.ps
    H, D = 4, 128
    assert NT == 2
    with ExitStack() as own:
        sb = lambda name, shape: own.enter_context(nc.sbuf_tensor("gdn_" + name, shape, F32))
        cw = sb("cw", [P, 4, 12])
        alog, dt, gain = sb("alog", [P, H]), sb("dt", [P, H]), sb("gain", [P, D])
        Z = sb("Z", [P, NT, 520])
        raw, conv = sb("raw", [P, 12, T + 3]), sb("conv", [P, 12, T])
        tok = sb("tok", [P, NT, 1536])
        gemm(k, "gdn_in", k.hT, k.W["gdn_in"], features_to(k, raw[:, :, 3:]),
             feature_major=True,
             then=k.W["gdn_z"],
             also=[(cw[:, j, :], column(A["gdn_conv_w"][0, j])) for j in range(4)] + [(alog[:], rows(A["gdn_a_log"][0])), (dt[:], rows(A["gdn_dt_bias"][0])), (gain[:], rows(A["gdn_out_gain"][0]))])
        gemm(k, "gdn_z", k.hT, k.W["gdn_z"], tokens_to(k, Z),
             then=k.W["mb_gates"])

        def convolve(dve, after):
            after(dve.memset(raw[:, :, 0:3], 0.0))
            for j in range(4):
                for i in range(12):
                    if j == 0:
                        op = dve.tensor_scalar(conv[:, i, :], raw[:, i, 0:T], cw[:, 0, i:i + 1], None, ALU.mult)
                    else:
                        op = dve.scalar_tensor_tensor(conv[:, i, :], raw[:, i, j:j + T], cw[:, j, i:i + 1],
                                                      conv[:, i, :], ALU.mult, ALU.add)
                after(op)
        on_vector(k, "gdn_conv", convolve)
        on_scalar(k, "gdn_silu", lambda act, after: act.activation(conv[:], conv[:], ACT.Silu))
        turn_out(k, "gdn_tok", conv, tok, 12)
        rms_rows(k, "gdn_q", tok[:, :, 0:512], tok[:, :, 0:512], groups=H, mean=False, factor=D ** -0.5)
        rms_rows(k, "gdn_k", tok[:, :, 512:1024], tok[:, :, 512:1024], groups=H, mean=False)
        beta, sp, ab, g = (sb(n, [P, NT, H]) for n in ("beta", "sp", "ab", "g"))
        gcs = sb("gcs", [P, NT, 2, H])
        e1, e2 = sb("e1", [P, NT, H]), sb("e2", [P, NT, H])

        def decay_in(dve, after):
            after(dve.tensor_tensor(sp[:], Z[:, :, 516:520], dt[:].unsqueeze(1).to_broadcast([P, NT, H]), ALU.add))
            after(dve.tensor_scalar(ab[:], sp[:], -1.0, None, ALU.mult))
            after(dve.tensor_tensor(ab[:], ab[:], sp[:], ALU.min))
        on_vector(k, "gdn_g1", decay_in)

        def soft(act, after):
            after(act.activation(ab[:], ab[:], ACT.Exp))
            after(act.activation(ab[:], ab[:], ACT.Ln, bias=1.0))
            act.activation(alog[:], alog[:], ACT.Exp)
            act.activation(beta[:], Z[:, :, 512:516], ACT.Sigmoid)
            act.activation(Z[:, :, 0:512], Z[:, :, 0:512], ACT.Silu)
        on_scalar(k, "gdn_g2", soft)

        def decay(dve, after):
            after(dve.scalar_tensor_tensor(g[:], sp[:], 0.0, ab[:], ALU.max, ALU.add))
            after(dve.scalar_tensor_tensor(g[:], g[:], -1.0, alog[:].unsqueeze(1).to_broadcast([P, NT, H]),
                                           ALU.mult, ALU.mult))
        on_vector(k, "gdn_g3", decay)
        part = lambda x, i: x[:].rearrange("p a b -> p (a b)")[:, i * NT * H * P:(i + 1) * NT * H * P].rearrange(
            "p (t h c) -> p t h c", t=NT, h=H)
        grep, Ti, XX = (part(conv, i) for i in range(3))
        kb, kbg, CT = (part(raw, i) for i in range(3))
        on_vector(k, "gdn_g4", lambda dve, after: dve.tensor_copy(
            grep, g[:].unsqueeze(3).to_broadcast([P, NT, H, P])))

        def running(pe):
            for t in range(NT):
                pe.matmul(ps[:, t, 0:H], k.upto[:], g[:, t, :], start=True, stop=True)
                pe.matmul(ps[:, t, H:2 * H], k.ones[:], g[:, t, :], start=True, stop=True)
                for h in range(H):
                    pe.matmul(ps[:, 2 + t, h * P:(h + 1) * P], grep[:, t, h, :], k.upto[:], start=True, stop=True)
        on_tensor(k, "gdn_run", running)
        DT = sb("DT", [P, NT, H, P])

        def decays(dve, after):
            after(dve.tensor_copy(gcs[:].rearrange("p t u h -> p t (u h)"), ps[:, 0:2, :2 * H]))
            after(dve.tensor_copy(e1[:], gcs[:, :, 0, :]))
            after(dve.tensor_tensor(e2[:], gcs[:, :, 1, :], gcs[:, :, 0, :], ALU.subtract))
            after(dve.tensor_tensor(DT[:], ps[:, 2:4, :].rearrange("p t (h c) -> p t h c", h=H),
                                    e1[:].unsqueeze(3).to_broadcast([P, NT, H, P]), ALU.subtract))
            after(dve.tensor_scalar(DT[:], DT[:], 0.0, None, ALU.min))
        on_vector(k, "gdn_d1", decays)

        el = sb("el", [P, NT, H])

        def exps(act, after):
            act.activation(DT[:], DT[:], ACT.Exp)
            act.activation(el[:], gcs[:, :, 1, :], ACT.Exp)
            act.activation(e1[:], e1[:], ACT.Exp)
            act.activation(e2[:], e2[:], ACT.Exp)
        on_scalar(k, "gdn_d2", exps)
        vb, kd = (sb(n, [P, NT, H, D]) for n in ("vb", "kd"))
        qd = sb("qd", [P, H, D])
        q4, k4, v4 = (tok[:, :, a:a + 512].rearrange("p t (h d) -> p t h d", h=H) for a in (0, 512, 1024))
        by = lambda x: x.unsqueeze(3).to_broadcast([P, NT, H, D])

        def weigh(dve, after):
            dve.tensor_tensor(DT[:], DT[:], k.upto[:].unsqueeze(1).unsqueeze(1).to_broadcast([P, NT, H, P]), ALU.mult)
            dve.tensor_tensor(vb[:], v4, by(beta[:]), ALU.mult)
            dve.tensor_tensor(kd[:], k4, by(e2[:]), ALU.mult)
            dve.tensor_tensor(qd[:], q4[:, 1], e1[:, 1].unsqueeze(2).to_broadcast([P, H, D]), ALU.mult)
            after(dve.tensor_tensor(kb, k4, by(beta[:]), ALU.mult))
            dve.tensor_tensor(kbg, kb, by(e1[:]), ALU.mult)
        on_vector(k, "gdn_w", weigh)
        qT, kT, kbT, qdT = (sb(n, [P, H, T]) for n in ("qT", "kT", "kbT", "qdT"))
        for n, (src, dst) in enumerate(((tok[:, :, 0:512], qT), (tok[:, :, 512:1024], kT),
                                        (kb.rearrange("p t h d -> p t (h d)"), kbT))):
            transpose_in(k, f"gdn_t{n}", src, dst, H)
        transpose_in(k, "gdn_t3", None, qdT, H, src_cols=lambda t, i: qd[:, i, :])
        MT, AT = sb("MT", [P, NT, H, P]), sb("AT", [P, NT, H, P])

        def products(pe):
            for t in range(NT):
                for h in range(H):
                    kh = kT[:, h, t * P:(t + 1) * P]
                    pe.matmul(ps[:, t, h * P:(h + 1) * P], kh, kbT[:, h, t * P:(t + 1) * P], start=True, stop=True)
                    pe.matmul(ps[:, 2 + t, h * P:(h + 1) * P], kh, qT[:, h, t * P:(t + 1) * P], start=True, stop=True)
        on_tensor(k, "gdn_kk", products)
        bank = lambda i: ps[:, i:i + 2, :].rearrange("p t (h c) -> p t h c", h=H)
        on_vector(k, "gdn_m", lambda dve, after: [
            dve.tensor_tensor(MT[:], bank(0), DT[:], ALU.mult), dve.tensor_tensor(AT[:], bank(2), DT[:], ALU.mult)])
        TT = sb("TT", [P, NT, H, P])
        solve_unit_triangle(k, "gdn_s", MT, masks, Ti, TT[:], CT, XX, NT, H)

        vn, S = vb, sb("S", [P, H, D])
        wT = sb("wT", [P, H, P])

        def uw(pe):
            for h in range(H):
                for t in range(NT):
                    pe.matmul(ps[:, t, h * D:(h + 1) * D], TT[:, t, h, :], vb[:, t, h, :], start=True, stop=True)
                pe.matmul(ps[:, 2, h * P:(h + 1) * P], kbg[:, 1, h, :], TT[:, 1, h, :], start=True, stop=True)
        on_tensor(k, "gdn_uw", uw)
        on_vector(k, "gdn_u", lambda dve, after: [
            dve.tensor_copy(vn[:], bank(0)),
            dve.tensor_copy(wT[:], ps[:, 2, :].rearrange("p (h c) -> p h c", h=H))])

        def first_chunk(pe):
            for h in range(H):
                pe.matmul(ps[:, 0, h * D:(h + 1) * D], AT[:, 0, h, :], vn[:, 0, h, :], start=True, stop=True)
                pe.matmul(ps[:, 1, h * D:(h + 1) * D], kd[:, 0, h, :], vn[:, 0, h, :], start=True, stop=True)
        on_tensor(k, "gdn_c0", first_chunk)
        on_vector(k, "gdn_s0", lambda dve, after: [
            dve.tensor_copy(tok[:, 0, 0:512], ps[:, 0, :]),
            dve.tensor_copy(S[:], ps[:, 1, :].rearrange("p (h c) -> p h c", h=H))])
        on_tensor(k, "gdn_ws", lambda pe: [pe.matmul(ps[:, 0, h * D:(h + 1) * D], wT[:, h, :], S[:, h, :],
                                                     start=True, stop=True) for h in range(H)])
        on_vector(k, "gdn_v1", lambda dve, after: dve.tensor_tensor(
            vn[:, 1], vn[:, 1], ps[:, 0, :].rearrange("p (h c) -> p h c", h=H), ALU.subtract))

        def second_chunk(pe):
            for h in range(H):
                pe.matmul(ps[:, 1, h * D:(h + 1) * D], qdT[:, h, P:2 * P], S[:, h, :], start=True, stop=False)
                pe.matmul(ps[:, 1, h * D:(h + 1) * D], AT[:, 1, h, :], vn[:, 1, h, :], start=False, stop=True)
        on_tensor(k, "gdn_c1", second_chunk)
        on_vector(k, "gdn_o1", lambda dve, after: dve.tensor_copy(tok[:, 1, 0:512], ps[:, 1, :]))
        rms_rows(k, "gdn_o", tok[:, :, 0:512], tok[:, :, 512:1024], gain[:], groups=H)
        on_vector(k, "gdn_y", lambda dve, after: dve.tensor_tensor(
            y[:], tok[:, :, 512:1024], Z[:, :, 0:512], ALU.mult))


def solve_unit_triangle(k, name, MT, masks, Ti, TT, CT, XX, NT, H):
    ps, nc = k.ps, k.nc
    b = lambda i: ps[:, i, :].rearrange("p (h c) -> p h c", h=H)
    with Stage(nc, name) as st:
        step = st.sem("step")
        joined = [st.sem(f"joined{t}") for t in range(NT)]
        crossed = [st.sem(f"crossed{t}") for t in range(NT)]
        held = [st.sem(f"held{t}") for t in range(NT)]
        closed = [st.sem(f"closed{t}") for t in range(NT)]
        block = st.block()
        L = masks.shape[1]

        @block.vector
        def _(dve):
            after = Chain(dve, step)
            for x in (Ti, TT):
                op = dve.tensor_copy(x, k.ident[:].unsqueeze(1).unsqueeze(1).to_broadcast([P, NT, H, P]))
            after(op)
            for v in range(L):
                for t in range(NT):
                    dve.tensor_tensor(CT[:, t], MT[:, t], masks[:, v, :].unsqueeze(1).to_broadcast([P, H, P]),
                                      ALU.mult).then_inc(joined[t], 1)
                for t in range(NT):
                    dve.wait_ge(crossed[t], v + 1)
                    dve.tensor_copy(XX[:, t], b(t)).then_inc(held[t], 1)
                for t in range(NT):
                    dve.wait_ge(closed[t], v + 1)
                    dve.tensor_tensor(Ti[:, t], Ti[:, t], b(2 + t), ALU.subtract)
                    op = dve.tensor_tensor(TT[:, t], TT[:, t], b(4 + t), ALU.subtract)
                after(op)

        @block.tensor
        def _(pe):
            for v in range(L):
                for t in range(NT):
                    pe.wait_ge(joined[t], v + 1)
                    for h in range(H):
                        last = pe.matmul(b(t)[:, h], CT[:, t, h], Ti[:, t, h], start=True, stop=True)
                    last.then_inc(crossed[t], 1)
                for t in range(NT):
                    pe.wait_ge(held[t], v + 1)
                    for h in range(H):
                        pe.matmul(b(2 + t)[:, h], TT[:, t, h], XX[:, t, h], start=True, stop=True)
                        last = pe.matmul(b(4 + t)[:, h], XX[:, t, h], TT[:, t, h], start=True, stop=True)
                    last.then_inc(closed[t], 1)


def short_conv(k, A, y):
    nc, T = k.nc, k.T
    with ExitStack() as own:
        sb = lambda name, shape: own.enter_context(nc.sbuf_tensor("sc_" + name, shape, F32))
        cw, u, cx = sb("cw", [P, 3, 4]), sb("u", [P, 12, T]), sb("cx", [P, 4, T + 2])
        ahead(k, "sc_ahead", k.W["sc_in"])
        gemm(k, "sc_in", k.hT, k.W["sc_in"], features_to(k, u), feature_major=True,
             then=k.W["nsa_in"],
             also=[(cw[:, j, :], column(A["conv_a_w"][0, j])) for j in range(3)])

        def body(dve, after):
            after(dve.memset(cx[:, :, 0:2], 0.0))
            after(dve.tensor_tensor(cx[:, :, 2:], u[:, 4:8, :], u[:, 8:12, :], ALU.mult))
            for j in range(3):
                for i in range(4):
                    if j == 0:
                        op = dve.tensor_scalar(y[:, i, :], cx[:, i, 0:T], cw[:, 0, i:i + 1], None, ALU.mult)
                    else:
                        op = dve.scalar_tensor_tensor(y[:, i, :], cx[:, i, j:j + T], cw[:, j, i:i + 1],
                                                      y[:, i, :], ALU.mult, ALU.add)
                after(op)
            dve.tensor_tensor(y[:], y[:], u[:, 0:4, :], ALU.mult)
        on_vector(k, "sc_conv", body)


def merge_branches(k, A, yT):
    nc, NT = k.nc, k.NT
    with ExitStack() as own:
        sb = lambda name, shape: own.enter_context(nc.sbuf_tensor("mb_" + name, shape, F32))
        gates, tmp, merged = sb("gates", [P, NT, 3072]), sb("tmp", [P, NT, BANK]), sb("merged", [P, NT, 1024])
        bias = sb("bias", [1, 3072])
        load(k, "mb_load", [(bias[:], A["b_gate"])])
        gemm(k, "mb_gates", k.hT, k.W["mb_gates"], tokens_to(k, gates), bias=bias,
             then=k.W["mb_branch0"])
        on_scalar(k, "mb_sig", lambda act, after: act.activation(gates[:], gates[:], ACT.Sigmoid))
        for r in range(3):
            branch = sb(f"branch{r}", [P, NT, 1024]) if r == 0 else branch
            gemm(k, f"mb_branch{r}", yT[r], k.W[f"mb_branch{r}"], tokens_to(k, branch),
             then=k.W[f"mb_branch{r + 1}" if r < 2 else "mb_out"])

            def weigh(dve, after, r=r):
                g = gates[:, :, r * 1024:(r + 1) * 1024]
                after(dve.tensor_tensor(merged[:] if r == 0 else branch[:], branch[:], g, ALU.mult))
                if r:
                    dve.tensor_tensor(merged[:], merged[:], branch[:], ALU.add)
            on_vector(k, f"mb_w{r}", weigh)
        transpose_in(k, "mb_t", merged, k.hT)
        gemm(k, "mb_out", k.hT, k.W["mb_out"], tokens_to(k, branch),
             then=k.W["rt_g"])
        on_vector(k, "mb_x", lambda dve, after: dve.tensor_tensor(k.X[:], k.X[:], branch[:], ALU.add))


def swiglu(k, name, w_in, w_out, HID, y, ada=None):
    nc, T, NT, ps = k.nc, k.T, k.NT, k.ps
    U, FT, KIND = 2, 2, 3
    n_blocks = HID // (FT * P)
    whole, rest = divmod(n_blocks, U)
    G, UP, D = range(KIND)
    raw_all = k.wring[:].rearrange("p a b -> p (a b)").rearrange("p (u j n) -> p u j n", u=U, j=KIND)
    AH = 1024
    with Stage(nc, name) as st:
        hi, lo = (st.sb(n, [P, KIND, 2048], F32R) for n in ("hi", "lo"))
        h_hi, h_lo = (st.sb(n, [P, 8, T], F32R) for n in ("h_hi", "h_lo"))
        silu, hidden = st.sb("silu", [P, FT, T]), st.sb("hidden", [P, FT, T])
        hid_hi, hid_lo = (st.sb(n, [P, U, FT, T], F32R) for n in ("hid_hi", "hid_lo"))
        landed = [[st.sem(f"landed{j}{u}") for u in range(U)] for j in range(KIND)]
        high = [st.sem(f"high{j}") for j in range(KIND)]
        split = [st.sem(f"split{j}") for j in range(KIND)]
        h_high, h_split = st.sem("h_high"), st.sem("h_split")
        gate_read, down_read = st.sem("gate_read"), st.sem("down_read")
        filled = [st.sem(f"filled{f}") for f in range(FT)]
        silued = [st.sem(f"silued{f}") for f in range(FT)]
        made = [st.sem(f"made{f}") for f in range(FT)]
        hid_high = [st.sem(f"hid_high{f}") for f in range(FT)]
        hid_split = [st.sem(f"hid_split{f}") for f in range(FT)]
        summed = st.sem("summed")
        if ada is not None:
            own = st.sb("aw", [P, 2, AH])
            aw = ([own[:, q, :] for q in range(2)] + [y[:, t, :] for t in range(2)]
                  + [k.mod[:, q * AH:(q + 1) * AH] for q in range(2)])
            ada_landed, ada_base = k.ffn_ada_landed, k.ffn_ada_base
            k.ffn_ada_base += 8 * 16
            ada_zeroed, ada_added = st.sem("ada_zeroed"), st.sem("ada_added")
        block = st.block()

        def steps(eng, step, n_ada=0):
            for u in range(U):
                step(0, u, u == 0, u == 1, n_ada > 0)
            for a, z in ((1, n_ada // U), (max(1, n_ada // U), whole)):
                if a < z:
                    with eng.Fori(a, z) as i:
                        for u in range(U):
                            step(i, u, False, False, a < n_ada // U)
            for u in range(rest):
                step(whole, u, False, False, False)
        N_ADA = 8 if ada is not None else 0

        @block.sync
        def _(sp):
            def fetch(i, u, first, second, _a):
                b = i * U + u
                for j in range(KIND):
                    if not (first or second):
                        sp.wait_ge(split[j], b - 1)
                    if j == D:
                        src = w_out[bass.ds(b * FT * P, FT * P), :]
                    else:
                        src = w_in[:, bass.ds(b * FT * P + j * HID, FT * P)]
                    sp.dma_start(raw_all[:, u, j, :].rearrange("p (k n) -> p k n", k=8 if j < D else FT),
                                 src.rearrange("(k p) n -> p k n", p=P)).then_inc(landed[j][u], 16)
            steps(sp, fetch)

        @block.gpsimd
        def _(pool):
            if ada is None:
                return
            pool.memset(k.ada[:], 0.0).then_inc(ada_zeroed, 1)

            def fetch(b, first):
                for q in range(6):
                    s, third = divmod(q, 3)
                    if not first:
                        pool.wait_ge(ada_added, b * 6 + q - 5)
                    pool.dma_start(aw[q], ada[s][bass.ds(b * P, P), third * AH:(third + 1) * AH]
                                   ).then_inc(ada_landed[q], 16)
            fetch(0, True)
            with pool.Fori(1, 8) as b:
                fetch(b, False)

        def product(pe, out, a_hi, a_lo, b_hi, b_lo, start, stop):
            pe.matmul(out, a_hi, b_hi, start=start, stop=False, skip_group_check=True)
            pe.matmul(out, a_hi, b_lo, start=False, stop=False, skip_group_check=True)
            return pe.matmul(out, a_lo, b_hi, start=False, stop=stop, skip_group_check=True)

        @block.tensor
        def _(pe):
            def gate_up(b, u, early):
                for f in range(FT):
                    bank = u * FT + f
                    if not early:
                        pe.wait_ge(made[f], b - 1)
                    for j in (G, UP):
                        if f == 0:
                            pe.wait_ge(split[j], b + 1)
                        for kt in range(8):
                            at = slice(kt * FT * P + f * P, kt * FT * P + (f + 1) * P)
                            last = product(pe, ps[:, bank, j * T:(j + 1) * T], hi[:, j, at], lo[:, j, at],
                                           h_hi[:, kt, :], h_lo[:, kt, :], kt == 0, kt == 7)
                        if j == G and f == FT - 1:
                            last.then_inc(gate_read, 1)
                    last.then_inc(filled[f], 1)

            def down(b, u, first, final):
                pe.wait_ge(split[D], b + 1)
                for f in range(FT):
                    pe.wait_ge(hid_split[f], b + 1)
                    for t in range(NT):
                        at = slice(t * P, (t + 1) * P)
                        for n in range(2):
                            cols = slice(f * 1024 + n * BANK, f * 1024 + (n + 1) * BANK)
                            last = product(pe, ps[:, 4 + 2 * t + n, :], hid_hi[:, u, f, at], hid_lo[:, u, f, at],
                                           hi[:, D, cols], lo[:, D, cols], first and f == 0,
                                           final and f == FT - 1)
                last.then_inc(down_read, 1)

            def step(i, u, first, second, _a):
                b = i * U + u
                gate_up(b, u, first or second)
                if not first:
                    down(b - 1, 1 - u, second, False)
            pe.wait_ge(h_split, 1)
            steps(pe, step)
            down(n_blocks - 1, (n_blocks - 1) % U, False, True)
            pe.matmul(ps[:, 0, :P], k.zero[:], k.ident[:], start=True, stop=True).then_inc(summed, 1)

        @block.scalar
        def _(act):
            def take(i, u, j):
                act.wait_ge(landed[j][u], i * 16 + 16)
                act.copy(hi[:, j, :], raw_all[:, u, j, :]).then_inc(high[j], 1)

            def last_down(i, u, first, second):
                if first:
                    return
                if not second:
                    act.wait_ge(down_read, i * U + u - 1)
                take(i if u else i - 1, 1 - u, D)

            def ahead(i, u):
                b = i * U + u
                act.wait_ge(gate_read, b + 1)
                take(i + u, 1 - u, G)
                act.wait_ge(filled[FT - 1], b + 1)
                take(i + u, 1 - u, UP)

            def make(i, u):
                b = i * U + u
                for f in range(FT):
                    act.wait_ge(filled[f], b + 1)
                    act.activation(silu[:, f, :], ps[:, u * FT + f, 0:T], ACT.Silu).then_inc(silued[f], 1)
                for f in range(FT):
                    act.wait_ge(made[f], b + 1)
                    act.copy(hid_hi[:, u, f, :], hidden[:, f, :]).then_inc(hid_high[f], 1)

            def step(i, u, first, second, _a, final=False):
                last_down(i, u, first, second)
                if not final:
                    ahead(i, u)
                make(i, u)
            act.copy(h_hi[:].rearrange("p k t -> p (k t)"), k.hT[:].rearrange("p k t -> p (k t)")
                     ).then_inc(h_high, 1)
            take(0, 0, G)
            take(0, 0, UP)
            assert rest == 1
            for u in range(U):
                step(0, u, u == 0, u == 1, False)
            with act.Fori(1, whole) as i:
                for u in range(U):
                    step(i, u, False, False, False)
            step(whole, 0, False, False, False, final=True)
            act.wait_ge(down_read, n_blocks - 1)
            take(whole, 0, D)

        @block.vector
        def _(dve):
            def take(b, u, j):
                dve.wait_ge(high[j], b + 1)
                dve.tensor_tensor(lo[:, j, :], raw_all[:, u, j, :], hi[:, j, :].bitcast(F32), ALU.subtract
                                  ).then_inc(split[j], 1)

            def modulation_rows(b, first, qs):
                for q in qs:
                    s, third = divmod(q, 3)
                    dve.wait_ge(ada_landed[q], ada_base + b * 16 + 16)
                    if not (first and q == 0):
                        dve.wait_ge(ada_added, b * 6 + q)
                    part = k.ada[:, s, third * AH:(third + 1) * AH]
                    dve.scalar_tensor_tensor(part, aw[q], k.c[:, bass.ds(b, 1)], part,
                                             ALU.mult, ALU.add).then_inc(ada_added, 1)

            def step(i, u, first, second, with_ada, final=False):
                b = i * U + u
                if not first:
                    take(b - 1, 1 - u, D)
                if with_ada:
                    modulation_rows(b, first, (0, 1, 2))
                if not final:
                    take(b + 1, 1 - u, G)
                    take(b + 1, 1 - u, UP)
                if with_ada:
                    modulation_rows(b, first, (3, 4, 5))
                for f in range(FT):
                    dve.wait_ge(silued[f], b + 1)
                    if not first:
                        dve.wait_ge(hid_split[f], b)
                    dve.tensor_tensor(hidden[:, f, :], silu[:, f, :], ps[:, u * FT + f, T:2 * T], ALU.mult
                                      ).then_inc(made[f], 1)
                for f in range(FT):
                    dve.wait_ge(hid_high[f], b + 1)
                    dve.tensor_tensor(hid_lo[:, u, f, :], hidden[:, f, :], hid_hi[:, u, f, :].bitcast(F32),
                                      ALU.subtract).then_inc(hid_split[f], 1)
            dve.wait_ge(h_high, 1)
            dve.tensor_tensor(h_lo[:].rearrange("p k t -> p (k t)"), k.hT[:].rearrange("p k t -> p (k t)"),
                              h_hi[:].rearrange("p k t -> p (k t)").bitcast(F32), ALU.subtract).then_inc(h_split, 1)
            take(0, 0, G)
            take(0, 0, UP)
            if ada is not None:
                dve.wait_ge(ada_zeroed, 1)
            for u in range(U):
                step(0, u, u == 0, u == 1, N_ADA > 0)
            split_at = max(1, N_ADA // U)
            if split_at > 1:
                with dve.Fori(1, split_at) as i:
                    for u in range(U):
                        step(i, u, False, False, True)
            with dve.Fori(split_at, whole) as i:
                for u in range(U):
                    step(i, u, False, False, False)
            step(whole, 0, False, False, False, final=True)
            take(n_blocks - 1, 0, D)
            dve.wait_ge(summed, 1)
            if ada is not None:
                dve.wait_ge(ada_added, 8 * 6)
            dve.tensor_copy(y[:].rearrange("p t n -> p (t n)"), ps[:, 4:8, :].rearrange("p b n -> p (b n)"))


def route(k, A, h, one, pick, perm, permT, fac, hg, flags):
    nc, T, NT, ps = k.nc, k.T, k.NT, k.ps
    NG, NE = 4, 8
    assert T <= 2 * P
    with ExitStack() as own:
        sb = lambda name, shape: own.enter_context(nc.sbuf_tensor("rt_" + name, shape, F32))
        lg, le = sb("lg", [P, NT, NG]), sb("le", [P, NT, NG * NE])
        bg, be = sb("bg", [P, NG]), sb("be", [P, NG * NE])
        mg, zg, d2, w1, w2 = (sb(n, [P, NT]) for n in ("mg", "zg", "d2", "w1", "w2"))
        m1, m2 = sb("m1", [P, NT]), sb("m2", [P, NT])
        cum = sb("cum", [P, NT, NE])
        ex = sb("ex", [P, NT, NG])
        mine, two = (sb(n, [P, NT, NE]) for n in ("mine", "two"))
        rank, late = sb("rank", [P, NT]), sb("late", [P, NT])
        count, slots, fl = sb("count", [P, NG]), sb("slots", [P, P]), sb("fl", [P, 2])
        gemm(k, "rt_g", k.hT, k.W["rt_g"], tokens_to(k, lg),
             then=k.W["rt_e"],
             also=[(bg[:], rows(A["b_router_group"][0])), (be[:], rows(A["b_router_expert"][0]))])
        gemm(k, "rt_e", k.hT, k.W["rt_e"], tokens_to(k, le))

        def first(dve, after, x, best, mask, n):
            for t in range(NT):
                after(dve.tensor_scalar(mask[:, t, :], x[:, t, :], best[:, t:t + 1], None, ALU.is_equal))
                after(dve.tensor_tensor_scan(cum[:, t, :n], k.ones[:, :n], mask[:, t, :], 0.0, ALU.mult, ALU.add))
                after(dve.scalar_tensor_tensor(mask[:, t, :], cum[:, t, :n], 1.0, mask[:, t, :],
                                               ALU.is_equal, ALU.mult))

        def choose(dve, after):
            after(dve.tensor_tensor(lg[:], lg[:], bg[:].unsqueeze(1).to_broadcast([P, NT, NG]), ALU.add))
            after(dve.tensor_tensor(le[:], le[:], be[:].unsqueeze(1).to_broadcast([P, NT, NG * NE]), ALU.add))
            after(dve.tensor_reduce(mg[:], lg[:], AX.X, ALU.max))
            first(dve, after, lg, mg, pick, NG)
            after(dve.tensor_tensor(ex[:], lg[:], mg[:].unsqueeze(2).to_broadcast([P, NT, NG]), ALU.subtract))
            for g in range(NG):
                for t in range(NT):
                    lt, pt = le[:, t, g * NE:(g + 1) * NE], pick[:, t, g:g + 1]
                    if g == 0:
                        op = dve.tensor_scalar(mine[:, t, :], lt, pt, None, ALU.mult)
                    else:
                        op = dve.scalar_tensor_tensor(mine[:, t, :], lt, pt, mine[:, t, :], ALU.mult, ALU.add)
                after(op)
            after(dve.tensor_reduce(m1[:], mine[:], AX.X, ALU.max))
            first(dve, after, mine, m1, one, NE)
            after(dve.scalar_tensor_tensor(mine[:], one[:], NEG, mine[:], ALU.mult, ALU.add))
            after(dve.tensor_reduce(m2[:], mine[:], AX.X, ALU.max))
            first(dve, after, mine, m2, two, NE)
            after(dve.tensor_tensor(d2[:], m2[:], m1[:], ALU.subtract))
        on_vector(k, "rt_choose", choose)

        def exps(act, after):
            act.activation(ex[:], ex[:], ACT.Exp)
            act.activation(d2[:], d2[:], ACT.Exp)
        on_scalar(k, "rt_exp", exps)

        def positions(pe):
            for t in range(NT):
                for r in range(t + 1):
                    pe.matmul(ps[:, 0, t * NG:(t + 1) * NG], k.upto[:] if r == t else k.ones[:], pick[:, r, :],
                              start=r == 0, stop=r == t)
                pe.matmul(ps[:, 1, :NG], k.ones[:], pick[:, t, :], start=t == 0, stop=t == NT - 1)
        on_tensor(k, "rt_pos", positions)
        on_gpsimd(k, "rt_slots", lambda pool, after: pool.iota(
            slots[:], pattern=[[1, P]], base=0, channel_multiplier=0, allow_small_or_imprecise_dtypes=True))

        def weights(dve, after):
            after(dve.tensor_reduce(zg[:], ex[:], AX.X, ALU.add))
            after(dve.scalar_tensor_tensor(w1[:], d2[:], 1.0, zg[:], ALU.add, ALU.mult))
            after(dve.reciprocal(w1[:], w1[:]))
            after(dve.tensor_tensor(w2[:], w1[:], d2[:], ALU.mult))
            by = lambda x: x[:].unsqueeze(2).to_broadcast([P, NT, NE])
            after(dve.tensor_tensor(one[:], one[:], by(w1), ALU.mult))
            after(dve.tensor_tensor(two[:], two[:], by(w2), ALU.mult))
            after(dve.tensor_tensor(one[:], one[:], two[:], ALU.add))
            after(dve.tensor_tensor(ex[:], ps[:, 0, :NT * NG].rearrange("p (t g) -> p t g", t=NT), pick[:], ALU.mult))
            after(dve.tensor_reduce(rank[:], ex[:], AX.X, ALU.add))
            after(dve.tensor_scalar(rank[:], rank[:], -1.0, None, ALU.add))
            after(dve.tensor_scalar(late[:], rank[:], -float(P), None, ALU.add))
            for t in range(NT):
                for j in range(NG):
                    dve.tensor_scalar(perm[:, t, j, :], slots[:], rank[:, t:t + 1], pick[:, t, j:j + 1],
                                      ALU.is_equal, ALU.mult)
                dve.tensor_scalar(perm[:, t, NG, :], slots[:], late[:, t:t + 1], None, ALU.is_equal)
            after(dve.tensor_scalar(count[:], ps[:, 1, :NG], float(P), None, ALU.is_gt))
            after(dve.tensor_reduce(fl[:, 0:1], count[:], AX.X, ALU.add))
            after(dve.tensor_tensor(count[:], count[:], slots[:, 0:NG], ALU.mult))
            after(dve.tensor_reduce(fl[:, 1:2], count[:], AX.X, ALU.add))
            after(dve.tensor_scalar(fl[:, 1:2], fl[:, 1:2], float(NE), None, ALU.mult))
            dve.tensor_copy(flags[:], fl[:])
        on_vector(k, "rt_weights", weights)

        def turn(pe):
            for j in range(NG + 1):
                for t in range(NT):
                    pe.transpose(ps[:, j // 2, j % 2 * T + t * P:j % 2 * T + (t + 1) * P], perm[:, t, j, :], k.ident[:])
                    pe.matmul(ps[:, 3, j * NE:(j + 1) * NE], perm[:, t, j, :], one[:, t, :],
                              start=t == 0, stop=t == NT - 1)
        on_tensor(k, "rt_turn", turn)
        on_vector(k, "rt_copy", lambda dve, after: [
            dve.tensor_copy(permT[:].rearrange("p j t -> p (j t)"),
                            ps[:, 0:3, :].rearrange("p b n -> p (b n)")[:, :(NG + 1) * T]),
            dve.tensor_copy(fac[:].rearrange("p j e -> p (j e)"), ps[:, 3, :(NG + 1) * NE])])
        with Stage(nc, "rt_gather") as st:
            filled, high, drained = st.sem("filled"), st.sem("high"), st.sem("drained")
            hg_hi, hg_lo = hg
            block = st.block()
            parts = [(j, q) for j in range(NG + 1) for q in range(2)]
            to = lambda x, j, q: x[:, j, 4 * q:4 * q + 4, :].rearrange("p k s -> p (k s)")

            @block.tensor
            def _(pe):
                for n, (j, q) in enumerate(parts):
                    if n >= 8:
                        pe.wait_ge(drained, n - 7)
                    for i in range(4):
                        kt = 4 * q + i
                        for t in range(NT):
                            last = pe.matmul(ps[:, n % 8, i * P:(i + 1) * P], h[:, t, kt * P:(kt + 1) * P],
                                             perm[:, t, j, :], start=t == 0, stop=t == NT - 1)
                    last.then_inc(filled, 1)

            @block.scalar
            def _(act):
                for n, (j, q) in enumerate(parts):
                    act.wait_ge(filled, n + 1)
                    act.copy(to(hg_hi, j, q), ps[:, n % 8, :]).then_inc(high, 1)

            @block.vector
            def _(dve):
                for n, (j, q) in enumerate(parts):
                    dve.wait_ge(high, n + 1)
                    dve.tensor_tensor(to(hg_lo, j, q), ps[:, n % 8, :], to(hg_hi, j, q).bitcast(F32), ALU.subtract
                                      ).then_inc(drained, 1)


def experts(k, name, A, tiles, fac, hg, sums, ada=None, flags=None):
    nc, NT, ps = k.nc, k.NT, k.ps
    U, FT, NE, HB = 2, 2, 8, 256
    wg, wu, wd = (A[f"w_expert_{n}"][0] for n in ("gate", "up", "down"))
    raw = k.wring[:].rearrange("p a b -> p (a b)").rearrange("p (u j n) -> p u j n", u=U, j=3)
    G, UP, D = range(3)
    hg_hi, hg_lo = hg
    with Stage(nc, name) as st:
        hi, lo = (st.sb(n, [P, 2, 2048], F32R) for n in ("hi", "lo"))
        idle = k.hT[:].rearrange("p k t -> p (k t)")
        silu, prod = (idle[:, i * U * HB:(i + 1) * U * HB].rearrange("p (u n) -> p u n", u=U) for i in range(2))
        hidT = idle[:, 2 * U * HB:3 * U * HB].rearrange("p (u f s) -> p u f s", u=U, f=FT)
        landed = [[st.sem(f"landed{j}{u}") for u in range(U)] for j in range(3)]
        high = [st.sem(f"high{j}") for j in range(2)]
        split = [st.sem(f"split{j}") for j in range(2)]
        filled = [st.sem("filled_g"), st.sem("filled_u")]
        silued, made = st.sem("silued"), st.sem("made")
        turned, copied = st.sem("turned"), st.sem("copied")
        applied = st.sem("applied")
        summed, kept = st.sem("summed"), st.sem("kept")
        if ada:
            aw = k.mod[:].rearrange("p (b n) -> p b n", b=2)
            ada_landed, ada_base = k.ada_landed, k.ada_base
            k.ada_base += 256
            ada_added = st.sem("ada_added")
            ada_w, cond, ada_sums = ada
        block = st.block()

        def guarded(eng, body):
            if flags is None:
                body(0)
                return
            any_late = eng.value_load(flags[0:1, 0:1], min_val=0, max_val=1)
            base = eng.value_load(flags[0:1, 1:2], min_val=0, max_val=24) if eng is nc.sync else 0
            with eng.If(any_late > 0):
                body(base)

        def steps(eng, expert):
            for m, j in enumerate(tiles):
                expert(0, m * NE, m, j)
                with eng.Fori(1, NE) as i:
                    expert(i, i + m * NE, m, j)

        @block.sync
        def _(sp):
            def program(base):
                def fetch(kind, e, n, u):
                    one, b = bass.ds(e, 1), n * U + u
                    if not isinstance(n, int) or n > 0:
                        sp.wait_ge(applied if kind == D else split[kind], b - 1)
                    flat = lambda x: x.rearrange("a k n -> (a k) n")
                    cut = slice(u * HB, (u + 1) * HB)
                    src = flat(wd[one, cut, :] if kind == D else (wg, wu)[kind][one, :, cut])
                    sp.dma_start(raw[:, u, kind, :].rearrange("p (k n) -> p k n", k=FT if kind == D else 8),
                                 src.rearrange("(k p) n -> p k n", p=P)).then_inc(landed[kind][u], 16)

                def expert(i, n, m, j):
                    e = i + (j * NE if flags is None else base)
                    for u in range(U):
                        for kind in (G, UP):
                            fetch(kind, e, n, u)
                        if u == 1:
                            fetch(D, e, n, 0)
                        elif not isinstance(n, int) or n > 0:
                            fetch(D, e - 1, n - 1 if not isinstance(n, int) or n > 1 else 0, 1)
                steps(sp, expert)
                last = (tiles[-1] * NE if flags is None else base) + NE - 1
                fetch(D, last, len(tiles) * NE - 1, 1)
            guarded(sp, program)

        @block.gpsimd
        def _(pool):
            if not ada:
                return
            def fetch(i, n, j, b, first):
                if not first:
                    pool.wait_ge(ada_added, n - 1)
                pool.dma_start(aw[:, b, :], ada_w[j // 2][bass.ds(i * P, P), (j % 2) * 1536:(j % 2 + 1) * 1536]
                               ).then_inc(ada_landed[b], 16)
            for m, j in enumerate(tiles):
                if m == 0:
                    for b in range(2):
                        fetch(b, b, j, b, True)
                with pool.Fori(1 if m == 0 else 0, NE // 2) as i:
                    for b in range(2):
                        fetch(i * 2 + b, i * 2 + b + m * NE, j, b, False)

        @block.tensor
        def _(pe):
            def body(kind, b, u, j, early):
                pe.wait_ge(split[kind], b + 1)
                if kind == G and not early:
                    pe.wait_ge(made, b - 1)
                out = ps[:, 2 * u + kind, :HB]
                for kt in range(8):
                    at = slice(kt * HB, (kt + 1) * HB)
                    x_hi, x_lo = hg_hi[:, j, kt, :], hg_lo[:, j, kt, :]
                    pe.matmul(out, x_hi, hi[:, kind, at], start=kt == 0, stop=False)
                    pe.matmul(out, x_hi, lo[:, kind, at], start=False, stop=False)
                    last = pe.matmul(out, x_lo, hi[:, kind, at], start=False, stop=kt == 7)
                last.then_inc(filled[kind], 1)

            def turn(b, u):
                pe.wait_ge(made, b + 1)
                for f in range(FT):
                    last = pe.transpose(ps[:, 6 + u, f * P:(f + 1) * P], prod[:, u, f * P:(f + 1) * P], k.ident[:])
                last.then_inc(turned, 1)

            def apply(n, u, fresh=False):
                b = n * U + u
                pe.wait_ge(landed[D][u], (n + 1) * 16)
                pe.wait_ge(copied, b + 1)
                for f in range(FT):
                    for c in range(2):
                        last = pe.matmul(ps[:, 4 + c, :], hidT[:, u, f, :],
                                         raw[:, u, D, f * 1024 + c * BANK:f * 1024 + (c + 1) * BANK],
                                         start=fresh and f == 0, stop=False, skip_group_check=True)
                last.then_inc(applied, 1)

            def close():
                for c in range(2):
                    last = pe.matmul(ps[:, 4 + c, :], k.zero[:], k.X[:, 0, c * BANK:(c + 1) * BANK],
                                     start=False, stop=True, skip_group_check=True)
                last.then_inc(summed, 1)

            def expert(i, n, m, j):
                peeled = isinstance(i, int)
                start = peeled and m == 0
                body(G, n * U, 0, j, start)
                if not start:
                    turn(n * U - 1, 1)
                body(UP, n * U, 0, j, start)
                if not start:
                    apply(n - 1, 1)
                    if peeled:
                        close()
                body(G, n * U + 1, 1, j, start)
                turn(n * U, 0)
                body(UP, n * U + 1, 1, j, start)
                if peeled and m > 0:
                    pe.wait_ge(kept, m)
                apply(n, 0, fresh=peeled)

            def program(base):
                steps(pe, expert)
                n = len(tiles) * NE - 1
                turn(n * U + 1, 1)
                apply(n, 1)
                close()
            guarded(pe, program)

        @block.scalar
        def _(act):
            def take(kind, n, u):
                act.wait_ge(landed[kind][u], (n + 1) * 16)
                act.copy(hi[:, kind, :], raw[:, u, kind, :]).then_inc(high[kind], 1)

            def copy(b, u):
                act.wait_ge(turned, b + 1)
                act.copy(hidT[:, u].rearrange("p f s -> p (f s)"), ps[:, 6 + u, :FT * P]).then_inc(copied, 1)

            def expert(i, n, m, j):
                for u in range(U):
                    b = n * U + u
                    if u == 1 or not isinstance(n, int) or n > 0:
                        copy(b - 1, 1 - u)
                    act.wait_ge(filled[G], b + 1)
                    take_next(G, n, u, j)
                    act.activation(silu[:, u, :], ps[:, 2 * u, :HB], ACT.Silu).then_inc(silued, 1)
                    act.wait_ge(filled[UP], b + 1)
                    take_next(UP, n, u, j)

            def take_next(kind, n, u, j):
                if u == 0:
                    take(kind, n, 1)
                else:
                    take(kind, n + 1, 0)

            def program(base):
                take(G, 0, 0)
                take(UP, 0, 0)
                total = len(tiles) * NE
                for m, j in enumerate(tiles):
                    expert(0, m * NE, m, j)
                    with act.Fori(1, NE if m < len(tiles) - 1 else NE - 1) as i:
                        expert(i, i + m * NE, m, j)
                n = total - 1
                for u in range(U):
                    b = n * U + u
                    copy(b - 1, 1 - u)
                    act.wait_ge(filled[G], b + 1)
                    if u == 0:
                        take(G, n, 1)
                    act.activation(silu[:, u, :], ps[:, 2 * u, :HB], ACT.Silu).then_inc(silued, 1)
                    act.wait_ge(filled[UP], b + 1)
                    if u == 0:
                        take(UP, n, 1)
                copy(n * U + 1, 1)
            guarded(act, program)

        @block.vector
        def _(dve):
            def take(kind, b, u):
                dve.wait_ge(high[kind], b + 1)
                dve.tensor_tensor(lo[:, kind, :], raw[:, u, kind, :], hi[:, kind, :].bitcast(F32), ALU.subtract
                                  ).then_inc(split[kind], 1)

            def expert(i, n, m, j, final=False):
                for u in range(U):
                    b = n * U + u
                    more = not (final and u == 1)
                    if more:
                        take(G, b + 1, 1 - u)
                    dve.wait_ge(filled[UP], b + 1)
                    dve.wait_ge(silued, b + 1)
                    dve.scalar_tensor_tensor(prod[:, u, :], silu[:, u, :], fac[:, j, bass.ds(i, 1)],
                                             ps[:, 2 * u + 1, :HB], ALU.mult, ALU.mult).then_inc(made, 1)
                    if more:
                        take(UP, b + 1, 1 - u)

            def pair(i2, m, j, first, final=False):
                for q in range(2):
                    i = i2 * 2 + q
                    expert(i, i + m * NE, m, j, final and q == 1)
                    if ada:
                        dve.wait_ge(ada_landed[q], ada_base + (i2 + m * NE // 2 + 1) * 16)
                        if not (first and q == 0):
                            dve.wait_ge(ada_added, i + m * NE)
                        part = ada_sums[:, j // 2, (j % 2) * 1536:(j % 2 + 1) * 1536]
                        dve.scalar_tensor_tensor(part, aw[:, q, :], cond[:, bass.ds(i, 1)], part,
                                                 ALU.mult, ALU.add).then_inc(ada_added, 1)
                    if q == 0 and isinstance(i2, int) and i2 == 0 and m > 0:
                        keep(m - 1)

            def keep(m):
                dve.wait_ge(summed, m + 1)
                dve.tensor_copy(sums[:, tiles[m], :], ps[:, 4:6, :].rearrange("p c n -> p (c n)")).then_inc(kept, 1)

            def program(base):
                take(G, 0, 0)
                take(UP, 0, 0)
                for m, j in enumerate(tiles):
                    last = m == len(tiles) - 1
                    pair(0, m, j, m == 0)
                    with dve.Fori(1, NE // 2 - 1 if last else NE // 2) as i2:
                        pair(i2, m, j, False)
                    if last:
                        pair(NE // 2 - 1, m, j, False, final=True)
                keep(len(tiles) - 1)
            guarded(dve, program)


def scatter(k, permT, sums, tiles):
    NT, ps = k.NT, k.ps

    def back(pe):
        for t in range(NT):
            for c in range(2):
                for j in range(tiles):
                    pe.matmul(ps[:, 2 * t + c, :], permT[:, j, t * P:(t + 1) * P], sums[:, j, c * BANK:(c + 1) * BANK],
                              start=j == 0, stop=j == tiles - 1)
    on_tensor(k, "scatter", back)
    on_vector(k, "scatter_add", lambda dve, after: dve.tensor_tensor(
        k.X[:].rearrange("p t n -> p (t n)"), k.X[:].rearrange("p t n -> p (t n)"),
        ps[:, 0:4, :].rearrange("p b n -> p (b n)"), ALU.add))


def hybrid_block(k, A, masks, scratch):
    nc, NT, T = k.nc, k.NT, k.T
    with ExitStack() as own:
        sb = lambda name, shape: own.enter_context(nc.sbuf_tensor("fb_" + name, shape, F32))
        gain = sb("gain", [P, 8])
        load(k, "fb_load", [(k.X[:], A["x"][0].rearrange("(t p) n -> p t n", p=P)),
                            (gain[:], column(A["norm_mix"][0])), (k.c[:], column(A["c_2"][0]))])
        on_scalar(k, "fb_cond", lambda act, after: act.activation(k.c[:], k.c[:], ACT.Silu))
        y = sb("y", [P, NT, 512])
        yT = [sb(f"yT{r}", [P, 4, T]) for r in range(3)]
        with nc.sbuf_tensor("fb_h", [P, NT, 1024], F32) as h:
            rms_rows(k, "fb_rms", k.X[:], h[:])
            transpose_in(k, "fb_hT", h, k.hT, scale=gain[:])
        short_conv(k, A, yT[0])
        sparse_attention(k, A, scratch, y)
        transpose_in(k, "fb_yn", y, yT[1], 4)
        gated_delta(k, A, masks, y)
        transpose_in(k, "fb_yg", y, yT[2], 4)
        merge_branches(k, A, yT)


def for_modulation(k, ctx):
    sb = lambda name, shape: ctx.enter_context(k.nc.sbuf_tensor(name, shape, F32))
    k.ada = sb("ada", [P, 2, 3072])
    k.ada_landed = [k.nc.alloc_semaphore(f"ada_landed{b}") for b in range(2)]
    k.ffn_ada_landed = [k.nc.alloc_semaphore(f"ffn_ada_landed{q}") for q in range(6)]
    k.ada_base = k.ffn_ada_base = 0
    k.mod = sb("mod", [P, 3072])


def moe_block(k, A):
    nc, NT, T = k.nc, k.NT, k.T
    with ExitStack() as own:
        sb = lambda name, shape, dt=F32: own.enter_context(nc.sbuf_tensor("moe_" + name, shape, dt))
        permT = sb("permT", [P, 5, T])
        fac, hg = sb("fac", [P, 5, 8]), [sb(n, [P, 5, 8, P], F32R) for n in ("hg_hi", "hg_lo")]
        flags, pick, one = sb("flags", [P, 2], I32), sb("pick", [P, NT, 4]), sb("one", [P, NT, 8])
        with (nc.sbuf_tensor("moe_h", [P, NT, 1024], F32) as h, nc.sbuf_tensor("moe_gain", [P, 1024], F32) as gain,
              nc.sbuf_tensor("moe_perm", [P, NT, 5, P], F32) as perm):
            load(k, "moe_load", [(gain[:], rows(A["norm_ffn"][0]))])
            rms_rows(k, "moe_rms", k.X[:], h[:], gain[:])
            transpose_in(k, "moe_hT", h, k.hT)
            route(k, A, h, one, pick, perm, permT, fac, hg, flags)
        sums = sb("sums", [P, 5, 1024])
        on_vector(k, "moe_zero", lambda dve, after: [dve.memset(sums[:, 4, :], 0.0), dve.memset(k.ada[:], 0.0)])
        experts(k, "moe", A, [0, 1, 2, 3], fac, hg, sums,
                ada=[[A["ada_w_2"][0, s] for s in range(2)], k.c, k.ada])
        experts(k, "late", A, [4], fac, hg, sums, flags=flags)
        scatter(k, permT, sums, 5)


ALPHA = 8 ** 0.25
ROPE_THETA = 500000.0


def modulation(k, name, site, bias):
    nc, ps = k.nc, k.ps
    N = 6
    with Stage(nc, name) as st:
        biased, filled = st.sem("biased"), st.sem("filled")
        block = st.block()

        @block.sync
        def _(sp):
            sp.dma_start(k.mod[:], rows(bias)).then_inc(biased, 16)

        @block.tensor
        def _(pe):
            for c in range(N):
                pe.matmul(ps[:, c, :], k.ones[:], k.ada[:, site, c * BANK:(c + 1) * BANK],
                          start=True, stop=True).then_inc(filled, 1)

        @block.vector
        def _(dve):
            dve.wait_ge(biased, 16)
            for c in range(N):
                dve.wait_ge(filled, c + 1)
                m = k.mod[:, c * BANK:(c + 1) * BANK]
                dve.scalar_tensor_tensor(m, ps[:, c, :], 0.0 if c < 2 else 1.0, m, ALU.add, ALU.add)


def modulate(k, name, h):
    shape = [P, k.NT, 1024]
    row = lambda i: k.mod[:, i * 1024:(i + 1) * 1024].unsqueeze(1).to_broadcast(shape)

    def body(dve, after):
        after(dve.tensor_tensor(h[:], k.X[:], row(1), ALU.mult))
        dve.tensor_tensor(h[:], h[:], row(0), ALU.add)
    on_vector(k, name + "_mod", body)
    transpose_in(k, name + "_hT", h, k.hT)


def residual_norm(k, name, y, g, b, site=None, bias=None, then=None):
    nc, T, NT, ps, X = k.nc, k.T, k.NT, k.ps, k.X
    gate = k.mod[:, 2048:3072]
    with Stage(nc, name) as st:
        gr, br = st.sb("g", [P, 1024]), st.sb("b", [P, 1024])
        mean, rstd, off = (st.sb(n, [P, NT]) for n in ("mean", "rstd", "off"))
        landed, small = st.sem("landed"), st.sem("small")
        step, step2 = st.sem("step"), st.sem("step2")
        added, squared, rooted, normed = (st.sem(n) for n in ("added", "squared", "rooted", "normed"))
        if site is not None:
            gb, cols = st.sb("gb", [P, 1024]), st.sb("cols", [P, 4, 8])
            summed, merged = st.sem("summed"), st.sem("merged")
            turned = [st.sem(f"turned{t}") for t in range(NT)]
        block = st.block()

        @block.sync
        def _(sp):
            if site is not None:
                with nc.allow_non_contiguous_dma("small vectors"):
                    sp.dma_start(cols[:, 0:2, :], bias[0:2048].rearrange("(a k p) -> p a k", p=P, a=2)
                                 ).then_inc(landed, 16)
                    sp.dma_start(cols[:, 2, :], column(g)).then_inc(landed, 16)
                    sp.dma_start(cols[:, 3, :], column(b)).then_inc(landed, 16)
                sp.dma_start(gb[:], rows(bias[2048:3072])).then_inc(landed, 16)
            sp.dma_start(gr[:], rows(g)).then_inc(landed, 16)
            sp.dma_start(br[:], rows(b)).then_inc(landed, 16)
            while then is not None and then.ahead < min(RING, len(then.units)):
                send(k, sp, then)
        N_LOADS = 16 * (2 if site is None else 6)

        @block.vector
        def _(dve):
            after = Chain(dve, step)
            for t in range(NT):
                after(dve.tensor_tensor(y[:, t], y[:, t], gate, ALU.mult))
                dve.scalar_tensor_tensor(X[:, t], X[:, t], ALPHA, y[:, t], ALU.mult, ALU.add).then_inc(added, 1)
            dve.wait_ge(landed, N_LOADS)
            if site is not None:
                dve.wait_ge(summed, 1)
                c, sums = cols, ps[:, 6, 0:16].rearrange("p (a k) -> p a k", a=2)
                after(dve.tensor_tensor(c[:, 0:2], c[:, 0:2], sums, ALU.add))
                after(dve.tensor_scalar(c[:, 1], c[:, 1], 1.0, None, ALU.add))
                after(dve.tensor_tensor(c[:, 2], c[:, 2], c[:, 1], ALU.mult))
                after(dve.tensor_tensor(c[:, 3], c[:, 3], c[:, 1], ALU.mult))
                dve.tensor_tensor(c[:, 3], c[:, 3], c[:, 0], ALU.add).then_inc(merged, 1)
                dve.scalar_tensor_tensor(gate, ps[:, 4:6, :].rearrange("p b n -> p (b n)"), 1.0, gb[:],
                                         ALU.add, ALU.add)
            for t in range(NT):
                dve.wait_ge(normed, t + 1)
                after(dve.tensor_tensor(X[:, t], y[:, t], gr[:], ALU.mult))
                dve.tensor_tensor(X[:, t], X[:, t], br[:], ALU.add)

        @block.scalar
        def _(act):
            for t in range(NT):
                act.wait_ge(added, t + 1)
                act.activation(y[:, t], X[:, t], ACT.Copy, scale=-1.0 / (1024 * 32), accum_out=mean[:, t:t + 1]
                               ).then_inc(small, 1)
                act.wait_ge(small, t + 1)
                act.activation(y[:, t], X[:, t], ACT.Square, scale=1.0 / 32, bias=mean[:, t:t + 1],
                               accum_out=rstd[:, t:t + 1]).then_inc(squared, 1)
            for t in range(NT):
                act.wait_ge(rooted, t + 1)
                act.activation(y[:, t], X[:, t], ACT.Identity, scale=rstd[:, t:t + 1], bias=off[:, t:t + 1]
                               ).then_inc(normed, 1)
            if site is not None:
                act.wait_ge(merged, 1)
                for i in range(8):
                    act.wait_ge(turned[NT - 1], i // 2 * 2 + 2)
                    act.activation(k.hT[:, i, :], ps[:, i // 2, i % 2 * T:(i % 2 + 1) * T], ACT.Identity,
                                   scale=cols[:, 2, i:i + 1], bias=cols[:, 3, i:i + 1])

        @block.gpsimd
        def _(pool):
            after = Chain(pool, step2)
            for t in range(NT):
                r, o = rstd[:, t:t + 1], off[:, t:t + 1]
                pool.wait_ge(squared, t + 1)
                after(pool.tensor_scalar(r, r, 1e-5, None, ALU.add))
                after(pool.tensor_tensor(r, r, k.nhalf[:, 0:1], ALU.pow))
                after(pool.tensor_tensor(o, mean[:, t:t + 1], r, ALU.mult))
                pool.tensor_scalar(o, o, 32.0, None, ALU.mult).then_inc(rooted, 1)

        @block.tensor
        def _(pe):
            if site is None:
                return
            for i in range(16):
                pe.matmul(ps[:, 6, i:i + 1], k.ada[:, site, i * P:(i + 1) * P], k.ones[:, 0:1], start=True, stop=True)
            for c in range(2):
                last = pe.matmul(ps[:, 4 + c, :], k.ones[:], k.ada[:, site, 2048 + c * BANK:2048 + (c + 1) * BANK],
                                 start=True, stop=True)
            last.then_inc(summed, 1)
            for t in range(NT):
                pe.wait_ge(normed, t + 1)
                for i in range(8):
                    at = i % 2 * T + t * P
                    pe.transpose(ps[:, i // 2, at:at + P], y[:, t, i * P:(i + 1) * P], k.ident[:]
                                 ).then_inc(turned[t], 1)


def mlstm(k, A, y):
    nc, T, NT, ps = k.nc, k.T, k.NT, k.ps
    H, DK, DV = 4, 128, 256
    with ExitStack() as own:
        sb = lambda name, shape: own.enter_context(nc.sbuf_tensor("ml_" + name, shape, F32))
        qkT, VO = sb("qkT", [P, 8, T]), sb("VO", [P, NT, 2056])
        bg, norm = sb("bg", [P, 8]), sb("norm", [P, 1024])
        gemm(k, "ml_qk", k.hT, k.W["ml_qk"], features_to(k, qkT), feature_major=True,
             then=k.W["ml_vo"],
             also=[(bg[:], rows(A["mlstm_b_gate_2"][0])), (norm[:], rows(A["mlstm_norm_2"][0]))])
        gemm(k, "ml_vo", k.hT, k.W["ml_vo"], tokens_to(k, VO),
             then=k.W["l0_out"])
        gt, ab, nf = sb("gt", [P, NT, 8]), sb("ab", [P, NT, H]), sb("nf", [P, NT, H])
        rep = sb("rep", [P, NT, 2, H, P])

        def pre(dve, after):
            after(dve.tensor_tensor(gt[:], VO[:, :, 2048:2056], bg[:].unsqueeze(1).to_broadcast([P, NT, 8]), ALU.add))
            after(dve.tensor_scalar(ab[:], gt[:, :, 4:8], -1.0, None, ALU.mult))
            after(dve.tensor_tensor(ab[:], ab[:], gt[:, :, 4:8], ALU.min))
        on_vector(k, "ml_p1", pre)

        def soft(act, after):
            after(act.activation(ab[:], ab[:], ACT.Exp))
            after(act.activation(ab[:], ab[:], ACT.Ln, bias=1.0))
            act.activation(VO[:, :, 1024:2048], VO[:, :, 1024:2048], ACT.Sigmoid)
        on_scalar(k, "ml_p2", soft)

        def repeat(dve, after):
            after(dve.tensor_scalar(nf[:], gt[:, :, 4:8], 0.0, None, ALU.min))
            after(dve.tensor_tensor(nf[:], ab[:], nf[:], ALU.subtract))
            dve.tensor_copy(rep[:, :, 0], gt[:, :, 0:4].unsqueeze(3).to_broadcast([P, NT, H, P]))
            dve.tensor_copy(rep[:, :, 1], nf[:].unsqueeze(3).to_broadcast([P, NT, H, P]))
        on_vector(k, "ml_p3", repeat)

        def rows_of_R(pe):
            for h in range(H):
                for t in range(NT):
                    out = ps[:, h // 2, (h % 2) * T + t * P:(h % 2) * T + (t + 1) * P]
                    pe.matmul(out, rep[:, t, 0, h], k.ident[:], start=True, stop=False)
                    for r in range(t):
                        pe.matmul(out, rep[:, r, 1, h], k.ones[:], start=False, stop=False)
                    pe.matmul(out, rep[:, t, 1, h], k.upto[:], start=False, stop=True)
            for t in range(NT):
                for r in range(t + 1):
                    pe.matmul(ps[:, 2, t * H:(t + 1) * H], k.upto[:] if r == t else k.ones[:], nf[:, r, :],
                              start=r == 0, stop=r == t)
        on_tensor(k, "ml_R", rows_of_R)
        W, c, em = sb("W", [P, NT, H, T]), sb("c", [P, NT, H]), sb("em", [P, NT, H])

        def weights(dve, after):
            for t in range(NT):
                after(dve.tensor_tensor(W[:, t], ps[:, 0:2, :].rearrange("p b (h s) -> p (b h) s", s=T),
                                        k.causal[:, t, :].unsqueeze(1).to_broadcast([P, H, T]), ALU.add))
            after(dve.tensor_reduce(c[:], W[:], AX.X, ALU.max))
            after(dve.tensor_scalar(c[:], c[:], 0.0, None, ALU.max))
            dve.tensor_tensor(W[:], W[:], c[:].unsqueeze(3).to_broadcast([P, NT, H, T]), ALU.subtract)
            dve.tensor_tensor(em[:], ps[:, 2, :NT * H].rearrange("p (t h) -> p t h", t=NT), c[:], ALU.subtract)
        on_vector(k, "ml_W", weights)
        on_scalar(k, "ml_E", lambda act, after: [act.activation(W[:], W[:], ACT.Exp),
                                                 act.activation(em[:], em[:], ACT.Exp)])
        den, PT = sb("den", [P, NT, H]), sb("PT", [P, H, T])
        for t in range(NT):
            n = (t + 1) * P
            on_tensor(k, f"ml_s{t}", lambda pe, t=t, n=n: [pe.matmul(
                ps[:, h // 2, (h % 2) * T:(h % 2) * T + n], qkT[:, h, t * P:(t + 1) * P], qkT[:, 4 + h, :n],
                start=True, stop=True) for h in range(H)])

            def weigh(dve, after, t=t, n=n):
                s = W[:, t, :, :n]
                after(dve.scalar_tensor_tensor(s, ps[:, 0:2, :].rearrange("p b (h s) -> p (b h) s", s=T)[:, :, :n],
                                               DK ** -0.5, s, ALU.mult, ALU.mult))
                after(dve.tensor_reduce(den[:, t], s, AX.X, ALU.add))
                after(dve.tensor_scalar(c[:, t], den[:, t], -1.0, None, ALU.mult))
                after(dve.tensor_tensor(den[:, t], den[:, t], c[:, t], ALU.max))
                after(dve.tensor_tensor(den[:, t], den[:, t], em[:, t], ALU.max))
                after(dve.reciprocal(den[:, t], den[:, t]))
            on_vector(k, f"ml_w{t}", weigh)
            on_tensor(k, f"ml_t{t}", lambda pe, t=t: [pe.transpose(
                ps[:, h // 2, (h % 2) * T + r * P:(h % 2) * T + (r + 1) * P], W[:, t, h, r * P:(r + 1) * P],
                k.ident[:]) for h in range(H) for r in range(t + 1)])
            on_vector(k, f"ml_c{t}", lambda dve, after, n=n: dve.tensor_copy(
                PT[:, :, :n], ps[:, 0:2, :].rearrange("p b (h s) -> p (b h) s", s=T)[:, :, :n]))

            def apply(pe, t=t):
                for h in range(H):
                    for r in range(t + 1):
                        pe.matmul(ps[:, 2 + h // 2, (h % 2) * DV:(h % 2 + 1) * DV], PT[:, h, r * P:(r + 1) * P],
                                  VO[:, r, h * DV:(h + 1) * DV], start=r == 0, stop=r == t)
            on_tensor(k, f"ml_a{t}", apply)
            on_vector(k, f"ml_o{t}", lambda dve, after, t=t: dve.tensor_tensor(
                y[:, t].rearrange("p (h d) -> p h d", h=H), ps[:, 2:4, :].rearrange("p b (h d) -> p (b h) d", d=DV),
                den[:, t].unsqueeze(2).to_broadcast([P, H, DV]), ALU.mult))
        rms_rows(k, "ml_n", y[:], y[:], groups=H)

        def gated(dve, after):
            after(dve.tensor_tensor(y[:], y[:], norm[:].unsqueeze(1).to_broadcast([P, NT, 1024]), ALU.mult))
            dve.tensor_tensor(y[:], y[:], VO[:, :, 1024:2048], ALU.mult)
        on_vector(k, "ml_y", gated)


def rope_tables(k, positions, cos, sin):
    nc, NT, half = k.nc, k.NT, 8
    with ExitStack() as own:
        sb = lambda name, shape, dt=F32: own.enter_context(nc.sbuf_tensor("rp_" + name, shape, dt))
        pi, pf = sb("pi", [P, NT], I32), sb("pf", [P, NT])
        ang, turns, whole = sb("ang", [P, NT, half]), sb("turns", [P, NT, half]), sb("whole", [P, NT, half], I32)
        load(k, "rp_load", [(pi[:], positions.rearrange("(t p) -> p t", p=P))])
        c1 = 6.28125
        c2 = float(np.float32(np.round((2 * math.pi - c1) * 2 ** 20) / 2 ** 20))
        c3 = 2 * math.pi - c1 - c2

        def body(dve, after):
            after(dve.tensor_copy(pf[:], pi[:]))
            for i in range(half):
                inv = float(np.float32(ROPE_THETA ** (-i * 2.0 / 16)))
                op = dve.tensor_scalar(ang[:, :, i], pf[:], inv, None, ALU.mult)
            after(op)
            for dst, quarter in ((cos, 0.25), (sin, 0.0)):
                after(dve.tensor_scalar(turns[:], ang[:], 1 / (2 * math.pi), quarter, ALU.mult, ALU.add))
                after(dve.tensor_copy(whole[:], turns[:]))
                after(dve.tensor_copy(turns[:], whole[:]))
                after(dve.scalar_tensor_tensor(dst[:], turns[:], -c1, ang[:], ALU.mult, ALU.add))
                after(dve.scalar_tensor_tensor(dst[:], turns[:], -c2, dst[:], ALU.mult, ALU.add))
                after(dve.scalar_tensor_tensor(dst[:], turns[:], -c3, dst[:], ALU.mult, ALU.add))
                after(dve.tensor_scalar(dst[:], dst[:], quarter * 2 * math.pi, math.pi, ALU.add, ALU.min))
                after(dve.tensor_scalar(dst[:], dst[:], -math.pi, None, ALU.max))
        on_vector(k, "rp_ang", body)
        on_scalar(k, "rp_sin", lambda act, after: [act.activation(cos[:], cos[:], ACT.Sin),
                                                   act.activation(sin[:], sin[:], ACT.Sin)])


def rotate(k, name, x, heads, cos, sin, tmp):
    shape = [P, k.NT, heads, 8]
    v = x.rearrange("p t (h d) -> p t h d", h=heads)
    x1, x2 = v[:, :, :, 0:8], v[:, :, :, 8:16]
    c, s = (z[:].unsqueeze(2).to_broadcast(shape) for z in (cos, sin))

    def body(dve, after):
        dve.tensor_tensor(tmp[:, 0], x1, c, ALU.mult)
        dve.tensor_tensor(tmp[:, 1], x2, s, ALU.mult)
        dve.tensor_tensor(tmp[:, 2], x2, c, ALU.mult)
        after(dve.tensor_tensor(tmp[:, 3], x1, s, ALU.mult))
        dve.tensor_tensor(x1, tmp[:, 0], tmp[:, 1], ALU.subtract)
        dve.tensor_tensor(x2, tmp[:, 2], tmp[:, 3], ALU.add)
    on_vector(k, name, body)


def windowed(k, A, cos, sin, y):
    nc, T, NT = k.nc, k.T, k.NT
    H, G, D = 16, 2, 64
    with ExitStack() as own:
        sb = lambda name, shape: own.enter_context(nc.sbuf_tensor("wa_" + name, shape, F32))
        U, KD = sb("U", [P, NT, 1280]), sb("KD", [P, NT, G, 2, D])
        qT, kT = sb("qT", [P, 8, T]), sb("kT", [P, G, T])
        band, sinks, tmp = sb("band", [P, NT, T]), sb("sinks", [P, H]), sb("tmp", [P, 4, NT, 18, 8])
        gemm(k, "wa_in", k.hT, k.W["wa_in"], tokens_to(k, U),
             then=k.W["l1_out"],
             also=[(sinks[:], rows(A["swa_sinks_2"][0]))])
        rotate(k, "wa_rope", U[:, :, 0:1152], 18, cos, sin, tmp)

        def mask(pool, after):
            for t in range(NT):
                pool.affine_select(out=band[:, t, :], in_=k.causal[:, t, :], compare_op=ALU.is_gt, fill=NEG,
                                   base=P - t * P, pattern=[[1, T]], channel_multiplier=-1)
        on_gpsimd(k, "wa_mask", mask)
        on_vector(k, "wa_twice", lambda dve, after: [dve.tensor_copy(
            KD[:, :, :, u, :], U[:, :, 1024:1152].rearrange("p t (g d) -> p t g d", g=G)) for u in range(2)])
        transpose_in(k, "wa_qT", U, qT, 8, factor=D ** -0.5)
        transpose_in(k, "wa_kT", None, kT, G, src_cols=lambda t, i: KD[:, t, i].rearrange("p u d -> p (u d)"))
        half = lambda h: slice((h % 2) * D, (h % 2 + 1) * D)
        attention(k, "wa_a", [(list(range(h, h + 4)), t) for t in range(NT) for h in range(0, H, 4)],
                  q_of=lambda h, t: qT[half(h), h // 2, t * P:(t + 1) * P],
                  k_of=lambda h, kt: kT[half(h), h // 8, kt * P:(kt + 1) * P],
                  v_of=lambda h, kt: U[:, kt, 1152 + (h // 8) * D:1152 + (h // 8 + 1) * D],
                  bias_of=lambda hs, t: band[:, t, :(t + 1) * P].unsqueeze(1).to_broadcast([P, 4, (t + 1) * P]),
                  out_of=lambda hs, t: y[:, t, hs[0] * D:(hs[-1] + 1) * D].rearrange("p (g d) -> p g d", d=D),
                  dv=D, sink_of=lambda hs: sinks[:, hs[0]:hs[-1] + 1])


def hgrn(k, A, masks, layer, y):
    nc, T, NT, ps = k.nc, k.T, k.NT, k.ps
    H, D = 8, 128
    LV = 8
    with ExitStack() as own:
        sb = lambda name, shape: own.enter_context(nc.sbuf_tensor("hg_" + name, shape, F32))
        QF, IG = sb("QF", [P, 16, T]), sb("IG", [P, NT, 2048])
        lo, norm = sb("lo", [P, 4, 8]), sb("norm", [P, 1024])
        lb, lc, mx = sb("lb", [P, 8]), sb("lc", [P, 8]), sb("mx", [P, 8])
        gemm(k, "hg_qf", k.hT, k.W["hg_qf"], features_to(k, QF), feature_major=True,
             then=k.W["hg_ig"],
             also=[(lo[:, i, :], column(A["hgrn_lower_bounds_2"][i])) for i in range(4)] + [(norm[:], rows(A["hgrn_norm_2"][0]))])
        gemm(k, "hg_ig", k.hT, k.W["hg_ig"], tokens_to(k, IG),
             then=k.W["l2_out"])
        K, cf = sb("K", [P, H, T]), sb("cf", [P, H, T])
        E, QE_ = sb("E", [P, 2, H, T]), sb("QE", [P, H, T])
        assert len(k.W["l2_out"].units) + 2 <= RING
        wide = lambda x: x.rearrange("p (h t) -> p h t", h=H)
        QE = [QE_[:], wide(k.ring[:, k.sent % RING, :])]
        KE = [QF[:, 8:16, :], wide(k.ring[:, (k.sent + 1) % RING, :])]
        aT, aX = sb("aT", [P, NT, H, P]), sb("aX", [P, H, P])
        on_vector(k, "hg_l1", lambda dve, after: [
            after(dve.tensor_reduce(mx[:], lo[:].rearrange("p l i -> p i l"), AX.X, ALU.max)),
            after(dve.tensor_tensor(lo[:], lo[:], mx[:].unsqueeze(1).to_broadcast([P, 4, 8]), ALU.subtract))])
        on_scalar(k, "hg_l2", lambda act, after: [
            act.activation(lo[:], lo[:], ACT.Exp),
            act.activation(K[:], QF[:, 8:16, :], ACT.Exp, scale=-1.0)])
        Q = QF[:, 0:8, :]
        wide_ = lambda x: x[:].unsqueeze(2).to_broadcast([P, H, T])
        F = QF[:, 8:16, :]

        def gates(dve, after):
            after(dve.tensor_reduce(mx[:], lo[:].rearrange("p l i -> p i l"), AX.X, ALU.add))
            after(dve.reciprocal(mx[:], mx[:]))
            after(dve.tensor_reduce(lb[:], lo[:, 1:layer + 1].rearrange("p l i -> p i l"), AX.X, ALU.add))
            after(dve.tensor_tensor(lb[:], lb[:], mx[:], ALU.mult))
            after(dve.tensor_scalar(lc[:], lb[:], -1.0, 1.0, ALU.mult, ALU.add))
            after(dve.tensor_scalar(K[:], K[:], 1e30, None, ALU.min))
            after(dve.tensor_scalar(F, K[:], 1.0, None, ALU.add))
            after(dve.reciprocal(F, F))
            after(dve.tensor_tensor(F, F, wide_(lc), ALU.mult))
            after(dve.tensor_tensor(K[:], K[:], F, ALU.mult))
            after(dve.tensor_tensor(F, F, wide_(lb), ALU.add))
            after(dve.memset(aT[:], 0.0))
        on_vector(k, "hg_g", gates)
        on_scalar(k, "hg_ln", lambda act, after: act.activation(F, F, ACT.Ln))

        def running(dve, after):
            for h in range(H):
                dve.tensor_tensor_scan(cf[:, h, :], k.onesT[:], F[:, h, :], 0.0, ALU.mult, ALU.add)
        on_vector(k, "hg_cf", running)

        with Stage(nc, "hg_lv") as st:
            step, ready = st.sem("step"), st.sem("ready")
            spread, raised = st.sem("spread"), st.sem("raised")
            scaled, multiplied, taken = st.sem("scaled"), st.sem("multiplied"), st.sem("taken")
            block = st.block()

            def cut(x, v):
                b = 2 ** v
                z = x.rearrange("p h (n u j) -> p h n u j", u=2, j=b)
                return z[:, :, :, 0, :], z[:, :, :, 1, :]

            @block.vector
            def _(dve):
                def exponents(v):
                    b, n = 2 ** v, T // 2 ** (v + 1)
                    c0, c1 = cut(cf[:], v)
                    e0, e1 = cut(E[:, v % 2], v)
                    mid = c0[:, :, :, b - 1:b]
                    if n == 1:
                        c0, c1, e0, e1, mid = (z[:, :, 0, :] for z in (c0, c1, e0, e1, mid))
                        mid = mid.to_broadcast([P, H, b])
                    else:
                        mid = mid.to_broadcast([P, H, n, b])
                    dve.tensor_tensor(e0, mid, c0, ALU.subtract)
                    dve.tensor_tensor(e1, c1, mid, ALU.subtract).then_inc(spread, 1)

                def scale(v):
                    if v >= 2:
                        dve.wait_ge(multiplied, v - 1)
                    dve.wait_ge(raised, v + 1)
                    dve.tensor_tensor(QE[v % 2], Q, E[:, v % 2], ALU.mult)
                    dve.tensor_tensor(KE[v % 2], K[:], E[:, v % 2], ALU.mult).then_inc(scaled, 1)

                def take(v, mask):
                    dve.wait_ge(multiplied, v + 1)
                    if v >= 1:
                        dve.wait_ge(taken, v)
                    psum = ps[:, 4 * (v % 2):4 * (v % 2) + 4, :].rearrange("p b (h c) -> p (b h) c", c=P)
                    if v == LV - 1:
                        op = dve.tensor_copy(aX[:], psum[:, :H])
                    else:
                        op = dve.copy_predicated(
                            aT[:].rearrange("p t h c -> p (t h) c"),
                            mask.bitcast(mybir.dt.uint32).unsqueeze(1).to_broadcast([P, NT * H, P]), psum)
                    op.then_inc(taken, 1)

                exponents(0)
                for v in range(LV):
                    if v + 1 < LV:
                        if v >= 1:
                            dve.wait_ge(scaled, v)
                        exponents(v + 1)
                    scale(v)
                    if v >= 1:
                        take(v - 1, masks[:, v - 1, :])
                take(LV - 1, None)
                take(LV, k.ident[:])

            @block.scalar
            def _(act):
                for v in range(LV):
                    act.wait_ge(spread, v + 1)
                    act.activation(E[:, v % 2], E[:, v % 2], ACT.Exp).then_inc(raised, 1)

            @block.tensor
            def _(pe):
                for v in range(LV + 1):
                    if v < LV:
                        pe.wait_ge(scaled, v + 1)
                    if v >= 2:
                        pe.wait_ge(taken, v - 1)
                    out = lambda i: ps[:, 4 * (v % 2) + i // 4, i % 4 * P:(i % 4 + 1) * P]
                    ke, qe = (KE[v % 2], QE[v % 2]) if v < LV else (K[:], Q)
                    for h in range(H):
                        if v == LV - 1:
                            last = pe.matmul(out(h), ke[:, h, 0:P], qe[:, h, P:T], start=True, stop=True)
                        else:
                            for t in range(NT):
                                at = slice(t * P, (t + 1) * P)
                                last = pe.matmul(out(t * H + h), ke[:, h, at], qe[:, h, at], start=True, stop=True)
                    last.then_inc(multiplied, 1)

        def apply(pe):
            for h in range(H):
                v = lambda t: IG[:, t, h * D:(h + 1) * D]
                o = lambda t: ps[:, 2 * t + h // 4, h % 4 * D:(h % 4 + 1) * D]
                pe.matmul(o(0), aT[:, 0, h], v(0), start=True, stop=True)
                pe.matmul(o(1), aX[:, h], v(0), start=True, stop=False)
                pe.matmul(o(1), aT[:, 1, h], v(1), start=False, stop=True)
        on_tensor(k, "hg_pv", apply)
        on_scalar(k, "hg_silu", lambda act, after: [
            act.activation(IG[:, :, 1024:2048], IG[:, :, 1024:2048], ACT.Silu)])
        on_vector(k, "hg_o", lambda dve, after: dve.tensor_copy(
            y[:].rearrange("p t n -> p (t n)"), ps[:, 0:4, :].rearrange("p b n -> p (b n)")))
        rms_rows(k, "hg_n", y[:], y[:], groups=H, sq=E[:, 0].rearrange("p h (t d) -> p t h d", t=NT))

        def gated(dve, after):
            after(dve.tensor_tensor(y[:], y[:], norm[:].unsqueeze(1).to_broadcast([P, NT, 1024]), ALU.mult))
            dve.tensor_tensor(y[:], y[:], IG[:, :, 1024:2048], ALU.mult)
        on_vector(k, "hg_y", gated)


def differential(k, A, cos, sin, layer, y):
    nc, T, NT = k.nc, k.T, k.NT
    H, D = 8, 64
    lam_init = 0.8 - 0.6 * math.exp(-0.3 * layer)
    with ExitStack() as own:
        sb = lambda name, shape: own.enter_context(nc.sbuf_tensor("df_" + name, shape, F32))
        U = sb("U", [P, NT, 3072])
        lv, gain = sb("lv", [P, 4, D]), sb("gain", [P, 2 * D])
        pr, lam = sb("pr", [P, 2, D]), sb("lam", [P, 2])
        gemm(k, "df_in", k.hT, k.W["df_in"], tokens_to(k, U),
             then=k.W["l3_out"],
             also=[(lv[:], A["diff_lambda_2"][0].partition_broadcast(P)), (gain[:], rows(A["diff_norm_2"][0]))])
        qT, kT, tmp = sb("qT", [P, 8, T]), sb("kT", [P, 8, T]), sb("tmp", [P, 4, NT, 32, 8])
        rotate(k, "df_rope", U[:, :, 0:2048], 32, cos, sin, tmp)

        def dots(dve, after):
            dve.tensor_tensor(pr[:, 0], lv[:, 0], lv[:, 1], ALU.mult)
            after(dve.tensor_tensor(pr[:, 1], lv[:, 2], lv[:, 3], ALU.mult))
            after(dve.tensor_reduce(lam[:], pr[:], AX.X, ALU.add))
        on_vector(k, "df_l1", dots)
        on_scalar(k, "df_l2", lambda act, after: act.activation(lam[:], lam[:], ACT.Exp))

        def lam_of(dve, after):
            after(dve.tensor_tensor(lam[:, 0:1], lam[:, 1:2], lam[:, 0:1], ALU.subtract))
            after(dve.tensor_scalar(lam[:, 0:1], lam[:, 0:1], -lam_init, None, ALU.add))
        on_vector(k, "df_l3", lam_of)
        transpose_in(k, "df_qT", U, qT, 8, factor=D ** -0.5)
        transpose_in(k, "df_kT", U[:, :, 1024:2048], kT, 8)
        half = lambda h: slice((h % 2) * D, (h % 2 + 1) * D)
        attention(k, "df_a", [(list(range(h, h + 4)), t) for t in range(NT) for h in range(0, 2 * H, 4)],
                  q_of=lambda h, t: qT[half(h), h // 2, t * P:(t + 1) * P],
                  k_of=lambda h, kt: kT[half(h), h // 2, kt * P:(kt + 1) * P],
                  v_of=lambda h, kt: U[:, kt, 2048 + (h // 2) * 2 * D:2048 + (h // 2 + 1) * 2 * D],
                  bias_of=lambda hs, t: k.causal[:, t, :(t + 1) * P].unsqueeze(1).to_broadcast([P, 4, (t + 1) * P]),
                  out_of=lambda hs, t: y[:, t, hs[0] * D:(hs[-1] + 1) * D].rearrange("p (g d) -> p g d", d=2 * D),
                  dv=2 * D, minus=lambda g: lam[:, 0:1])
        rms_rows(k, "df_n", y[:], y[:], gain[:], groups=H, factor=1.0 - lam_init)


def projections(A):
    w = A["w_in"][0]
    ml, hg = A["mlstm_w_in_2"][0], A["hgrn_w_in_2"][0]
    outs = ["mlstm_w_out_2", "swa_w_out_2", "hgrn_w_out_2", "diff_w_out_2"]
    return {
        "sc_in": Weights(w[:, 0:1536], 8, 1536), "nsa_in": Weights(w[:, 1536:2840], 8, 1304),
        "gdn_in": Weights(w[:, 2840:4376], 8, 1536), "gdn_z": Weights(w[:, 4376:4896], 8, 520),
        "mb_gates": Weights(A["w_gate"][0], 8, 3072),
        **{f"mb_branch{r}": Weights(A["w_branch"][0, r], 4, 1024) for r in range(3)},
        "mb_out": Weights(A["w_out"][0], 8, 1024),
        "rt_g": Weights(A["w_router_group"][0], 8, 4), "rt_e": Weights(A["w_router_expert"][0], 8, 32),
        "ml_qk": Weights(ml[:, 0:1024], 8, 1024), "ml_vo": Weights(ml[:, 1024:3080], 8, 2056),
        "wa_in": Weights(A["swa_w_in_2"][0], 8, 1280), "df_in": Weights(A["diff_w_in_2"][0], 8, 3072),
        "hg_qf": Weights(hg[:, 0:2048], 8, 2048), "hg_ig": Weights(hg[:, 2048:4096], 8, 2048),
        **{f"l{i}_out": Weights(A[outs[i]][0], 8, 1024) for i in range(4)},
    }


def second_block(k, A, masks):
    nc, T, NT = k.nc, k.T, k.NT
    with ExitStack() as own:
        sb = lambda name, shape: own.enter_context(nc.sbuf_tensor("sb_" + name, shape, F32))
        k.onesT = sb("onesT", [P, T])
        k.causal = sb("causal", [P, NT, T])
        cos, sin = sb("cos", [P, NT, 8]), sb("sin", [P, NT, 8])
        y = sb("y", [P, NT, 1024])
        on_vector(k, "sb_ones", lambda dve, after: dve.memset(k.onesT[:], 1.0))

        def mask(pool, after):
            after(pool.memset(k.causal[:], 0.0))
            for t in range(NT):
                pool.affine_select(out=k.causal[:, t, :], in_=k.causal[:, t, :], compare_op=ALU.is_ge, fill=NEG,
                                   base=t * P, pattern=[[-1, T]], channel_multiplier=1)
        on_gpsimd(k, "sb_causal", mask)
        rope_tables(k, A["positions_2"][0], cos, sin)
        mixers = [lambda: mlstm(k, A, y), lambda: windowed(k, A, cos, sin, y),
                  lambda: hgrn(k, A, masks, 2, y), lambda: differential(k, A, cos, sin, 3, y)]
        inputs = ["ml_qk", "wa_in", "hg_qf", "df_in"]
        for i in range(4):
            if i == 0:
                modulation(k, "l0_ada0", 0, A["ada_b_2"][0, 0])
                ahead(k, "l0_ahead", k.W["ml_qk"])
                modulate(k, "l0_m0", y)
            mixers[i]()
            transpose_in(k, f"l{i}_yT", y, k.hT)
            gemm(k, f"l{i}_out", k.hT, k.W[f"l{i}_out"], tokens_to(k, y))
            residual_norm(k, f"l{i}_n0", y, A["ln_g_2"][i, 0], A["ln_b_2"][i, 0],
                          1, A["ada_b_2"][i, 1])
            if k.stop == (i, 0):
                return
            swiglu(k, f"l{i}_ffn", A["ffn_w_in_2"][i], A["ffn_w_out_2"][i], 2816, y,
                   ada=[A["ada_w_2"][i + 1, s] for s in range(2)] if i < 3 else None)
            residual_norm(k, f"l{i}_n1", y, A["ln_g_2"][i, 1], A["ln_b_2"][i, 1],
                          *((0, A["ada_b_2"][i + 1, 0], k.W[inputs[i + 1]]) if i < 3 else ()))
            if k.stop == (i, 1):
                return


def program(nc, A, out):
    T = A["x"].shape[1]
    scratch = nc.dram_tensor("compress_rows", [2, 2, T, 64], F32, kind="Internal").ap()
    with ExitStack() as ctx:
        k = persistent(nc, ctx, T)
        k.W = projections(A)
        masks = ctx.enter_context(nc.sbuf_tensor("masks", [P, 7, P], F32))
        level_masks(k, masks)
        hybrid_block(k, A, masks, scratch)
        for_modulation(k, ctx)
        moe_block(k, A)
        second_block(k, A, masks)
        dump(k, "store", [(out[0].rearrange("(t p) n -> p t n", p=P), k.X[:])])


def kernel(**inputs):
    import numpy as _np
    import concourse.bacc as _bacc
    from concourse import mybir as _mybir
    from concourse.bass_utils import run_bass_kernel_spmd as _run

    nc = _bacc.Bacc("TRN2", target_bir_lowering=False, num_devices=1)
    arrays, aps = {}, {}
    for name, value in inputs.items():
        a = _np.ascontiguousarray(value)
        arrays[f"in_{name}_dram"] = a
        aps[name] = nc.dram_tensor(f"in_{name}_dram", a.shape, _mybir.dt.from_np(a.dtype), kind="ExternalInput").ap()
    shape = tuple(inputs["x"].shape)
    out = nc.dram_tensor("out_0_dram", shape, _mybir.dt.float32, kind="ExternalOutput").ap()
    program(nc, aps, out)
    r = _run(nc, [arrays], core_ids=[0])
    return r.results[0]["out_0_dram"]
```
